# Optimizing a Trainium2 kernel written in Bass

```python
import math
import jax, jax.numpy as jnp
from jax import lax
import numpy as np

D_MODEL = 2048
BATCH = 1
SEQ = 256
DEPTH = 2

HEAD_DIM = 128
BLOCK = 128
WINDOW = 128
RMS_EPS = 1e-6
NEG_INF = -1e30
SWA_HEADS = 8
SWA_KV_HEADS = 2
SWA_WIDTH = SWA_HEADS * HEAD_DIM
SWA_KV_WIDTH = SWA_KV_HEADS * HEAD_DIM
MLA_HEADS = 4
MLA_NOPE_DIM = 128
MLA_ROPE_DIM = 64
MLA_V_DIM = 128
MLA_Q_RANK = 384
MLA_KV_RANK = 256
MLA_WIDTH = MLA_HEADS * MLA_V_DIM
ROPE_THETA = 10000.0
DIFF_HEADS = 4
DIFF_QK_DIM = 64
DIFF_V_DIM = 128
DIFF_QK_WIDTH = DIFF_HEADS * 2 * DIFF_QK_DIM
DIFF_WIDTH = DIFF_HEADS * DIFF_V_DIM

D_MIX = SWA_WIDTH + MLA_WIDTH + DIFF_WIDTH
SPLIT_SIZES = (SWA_WIDTH, SWA_KV_WIDTH, SWA_KV_WIDTH, SWA_WIDTH,
               MLA_Q_RANK, MLA_KV_RANK, MLA_ROPE_DIM, MLA_WIDTH,
               DIFF_QK_WIDTH, DIFF_QK_WIDTH, DIFF_WIDTH, DIFF_WIDTH)
SPLIT_OFFSETS = tuple(int(o) for o in np.cumsum(SPLIT_SIZES)[:-1])
D_IN = int(sum(SPLIT_SIZES))


def rmsnorm(x, g):
    xf = x.astype(jnp.float32)
    xf = xf * lax.rsqrt(jnp.mean(xf * xf, axis=-1, keepdims=True) + RMS_EPS)
    return xf.astype(x.dtype) * g

def alibi_slopes(n):
    return jnp.asarray(np.array([2.0 ** (-8.0 * (i + 1) / n) for i in range(n)], dtype=np.float32))

def rope(x, positions):
    d = x.shape[-1]
    inv = ROPE_THETA ** (-jnp.arange(0, d, 2, dtype=jnp.float32) / d)
    ang = positions.astype(jnp.float32)[:, None] * inv[None, :]
    shape = (ang.shape[0],) + (1,) * (x.ndim - 3) + (d // 2,)
    cos = jnp.cos(ang).reshape(shape).astype(x.dtype)
    sin = jnp.sin(ang).reshape(shape).astype(x.dtype)
    x1, x2 = x[..., : d // 2], x[..., d // 2:]
    return jnp.concatenate([x1 * cos - x2 * sin, x1 * sin + x2 * cos], axis=-1)

def to_blocks(t):
    b, s = t.shape[:2]
    return jnp.moveaxis(t.reshape((b, s // BLOCK, BLOCK) + t.shape[2:]), 1, 0)

def from_blocks(t):
    nb, b = t.shape[:2]
    return jnp.moveaxis(t, 0, 1).reshape((b, nb * BLOCK) + t.shape[3:])

def swa_attention(q, k, v, sink, positions):
    b, s = q.shape[:2]
    nb = s // BLOCK
    g = SWA_HEADS // SWA_KV_HEADS
    qb = q.reshape(b, nb, BLOCK, SWA_KV_HEADS, g, HEAD_DIM)

    def band(t):
        pad = [(0, 0), (BLOCK, BLOCK)] + [(0, 0)] * (t.ndim - 2)
        tp = jnp.pad(t, pad).reshape((b, nb + 2, BLOCK) + t.shape[2:])
        return jnp.concatenate([tp[:, :-2], tp[:, 1:-1], tp[:, 2:]], axis=2)

    def band1d(t):
        tp = jnp.pad(t, (BLOCK, BLOCK)).reshape(nb + 2, BLOCK)
        return jnp.concatenate([tp[:-2], tp[1:-1], tp[2:]], axis=1)

    kb, vb = band(k), band(v)
    kpos = band1d(positions)
    valid = band1d(jnp.ones((s,), dtype=jnp.bool_))
    qpos = positions.reshape(nb, BLOCK)
    dist = jnp.abs(qpos[:, :, None] - kpos[:, None, :])
    mask = valid[:, None, :] & (dist <= WINDOW)

    scale = HEAD_DIM ** -0.5
    sc = jnp.einsum('bnqhgd,bnkhd->bnhgqk', qb, kb).astype(jnp.float32) * scale
    slopes = alibi_slopes(SWA_HEADS).reshape(SWA_KV_HEADS, g)
    sc = sc - slopes[None, None, :, :, None, None] * dist.astype(jnp.float32)[None, :, None, None]
    sc = jnp.where(mask[None, :, None, None], sc, NEG_INF)
    sk = sink.astype(jnp.float32).reshape(SWA_KV_HEADS, g)[None, None, :, :, None, None]
    m = jnp.maximum(jnp.max(sc, axis=-1, keepdims=True), sk)
    p = jnp.exp(sc - m)
    p = p / (jnp.sum(p, axis=-1, keepdims=True) + jnp.exp(sk - m))
    out = jnp.einsum('bnhgqk,bnkhd->bnqhgd', p.astype(v.dtype), vb)
    return out.reshape(b, s, SWA_WIDTH)

def mla_attention(c_q, c_kv, k_rope, q_norm, w_uq, kv_norm, w_ukv, positions):
    b, s = c_q.shape[:2]
    q = jnp.einsum('bsr,re->bse', rmsnorm(c_q, q_norm), w_uq)
    q = q.reshape(b, s, MLA_HEADS, MLA_NOPE_DIM + MLA_ROPE_DIM)
    q_nope = q[..., :MLA_NOPE_DIM]
    q_rope = rope(q[..., MLA_NOPE_DIM:], positions)
    kv = jnp.einsum('bsr,re->bse', rmsnorm(c_kv, kv_norm), w_ukv)
    kv = kv.reshape(b, s, MLA_HEADS, MLA_NOPE_DIM + MLA_V_DIM)
    k_nope, v = kv[..., :MLA_NOPE_DIM], kv[..., MLA_NOPE_DIM:]
    k_r = rope(k_rope, positions)
    scale = (MLA_NOPE_DIM + MLA_ROPE_DIM) ** -0.5

    def block(xs):
        qn, qr = xs
        sc = (jnp.einsum('bqhd,bkhd->bhqk', qn, k_nope)
              + jnp.einsum('bqhd,bkd->bhqk', qr, k_r)).astype(jnp.float32) * scale
        a = jax.nn.softmax(sc, axis=-1).astype(v.dtype)
        return jnp.einsum('bhqk,bkhd->bqhd', a, v)

    out = from_blocks(lax.map(block, (to_blocks(q_nope), to_blocks(q_rope))))
    return out.reshape(b, s, MLA_WIDTH)

def diff_attention(q, k, v, lam_params, subln_g, positions, lam_init):
    b, s = q.shape[:2]
    nb = s // BLOCK
    lp = lam_params.astype(jnp.float32)
    lam = jnp.exp(jnp.sum(lp[0] * lp[1])) - jnp.exp(jnp.sum(lp[2] * lp[3])) + lam_init
    slopes = alibi_slopes(DIFF_HEADS)
    scale = DIFF_QK_DIM ** -0.5

    def block(xs):
        qb, qpos = xs
        sc = jnp.einsum('bqhcd,bkhcd->bhcqk', qb, k).astype(jnp.float32) * scale
        dist = jnp.abs(qpos[:, None] - positions[None, :]).astype(jnp.float32)
        sc = sc - slopes[None, :, None, None, None] * dist[None, None, None]
        a = jax.nn.softmax(sc, axis=-1)
        attn = (a[:, :, 0] - lam * a[:, :, 1]).astype(v.dtype)
        return jnp.einsum('bhqk,bkhd->bqhd', attn, v)

    out = from_blocks(lax.map(block, (to_blocks(q), positions.reshape(nb, BLOCK))))
    out = rmsnorm(out, subln_g) * (1.0 - lam_init)
    return out.reshape(b, s, DIFF_WIDTH)

def first_inputs(seed: int = 0) -> dict:
    key = jax.random.key(seed)
    ks = jax.random.split(key, 16)
    f32 = jnp.float32
    nrm = lambda k, shape, sc: jax.random.normal(k, shape, dtype=f32) * sc
    return {
        "x": nrm(ks[0], (BATCH, SEQ, D_MODEL), 1.0),
        "positions": jnp.arange(SEQ, dtype=jnp.int32),
        "norm_g": 1.0 + nrm(ks[1], (DEPTH, D_MODEL), 0.02),
        "w_in": nrm(ks[2], (DEPTH, D_MODEL, D_IN), D_MODEL ** -0.5),
        "swa_sink": nrm(ks[3], (DEPTH, SWA_HEADS), 0.5),
        "mla_q_norm": 1.0 + nrm(ks[4], (DEPTH, MLA_Q_RANK), 0.02),
        "mla_w_uq": nrm(ks[5], (DEPTH, MLA_Q_RANK, MLA_HEADS * (MLA_NOPE_DIM + MLA_ROPE_DIM)), MLA_Q_RANK ** -0.5),
        "mla_kv_norm": 1.0 + nrm(ks[6], (DEPTH, MLA_KV_RANK), 0.02),
        "mla_w_ukv": nrm(ks[7], (DEPTH, MLA_KV_RANK, MLA_HEADS * (MLA_NOPE_DIM + MLA_V_DIM)), MLA_KV_RANK ** -0.5),
        "diff_lambda": nrm(ks[8], (DEPTH, 4, DIFF_QK_DIM), 0.1),
        "diff_subln": 1.0 + nrm(ks[9], (DEPTH, DIFF_V_DIM), 0.02),
        "w_out": nrm(ks[10], (DEPTH, D_MIX, D_MODEL), D_MIX ** -0.5),
        "final_norm": 1.0 + nrm(ks[11], (D_MODEL,), 0.02),
    }

def first_block(x, positions, norm_g, w_in, swa_sink, mla_q_norm, mla_w_uq, mla_kv_norm,
              mla_w_ukv, diff_lambda, diff_subln, w_out, final_norm):
    b, s, _ = x.shape
    for l in range(DEPTH):
        h = rmsnorm(x, norm_g[l])
        proj = jnp.einsum('bsd,de->bse', h, w_in[l])
        (a_q, a_k, a_v, a_g, b_cq, b_ckv, b_kr, b_g,
         c_q, c_k, c_v, c_g) = jnp.split(proj, SPLIT_OFFSETS, axis=-1)
        ya = swa_attention(a_q.reshape(b, s, SWA_HEADS, HEAD_DIM),
                           a_k.reshape(b, s, SWA_KV_HEADS, HEAD_DIM),
                           a_v.reshape(b, s, SWA_KV_HEADS, HEAD_DIM),
                           swa_sink[l], positions)
        yb = mla_attention(b_cq, b_ckv, b_kr, mla_q_norm[l], mla_w_uq[l],
                           mla_kv_norm[l], mla_w_ukv[l], positions)
        lam_init = 0.8 - 0.6 * math.exp(-0.3 * l)
        yc = diff_attention(c_q.reshape(b, s, DIFF_HEADS, 2, DIFF_QK_DIM),
                            c_k.reshape(b, s, DIFF_HEADS, 2, DIFF_QK_DIM),
                            c_v.reshape(b, s, DIFF_HEADS, DIFF_V_DIM),
                            diff_lambda[l], diff_subln[l], positions, lam_init)
        y = jnp.concatenate([ya * jax.nn.silu(a_g), yb * jax.nn.silu(b_g),
                             yc * jax.nn.silu(c_g)], axis=-1)
        x = x + jnp.einsum('bse,ed->bsd', y, w_out[l])
    return rmsnorm(x, final_norm)


DEPTH_2 = 1

H_A = 8
DH_A = 64
DILATED_PATTERNS = ((128, 1), (512, 4), (2048, 16))
H_K_B = 4
H_V_B = 8
DK_B = 128
DV_B = 128
CONV_K = 4
DN_CHUNK = 64
H_C = 8
HKV_C = 2
GRP_C = H_C // HKV_C
DH_C = 64
SWA_WINDOW = 128
A_W = H_A * DH_A
BK_W = H_K_B * DK_B
BV_W = H_V_B * DV_B
C_Q_W = H_C * DH_C
C_KV_W = HKV_C * DH_C
CONV_CH = 2 * BK_W + BV_W
MIX = A_W + BV_W + C_Q_W
N_IN = 3 * A_W + 2 * BK_W + 2 * BV_W + 2 * H_V_B + C_Q_W + 2 * C_KV_W
N_GROUPS = 4
EXPERTS_PER_GROUP = 8
N_EXPERTS = N_GROUPS * EXPERTS_PER_GROUP
TOP_K = 2
D_FF = 512
MOE_BLOCK = 128
EPS = 1e-6


def rmsnorm_2(x, g):
    xf = x.astype(jnp.float32)
    y = xf * lax.rsqrt(jnp.mean(xf * xf, axis=-1, keepdims=True) + EPS)
    return y.astype(x.dtype) * g

def l2norm(x):
    return x * lax.rsqrt(jnp.sum(x * x, axis=-1, keepdims=True) + EPS)

def alibi_slopes_2(n):
    return 2.0 ** (-8.0 * jnp.arange(1, n + 1, dtype=jnp.float32) / n)

def banded_attention(q, k, v, max_dist, slopes, dist_scale, sinks=None):
    N, G, R, L, dh = q.shape
    nb = -(-L // BLOCK)
    pad = nb * BLOCK - L
    qb = jnp.pad(q, ((0, 0), (0, 0), (0, 0), (0, pad), (0, 0))).reshape(N, G, R, nb, BLOCK, dh)
    kp = jnp.pad(k, ((0, 0), (0, 0), (BLOCK, pad), (0, 0))).reshape(N, G, nb + 1, BLOCK, dh)
    vp = jnp.pad(v, ((0, 0), (0, 0), (BLOCK, pad), (0, 0))).reshape(N, G, nb + 1, BLOCK, dh)
    kb = jnp.concatenate([kp[:, :, :-1], kp[:, :, 1:]], axis=3)
    vb = jnp.concatenate([vp[:, :, :-1], vp[:, :, 1:]], axis=3)
    s = jnp.einsum('ngrbqd,ngbkd->ngrbqk', qb, kb, preferred_element_type=jnp.float32) * (dh ** -0.5)
    rel = (jnp.arange(BLOCK)[:, None] + BLOCK) - jnp.arange(2 * BLOCK)[None, :]
    kabs = jnp.arange(nb)[:, None] * BLOCK - BLOCK + jnp.arange(2 * BLOCK)[None, :]
    valid = ((rel >= 0) & (rel <= max_dist))[None] & (kabs >= 0)[:, None, :]
    bias = -(slopes.astype(jnp.float32) * dist_scale)[None, :, :, None, None, None] * rel.astype(jnp.float32)
    s = jnp.where(valid, s + bias, -jnp.inf)
    m = jnp.max(s, axis=-1, keepdims=True)
    if sinks is not None:
        sk = sinks.astype(jnp.float32)[None, :, :, None, None, None]
        m = jnp.maximum(m, sk)
    p = jnp.exp(s - m)
    denom = jnp.sum(p, axis=-1, keepdims=True)
    if sinks is not None:
        denom = denom + jnp.exp(sk - m)
    o = jnp.einsum('ngrbqk,ngbkd->ngrbqd', p, vb.astype(jnp.float32)) / denom
    lse = (m + jnp.log(denom))[..., 0]
    o = o.reshape(N, G, R, nb * BLOCK, dh)[:, :, :, :L].astype(v.dtype)
    lse = lse.reshape(N, G, R, nb * BLOCK)[..., :L]
    return o, lse

def dilated_branch(q, k, v, window, dilation, slopes):
    B, S, H, dh = q.shape
    Ld = S // dilation

    def split(t):
        return t.reshape(B, Ld, dilation, H, dh).transpose(0, 2, 3, 1, 4).reshape(B * dilation, H, Ld, dh)

    o, lse = banded_attention(split(q)[:, :, None], split(k), split(v), window // dilation,
                              slopes[:, None], float(dilation))
    o = o[:, :, 0].reshape(B, dilation, H, Ld, dh).transpose(0, 3, 1, 2, 4).reshape(B, S, H, dh)
    lse = lse[:, :, 0].reshape(B, dilation, H, Ld).transpose(0, 3, 1, 2).reshape(B, S, H)
    return o, lse

def causal_depthwise_conv(x, w):
    K, C = w.shape
    return lax.conv_general_dilated(x, w[:, None, :].astype(x.dtype), window_strides=(1,),
                                    padding=[(K - 1, 0)], dimension_numbers=('NWC', 'WIO', 'NWC'),
                                    feature_group_count=C)

def gated_delta_rule(q, k, v, g, beta):
    B, H, S, dk = q.shape
    dv = v.shape[-1]
    C = DN_CHUNK
    n = S // C
    q = q * (dk ** -0.5)

    def chunks(t):
        return t.reshape(B, H, n, C, *t.shape[3:])

    q, k, v, g, beta = chunks(q), chunks(k), chunks(v), chunks(g), chunks(beta)
    gc = jnp.cumsum(g, axis=-1)
    incl = jnp.tril(jnp.ones((C, C), bool))
    strict = jnp.tril(jnp.ones((C, C), bool), -1)
    decay = jnp.exp(jnp.where(incl, gc[..., :, None] - gc[..., None, :], -jnp.inf))
    kb = k * beta[..., None]
    lmat = jnp.where(strict, jnp.einsum('bhnid,bhnjd->bhnij', kb, k) * decay, 0.0)
    a_mat = lmat + jnp.eye(C, dtype=lmat.dtype)
    rhs = jnp.concatenate([v * beta[..., None], kb * jnp.exp(gc)[..., None]], axis=-1)
    sol = lax.linalg.triangular_solve(a_mat, rhs, left_side=True, lower=True, unit_diagonal=True)
    u, w = sol[..., :dv], sol[..., dv:]
    qk = jnp.where(incl, jnp.einsum('bhnid,bhnjd->bhnij', q, k) * decay, 0.0)
    q_dec = q * jnp.exp(gc)[..., None]
    k_dec = k * jnp.exp(gc[..., -1:] - gc)[..., None]
    g_last = jnp.exp(gc[..., -1])

    def step(state, xs):
        q_i, k_i, u_i, w_i, qk_i, gl_i = xs
        v_new = u_i - jnp.einsum('bhck,bhkv->bhcv', w_i, state)
        o = jnp.einsum('bhck,bhkv->bhcv', q_i, state) + jnp.einsum('bhcj,bhjv->bhcv', qk_i, v_new)
        state = state * gl_i[..., None, None] + jnp.einsum('bhck,bhcv->bhkv', k_i, v_new)
        return state, o

    xs = tuple(jnp.moveaxis(t, 2, 0) for t in (q_dec, k_dec, u, w, qk, g_last))
    _, o = lax.scan(step, jnp.zeros((B, H, dk, dv), jnp.float32), xs)
    return jnp.moveaxis(o, 0, 2).reshape(B, H, S, dv)

def gated_deltanet(bq, bk, bv, bz, bb, ba, conv_w, a_log, dt_bias, norm_g):
    B, S, _ = bq.shape
    qkv = jax.nn.silu(causal_depthwise_conv(jnp.concatenate([bq, bk, bv], axis=-1), conv_w)).astype(jnp.float32)
    q, k, v = jnp.split(qkv, [BK_W, 2 * BK_W], axis=-1)
    rep = H_V_B // H_K_B
    q = jnp.repeat(l2norm(q.reshape(B, S, H_K_B, DK_B)), rep, axis=2)
    k = jnp.repeat(l2norm(k.reshape(B, S, H_K_B, DK_B)), rep, axis=2)
    v = v.reshape(B, S, H_V_B, DV_B)
    beta = jax.nn.sigmoid(bb.astype(jnp.float32))
    g = -jnp.exp(a_log.astype(jnp.float32)) * jax.nn.softplus(ba.astype(jnp.float32) + dt_bias.astype(jnp.float32))
    o = gated_delta_rule(jnp.moveaxis(q, 2, 1), jnp.moveaxis(k, 2, 1), jnp.moveaxis(v, 2, 1),
                         jnp.moveaxis(g, 2, 1), jnp.moveaxis(beta, 2, 1))
    o = jnp.moveaxis(o, 1, 2)
    o = rmsnorm_2(o, norm_g.astype(jnp.float32)) * jax.nn.silu(bz.astype(jnp.float32).reshape(B, S, H_V_B, DV_B))
    return o.reshape(B, S, BV_W).astype(bq.dtype)

def hybrid_mixer(h, w_in, conv_w, a_log, dt_bias, dn_norm_g, sinks, w_out):
    B, S, _ = h.shape
    proj = h @ w_in
    sizes = [A_W, A_W, A_W, BK_W, BK_W, BV_W, BV_W, H_V_B, H_V_B, C_Q_W, C_KV_W, C_KV_W]
    cuts = [int(i) for i in np.cumsum(sizes)[:-1]]
    aq, ak, av, bq, bk, bv, bz, bb, ba, cq, ck, cv = jnp.split(proj, cuts, axis=-1)

    aq, ak, av = (t.reshape(B, S, H_A, DH_A) for t in (aq, ak, av))
    slopes_a = alibi_slopes_2(H_A)
    outs, lses = zip(*[dilated_branch(aq, ak, av, wdw, dil, slopes_a) for (wdw, dil) in DILATED_PATTERNS])
    wts = jax.nn.softmax(jnp.stack(lses, axis=0), axis=0)
    o_a = jnp.einsum('pbsh,pbshd->bshd', wts, jnp.stack(outs, axis=0).astype(jnp.float32))
    o_a = o_a.astype(h.dtype).reshape(B, S, A_W)

    o_b = gated_deltanet(bq, bk, bv, bz, bb, ba, conv_w, a_log, dt_bias, dn_norm_g)

    cq = cq.reshape(B, S, HKV_C, GRP_C, DH_C).transpose(0, 2, 3, 1, 4)
    ck = ck.reshape(B, S, HKV_C, DH_C).transpose(0, 2, 1, 3)
    cv = cv.reshape(B, S, HKV_C, DH_C).transpose(0, 2, 1, 3)
    o_c, _ = banded_attention(cq, ck, cv, SWA_WINDOW - 1, alibi_slopes_2(H_C).reshape(HKV_C, GRP_C), 1.0,
                              sinks.reshape(HKV_C, GRP_C))
    o_c = o_c.transpose(0, 3, 1, 2, 4).reshape(B, S, C_Q_W)

    return jnp.concatenate([o_a, o_b, o_c], axis=-1) @ w_out

def grouped_expert_mlp(xt, eidx, w_gate, w_up, w_down):
    T, K = eidx.shape
    E = w_gate.shape[0]
    A = T * K
    flat_e = eidx.reshape(A)
    order = jnp.argsort(flat_e)
    sorted_e = flat_e[order]
    counts = jnp.bincount(flat_e, length=E)
    starts = jnp.cumsum(counts) - counts
    padded = (counts + MOE_BLOCK - 1) // MOE_BLOCK * MOE_BLOCK
    pad_ends = jnp.cumsum(padded)
    pad_starts = pad_ends - padded
    dest = pad_starts[sorted_e] + jnp.arange(A) - starts[sorted_e]
    nblk = -(-A // MOE_BLOCK) + E
    rows = jnp.zeros((nblk * MOE_BLOCK, xt.shape[1]), xt.dtype).at[dest].set(xt[order // K])
    blk_expert = jnp.minimum(jnp.searchsorted(pad_ends, jnp.arange(nblk) * MOE_BLOCK, side='right'), E - 1)

    def expert_block(args):
        xb, e = args
        hid = jax.nn.silu(xb @ w_gate[e]) * (xb @ w_up[e])
        return hid @ w_down[e]

    yb = lax.map(expert_block, (rows.reshape(nblk, MOE_BLOCK, -1), blk_expert))
    y_sorted = yb.reshape(nblk * MOE_BLOCK, -1)[dest]
    y = jnp.zeros((A, y_sorted.shape[-1]), y_sorted.dtype).at[order].set(y_sorted)
    return y.reshape(T, K, -1)

def hierarchical_moe(h, rg_w, rg_b, re_w, re_b, w_gate, w_up, w_down):
    B, S, D = h.shape
    xt = h.reshape(-1, D)
    T = xt.shape[0]
    tok = jnp.arange(T)
    glog = (xt @ rg_w).astype(jnp.float32) + rg_b.astype(jnp.float32)
    gsel = jnp.argmax(glog, axis=-1)
    pg = jax.nn.softmax(glog, axis=-1)[tok, gsel]
    elog = ((xt @ re_w).astype(jnp.float32) + re_b.astype(jnp.float32)).reshape(T, N_GROUPS, EXPERTS_PER_GROUP)
    top_v, top_i = lax.top_k(elog[tok, gsel], TOP_K)
    gates = pg[:, None] * jax.nn.softmax(top_v, axis=-1)
    eidx = gsel[:, None] * EXPERTS_PER_GROUP + top_i
    y = grouped_expert_mlp(xt, eidx, w_gate, w_up, w_down)
    return jnp.einsum('tk,tkd->td', gates.astype(y.dtype), y).reshape(B, S, D)

def second_inputs(seed: int = 0) -> dict:
    key = jax.random.key(seed)
    ks = jax.random.split(key, 21)
    L, D = DEPTH_2, D_MODEL

    def nrm(k, shape, scale):
        return jax.random.normal(k, shape, jnp.float32) * scale

    dt = jnp.exp(jax.random.uniform(ks[9], (L, H_V_B), jnp.float32, math.log(1e-3), math.log(1e-1)))
    return {
        'x': nrm(ks[0], (BATCH, SEQ, D), 1.0),
        'c': nrm(ks[1], (BATCH, D), 1.0),
        'norm1_g': 1.0 + nrm(ks[2], (L, D), 0.02),
        'norm2_g': 1.0 + nrm(ks[3], (L, D), 0.02),
        'ada_w': nrm(ks[4], (L, D, 6 * D), 0.5 * D ** -0.5),
        'ada_b': nrm(ks[5], (L, 6 * D), 0.02),
        'w_in': nrm(ks[6], (L, D, N_IN), D ** -0.5),
        'dn_conv_w': nrm(ks[7], (L, CONV_K, CONV_CH), CONV_K ** -0.5),
        'dn_a_log': jnp.log(jax.random.uniform(ks[8], (L, H_V_B), jnp.float32, 1.0, 16.0)),
        'dn_dt_bias': dt + jnp.log(-jnp.expm1(-dt)),
        'dn_norm_g': 1.0 + nrm(ks[10], (L, DV_B), 0.02),
        'attn_sinks': nrm(ks[11], (L, H_C), 1.0),
        'w_out': nrm(ks[12], (L, MIX, D), MIX ** -0.5),
        'router_group_w': nrm(ks[13], (L, D, N_GROUPS), D ** -0.5),
        'router_group_b': nrm(ks[14], (L, N_GROUPS), 0.01),
        'router_expert_w': nrm(ks[15], (L, D, N_EXPERTS), D ** -0.5),
        'router_expert_b': nrm(ks[16], (L, N_EXPERTS), 0.01),
        'expert_w_gate': nrm(ks[17], (L, N_EXPERTS, D, D_FF), D ** -0.5),
        'expert_w_up': nrm(ks[18], (L, N_EXPERTS, D, D_FF), D ** -0.5),
        'expert_w_down': nrm(ks[19], (L, N_EXPERTS, D_FF, D), D_FF ** -0.5),
        'final_norm_g': 1.0 + nrm(ks[20], (D,), 0.02),
    }

def second_block(x, c, norm1_g, norm2_g, ada_w, ada_b, w_in, dn_conv_w, dn_a_log, dn_dt_bias, dn_norm_g,
              attn_sinks, w_out, router_group_w, router_group_b, router_expert_w, router_expert_b,
              expert_w_gate, expert_w_up, expert_w_down, final_norm_g):
    c_act = jax.nn.silu(c)
    for l in range(DEPTH_2):
        mod = (c_act @ ada_w[l] + ada_b[l])[:, None, :]
        sh1, sc1, g1, sh2, sc2, g2 = jnp.split(mod, 6, axis=-1)
        h = rmsnorm_2(x, norm1_g[l]) * (1.0 + sc1) + sh1
        x = x + g1 * hybrid_mixer(h, w_in[l], dn_conv_w[l], dn_a_log[l], dn_dt_bias[l], dn_norm_g[l],
                                  attn_sinks[l], w_out[l])
        h = rmsnorm_2(x, norm2_g[l]) * (1.0 + sc2) + sh2
        x = x + g2 * hierarchical_moe(h, router_group_w[l], router_group_b[l], router_expert_w[l],
                                      router_expert_b[l], expert_w_gate[l], expert_w_up[l], expert_w_down[l])
    return rmsnorm_2(x, final_norm_g)


def setup_inputs(seed=0):
    out = dict(first_inputs(seed))
    for name, value in second_inputs(seed + 1).items():
        if name != "x":
            out[name + "_2"] = value
    return out


def reference(
    x, positions, norm_g, w_in, swa_sink, mla_q_norm, mla_w_uq, mla_kv_norm, mla_w_ukv,
    diff_lambda, diff_subln, w_out, final_norm, c_2, norm1_g_2, norm2_g_2, ada_w_2, ada_b_2,
    w_in_2, dn_conv_w_2, dn_a_log_2, dn_dt_bias_2, dn_norm_g_2, attn_sinks_2, w_out_2,
    router_group_w_2, router_group_b_2, router_expert_w_2, router_expert_b_2, expert_w_gate_2,
    expert_w_up_2, expert_w_down_2, final_norm_g_2,
):
    x = first_block(
        x, positions, norm_g, w_in, swa_sink, mla_q_norm, mla_w_uq, mla_kv_norm, mla_w_ukv,
        diff_lambda, diff_subln, w_out, final_norm,
    )
    return second_block(
        x, c_2, norm1_g_2, norm2_g_2, ada_w_2, ada_b_2, w_in_2, dn_conv_w_2, dn_a_log_2,
        dn_dt_bias_2, dn_norm_g_2, attn_sinks_2, w_out_2, router_group_w_2, router_group_b_2,
        router_expert_w_2, router_expert_b_2, expert_w_gate_2, expert_w_up_2, expert_w_down_2,
        final_norm_g_2,
    )


_drawn_inputs = setup_inputs


def setup_inputs(seed=0):
    import zlib

    import numpy as np

    out = dict(_drawn_inputs(seed))
    spreads = {}
    factors = {'norm_g': 3.264,
     'swa_sink': 59.488,
     'mla_q_norm': 8.0,
     'mla_kv_norm': 8.0,
     'diff_lambda': 3.19,
     'diff_subln': 5.437,
     'norm1_g_2': 7.158,
     'norm2_g_2': 5.288,
     'ada_b_2': 2.746,
     'dn_norm_g_2': 8.0,
     'attn_sinks_2': 49.472,
     'router_group_b_2': 38.617,
     'router_expert_b_2': 36.041,
     'final_norm_g_2': 20.987}
    for name, (base, spread) in spreads.items():
        noise = np.random.default_rng([zlib.crc32(name.encode()), seed]).standard_normal(out[name].shape)
        drawn = base * np.exp(spread * noise) if base else spread * noise
        out[name] = __import__('jax').numpy.asarray(drawn.astype(out[name].dtype))
    for name, factor in factors.items():
        out[name] = (out[name] * factor).astype(out[name].dtype)
    return out
```

```python
import math
from contextlib import ExitStack

import numpy as np

import concourse.bass as bass
from concourse import mybir
from concourse.alu_op_type import AluOpType as ALU

P = 128
S = 256
TT = S // P
D = 2048
KB = D // P
LAYERS = 2
U = 512
HALF = 8 * U
RING = 4

AQ, AK, AV, AG, CQ, CKV, KR, BG, DQ, DK, DV, DG, D_IN = 0, 1024, 1280, 1536, 2560, 2944, 3200, 3264, 3776, 4288, 4800, 5312, 5824
REST = D_IN - 11 * U
QR_K, KVR_K = 3, 2
UQ, UKV = 768, 1024
EPS = 1e-6
BIG = 1e32

A2Q, A2K, A2V, BQ, BK, BV, BZ, BB, BA, C2Q, C2K, C2V, N_IN = 0, 512, 1024, 1536, 2048, 2560, 3584, 4608, 4616, 4624, 5136, 5264, 5392

ORDER = (5, 6, 11, 7, 8, 9, 10, 0, 2, 3, 1, 4)
SLOPES8 = [2.0 ** -(i + 1) for i in range(8)]
SLOPES4 = [2.0 ** -(2 * (i + 1)) for i in range(4)]
SC128, SC64, SC192 = 128 ** -0.5, 64 ** -0.5, 192 ** -0.5
MAGIC = 12582912.0
TWO_PI_A = 6.28125
TWO_PI_B = float(np.float32(2 * math.pi - 6.28125))
TWO_PI_C = 2 * math.pi - 6.28125 - TWO_PI_B

G_, QN_, SK_, LP_, SB_, LC_, SMALL = 0, 16, 21, 29, 285, 413, 415

C_ID, C_FREQ, C_SEL, C1 = 0, 128, 160, 161


class Parts:
    pass


class Tally:

    def __init__(self, base=0, first=0):
        self.base, self.n = base, first

    def next(self, by=1):
        self.n += by
        return self.base + self.n

    def now(self):
        return self.base + self.n


PER = dict(hu=56, pj=4, ta=32, td=42, tdr=30, pja=16, xo=4, s=20, m=20, e=20, c=4, o=16, q=6, rin=6, rout=6, dve=73)

TASKS = {1: [("mla_norm", 0)], 2: [("mla_up", 0)], 3: [("mla_rope", 0)], 4: [("soft", "M0")],
         5: [("out", "M0"), ("soft", "M1")], 6: [("out", "M1"), ("prep_d", 0), ("soft", "D0")],
         7: [("out", "D0"), ("soft", "D1")], 8: [("out", "D1"), ("soft", "D2")],
         9: [("out", "D2"), ("soft", "D3"), ("prep_w", 0)], 10: [("out", "D3"), ("soft", "W0")],
         11: [("out", "W0"), ("prep_w", 1), ("soft", "W1")],
         12: [("out", "W1"), ("soft", "W2"), ("out", "W2"), ("soft", "W3"), ("out", "W3")]}


K_LEV, K_U, K_NEG, K_ONE = 0, 6 * P, 7 * P, 8 * P
ORDER2 = (3, 4, 5, 6, 9, 0, 1, 2, 10, 7, 8)
PIECES = 8
GAPS = [("gates", 0, 0)] + [(kind, t, n) for t in range(TT) for kind, n in
        [("expand", 0), ("gram", 0), ("first", 0)] + [(x, i) for i in range(1, 6) for x in ("x", "grow")] +
        [("apply", 0), ("qdec", 0)] + [(x, c) for c in (0, 1) for x in ("new", "state")]]
PAIRS2 = [("A", g) for g in range(4)] + [("C", g) for g in range(4)]


def levels_of(m):
    return [m.cb[:, :, :].rearrange("p k n -> p (k n)")[:, i * P:(i + 1) * P] for i in range(4)] + \
           [m.ropeq[:, :, :, :].rearrange("p t h n -> p (t h n)")[:, i * P:(i + 1) * P] for i in range(2)]


def second_buffers(m):
    rq = m.ropeq[:, :, :, :].rearrange("p t h n -> p (t h n)")
    m.level = levels_of(m)
    m.uincl, m.neg = rq[:, 2 * P:3 * P], rq[:, 3 * P:4 * P]
    m.ones = m.ropet[:, :, :, :].rearrange("p t h n -> p (t h n)")[:, 0:P]
    m.rel = {"A": m.dist[:, :, :], "C": m.distm[:, :, :]}
    m.cnt = m.ada_part[:, :].rearrange("p (t n) -> p t n", t=TT)
    h4 = lambda x: x.rearrange("p (h n) -> p h n", n=P)
    qk = m.QK[:, :, :].rearrange("p k n -> p (k n)")
    m.raw = [m.QK[:, 8 * i:8 * i + 4, :] for i in range(2)]
    m.conv = [m.QK[:, 8 * i + 4:8 * i + 8, :] for i in range(2)]
    m.u, m.wt, m.qkt, m.qd = (h4(qk[:, i * 1024:(i + 1) * 1024]) for i in range(4))
    r2, r3 = m.ring[:, 2, :], m.ring[:, 3, :]
    m.kdec, m.kq, m.state = h4(r2[:, 0:1024]), h4(r2[:, 1024:2048]), h4(r2[:, 2048:3072])
    m.lt = [h4(r2[:, 3072:3584]), h4(r2[:, 3584:4096])]
    m.mt, m.t_, m.tt, m.x_ = ([h4(r3[:, (2 * i + b) * U:(2 * i + b + 1) * U]) for b in (0, 1)] for i in range(4))
    m.dt = [h4(m.PB[:, b, :, :].rearrange("p t n -> p (t n)")) for b in (0, 1)]
    m.sq2 = m.ring[:, 2, 0:2048].rearrange("p (t n) -> p t n", t=TT)
    m.g1 = m.ring[:, 2, 0:2048]
    m.fn, m.gn = m.PROJ[:, 0, 0:D], m.PROJ[:, 0, D:2 * D]
    m.sc, m.sh = m.PROJ[:, 1, 0:D], m.PROJ[:, 1, D:2 * D]
    m.cw_rows = m.kr2[:, :, :, :].rearrange("p t h n -> p (t h n)")[0:64, 0:P]
    m.ck4 = m.PT[:, :, :, :].rearrange("p a b c -> p a (b c)")
    m.tmp = m.ring[:, 3, 0:2 * U].rearrange("p (t n) -> p t n", t=TT)
    m.sqo = m.ring[:, 3, 2 * U:4 * U]


def second_sync(m, sp):
    a, ring = m.a, m.ring
    load = 0
    w, wo = a["w_in_2"][0], a["w_out_2"][0]

    def half(src, width, j):
        nonlocal load
        sp.wait_ge(m.hu_used, LAYERS * PER["hu"] + RING + load - 1)
        sp.dma_start(ring[:, load % 2, 0:8 * width].rearrange("p (k n) -> p k n", k=8),
                     m.half_rows(src, j)).then_inc(m.w_in[load % 2], 16)
        load += 1

    for p, u in enumerate(ORDER2):
        hi = min((u + 1) * U, N_IN)
        for j in (0, 1):
            half(w[:, u * U:hi], hi - u * U, j)
        if p == 0:
            sp.wait_ge(m.xo, 4 * LAYERS + 1)
            sp.wait_ge(m.mod_out, 16 * 24)
            for dst, src in ((m.fn, a["final_norm"].rearrange("(a n) -> a n", a=1)), (m.gn, a["norm1_g_2"]),
                             (m.sc, m.mod[:, D:2 * D]), (m.sh, m.mod[:, 0:D])):
                sp.dma_start(dst, src.partition_broadcast(P)).then_inc(m.rows_in, 16)
    for u in range(4):
        for j in (0, 1):
            half(wo[:, u * U:(u + 1) * U], U, j)
        if u == 0:
            sp.wait_ge(m.r_done, 4 * TT)
            sp.dma_start(m.g1, m.mod[:, 2 * D:3 * D].partition_broadcast(P)).then_inc(m.rows_in, 16)


def second_gpsimd(nc, m, pool):
    a = m.a
    pool.wait_ge(m.xo, 4 * LAYERS + 1)
    lev = m.cb[:, :, :].rearrange("p k n -> p (k n)")
    rq = m.ropeq[:, :, :, :].rearrange("p t h n -> p (t h n)")
    for dst, src in ((lev, a["cst2"][:, 0:4 * P]), (rq, a["cst2"][:, 4 * P:8 * P]), (m.ones, a["cst2"][:, 8 * P:9 * P]),
                     (m.dist[:, :, :].rearrange("p t n -> p (t n)"), a["rel_a"]),
                     (m.distm[:, :, :].rearrange("p t n -> p (t n)"), a["rel_c"]), (m.ada_part[:, :], a["cnt_a"]),
                     (m.cw_rows, a["dn_conv_w_2"][0].rearrange("j (b c) -> (j b) c", c=P)),
                     (m.sm2[:, 0:8], a["dn_a_log_2"].partition_broadcast(P)), (m.sm2[:, 8:16], a["dn_dt_bias_2"].partition_broadcast(P)),
                     (m.sm2[:, 16:24], a["attn_sinks_2"].partition_broadcast(P)), (m.sm2[:, 24:152], a["dn_norm_g_2"].partition_broadcast(P))):
        pool.dma_start(dst, src).then_inc(m.cst2_in, 16)
    n = LAYERS * PER["rin"]
    for _ in (0, 1):
        n += 1
        pool.wait_ge(m.rin_ready, n)
        nc.gpsimd.tensor_tensor(m.rms[:, 0:2], m.rin[:, 0:2], m.half[:, 0:2], ALU.pow).then_inc(m.rms_ready, 1)
    nc.gpsimd.memset(m.half16[:, :], -0.5).then_inc(m.half_ready, 1)
    pool.wait_ge(m.half_ready, 2)
    for _ in range(1 + TT):
        n += 1
        pool.wait_ge(m.rin_ready, n)
        nc.gpsimd.tensor_tensor(m.rms16[:, :], m.rin16[:, :], m.half16[:, :], ALU.pow).then_inc(m.rms_ready, 1)


def second_tensor(nc, m, pe):
    PROJ, HT, QK, Y, bank, ident = m.PROJ, m.HT, m.QK, m.Y, m.bank, m.ident
    mm = nc.tensor.matmul
    ta, td = Tally(LAYERS * PER["ta"], 1), Tally(LAYERS * PER["td"], 1)
    load = [Tally(LAYERS * 15 * 16) for _ in (0, 1)]
    pjc = LAYERS * PER["pja"]
    hu = 0

    def transposes(by_act, sources):
        t, ready, copied, ps = (ta, m.ta_ready, m.ta_copied, bank[6]) if by_act else (td, m.td_ready, m.td_copied, bank[7])
        pe.wait_ge(copied, t.now())
        for i, src in enumerate(sources):
            last = nc.tensor.transpose(ps[:, i * P:(i + 1) * P], src, ident)
        last.then_inc(ready, 1)
        t.next()

    def copied():
        pe.wait_ge(m.ta_copied, ta.now())
        pe.wait_ge(m.td_copied, td.now())

    def halves(v, width, gaps=()):
        nonlocal hu
        gaps = list(gaps)
        for j in (0, 1):
            pe.wait_ge(m.w_in[hu % 2], load[hu % 2].next(16))
            w = m.ring[:, hu % 2, 0:8 * width].rearrange("p (k n) -> p k n", k=8)
            for k in range(8):
                if k % 2 == 0 and gaps:
                    delta(*gaps.pop(0))
                for t in range(TT):
                    last = mm(bank[2 * (v % 2) + t][:, 0:width], HT[:, 8 * j + k, t * P:(t + 1) * P],
                              w[:, k, :], start=j == 0 and k == 0, stop=j == 1 and k == 7)
            last.then_inc(m.hu_used, 1)
            hu += 1

    stage = [0, 0]
    rec = 0

    def delta(kind, t, n):
        nonlocal rec
        if kind == "gates":
            pe.wait_ge(m.g_done, 1)
            for i in range(TT):
                last = mm(bank[4][:, i * 8:i * 8 + 8], m.uincl, m.g[:, i, :], start=True, stop=True)
            last.then_inc(m.gc_ready, 1)
            return
        if kind in ("new", "state"):
            c = slice(64 * n, 64 * n + 64)
            rec += 1
            if kind == "new":
                pe.wait_ge(m.b_done[0], stage[0])
                pe.wait_ge(m.b_done[1], stage[1])
                pe.wait_ge(m.r_done, rec - 1) if rec > 1 else pe.wait_ge(m.state_zero, 1)
                for h in range(8):
                    last = mm(bank[4 + h // 4][c, (h % 4) * P:(h % 4 + 1) * P], m.wt[:, h, c], m.state[:, h, :], start=True, stop=True)
                last.then_inc(m.r_ready, 1)
            else:
                pe.wait_ge(m.r_done, rec - 1)
                pe.wait_ge(m.oc_done, 2 * t + n) if 2 * t + n else None
                for h in range(8):
                    kt = m.kdec[c, h, :]
                    last = mm(bank[4 + h // 4][:, (h % 4) * P:(h % 4 + 1) * P], kt, m.u[c, h, :], start=True, stop=True)
                for h in range(8):
                    out = bank[6 + h // 4][c, (h % 4) * P:(h % 4 + 1) * P]
                    mm(out, m.qd[:, h, c], m.state[:, h, :], start=True, stop=False)
                    last = mm(out, m.qkt[c, h, c], m.u[c, h, :], start=False, stop=True)
                last.then_inc(m.r_ready, 1)
            return
        for b in (0, 1):
            A, B = bank[4 + 2 * b], bank[5 + 2 * b]
            s4 = lambda ps, i: ps[:, i * P:(i + 1) * P]
            pe.wait_ge(m.b_done[b], stage[b]) if stage[b] else pe.wait_ge(m.bd_ready[b], 1)
            if kind == "expand":
                if t == 0:
                    pe.wait_ge(m.gc_copied, 1)
                if t:
                    pe.wait_ge(m.r_done, rec)
                    pe.wait_ge(m.oc_done, 2 * t)
                    pe.wait_ge(m.bd_ready[b], t + 1)
                for i in (0, 1):
                    kh = 2 * b + i
                    nc.tensor.transpose(s4(A, i), PROJ[:, t, BK + kh * P:BK + (kh + 1) * P], ident)
                    nc.tensor.transpose(s4(A, 2 + i), PROJ[:, t, BQ + kh * P:BQ + (kh + 1) * P], ident)
                last = mm(B[:, :], m.ones, m.x_[b].rearrange("p h n -> p (h n)"), start=True, stop=True)
            elif kind == "gram":
                for i in (0, 1):
                    k, q = m.kq[:, 4 * b + i, :], m.kq[:, 4 * b + 2 + i, :]
                    mm(s4(A, i), k, k, start=True, stop=True)
                    mm(s4(A, 2 + i), k, q, start=True, stop=True)
                last = mm(B[:, :], m.ones, m.x_[b].rearrange("p h n -> p (h n)"), start=True, stop=True)
            elif kind == "first":
                for h in range(4):
                    last = nc.tensor.transpose(s4(A, h), m.mt[b][:, h, :], ident)
            elif kind == "x":
                for h in range(4):
                    last = mm(s4(A, h), m.mt[b][:, h, :], m.t_[b][:, h, :], start=True, stop=True)
            elif kind == "grow":
                if n < 5:
                    for h in range(4):
                        mm(s4(A, h), m.tt[b][:, h, :], m.x_[b][:, h, :], start=True, stop=True)
                for h in range(4):
                    last = mm(s4(B, h), m.x_[b][:, h, :], m.tt[b][:, h, :], start=True, stop=True)
            elif kind == "apply":
                for h in range(4):
                    mm(s4(A, h), m.tt[b][:, h, :], m.x_[b][:, h, :], start=True, stop=True)
                for h in range(4):
                    last = mm(s4(B, h), m.mt[b][:, h, :], m.tt[b][:, h, :], start=True, stop=True)
            elif kind == "qdec":
                for h in range(4):
                    last = nc.tensor.transpose(s4(A, h), m.t_[b][:, h, :], ident)
            last.then_inc(m.b_ready[b], 1)
            stage[b] += 1

    pe.wait_ge(m.h_ready, LAYERS + 1)
    for j in range(8):
        transposes(j % 2 == 0, [Y[:, t, (2 * j + b) * P:(2 * j + b + 1) * P] for b in (0, 1) for t in range(TT)])
    pe.wait_ge(m.cst2_in, 16 * 11)
    pe.wait_ge(m.ta_copied, ta.now())
    nc.tensor.transpose(bank[6][:, 0:64], m.cw_rows, ident[0:64, 0:64]).then_inc(m.ta_ready, 1)
    ta.next()
    copied()
    at = 0
    for p, u in enumerate(ORDER2):
        width = min(U, N_IN - u * U)
        if p >= 2:
            pe.wait_ge(m.pj_copied, pjc + p - 1)
        gaps = GAPS[at:at + PIECES] if p >= 5 else ()
        at += len(gaps)
        if p == 5:
            copied()
        halves(p, width, gaps)
        if p < 4:
            pe.wait_ge(m.pj_copied, pjc + p + 1)
            for i in (0, 1):
                transposes(i == 0, [PROJ[:, t, BQ + p * U + (2 * i + b) * P:BQ + p * U + (2 * i + b + 1) * P] for b in (0, 1) for t in range(TT)])
        if 1 <= p <= 4:
            pe.wait_ge(m.conv_ready, p)
            src = m.conv[(p - 1) % 2]
            for t in range(TT):
                transposes(t == 0, [src[:, b, t * P:(t + 1) * P] for b in range(4)])
    for g in GAPS[at:]:
        delta(*g)
    pe.wait_ge(m.oc_done, 2 * TT)
    pe.wait_ge(m.r_done, 4 * TT)
    pe.wait_ge(m.pj_copied, pjc + len(ORDER2))
    cols = [A2Q, A2Q + 2 * P, A2K, A2K + 2 * P, C2Q, C2Q + 2 * P]
    for i, c in enumerate(cols):
        transposes(i % 2 == 0, [PROJ[:, t, c + b * P:c + (b + 1) * P] for b in (0, 1) for t in range(TT)])
    pe.wait_ge(m.ck_ready, 1)
    transposes(True, [m.ck4[:, t, i * P:(i + 1) * P] for i in (0, 1) for t in range(TT)])
    copied()
    s_n, o_n, e_n = LAYERS * PER["s"], LAYERS * PER["o"], LAYERS * PER["e"]

    def scores(kind, h):
        nonlocal s_n
        pe.wait_ge(m.s_used, s_n + 1)
        q = slice(64 * (h % 2), 64 * (h % 2) + 64)
        qb, kb = (h // 2, 4 + h // 2) if kind == "A" else (8 + h // 2, 12 + h // 4)
        for t in range(TT):
            last = mm(bank[4][:, t * S:(t + 1) * S], HT[q, qb, t * P:(t + 1) * P], HT[q, kb, :], start=True, stop=True)
        last.then_inc(m.s_ready, 1)
        s_n += 1

    def out(kind, h, i):
        nonlocal o_n, e_n
        e_n += 1
        pe.wait_ge(m.c_ready if kind == "A" else m.e_ready, (LAYERS * PER["c"] + h + 1) if kind == "A" else e_n)
        transposes(True, [m.PB[:, i, qt, kt * P:(kt + 1) * P] for kt in range(TT) for qt in range(TT)])
        pe.wait_ge(m.o_used, o_n + 1)
        pe.wait_ge(m.ta_copied, ta.now())
        v = A2V + h * 64 if kind == "A" else C2V + (h // 4) * 64
        for t in range(TT):
            for kt in range(TT):
                last = mm(bank[5][:, t * P:t * P + 64], m.PT[:, kt, t, :], PROJ[:, kt, v:v + 64], start=kt == 0, stop=kt == TT - 1)
        last.then_inc(m.o_ready, 1)
        o_n += 1

    for n, (kind, g) in enumerate(PAIRS2):
        for i in (0, 1):
            scores(kind, 2 * g + i)
        for i in (0, 1):
            out(kind, 2 * g + i, i)
    pe.wait_ge(m.o_used, o_n + 1)
    pe.wait_ge(m.on_done, TT)
    for j in range(8):
        transposes(j % 2 == 0, [Y[:, t, (2 * j + b) * P:(2 * j + b + 1) * P] for b in (0, 1) for t in range(TT)])
    copied()
    for n in range(4):
        v = len(ORDER2) + n
        if n >= 2:
            pe.wait_ge(m.xo, 4 * LAYERS + n)
        else:
            pe.wait_ge(m.pj_copied, pjc + v - 1)
        halves(v, U)


def second_scalar(nc, m, act, ACT):
    A_ = nc.scalar.activation
    PROJ, bank, X, Y = m.PROJ, m.bank, m.X, m.Y
    ta = Tally(LAYERS * PER["ta"])

    def copy(dst, src):
        act.wait_ge(m.ta_ready, ta.next())
        A_(dst, src, ACT.Copy).then_inc(m.ta_copied, 1)

    act.wait_ge(m.xo, 4 * LAYERS + 1)
    for t in range(TT):
        last = A_(Y[:, t, :], X[:, t, :], ACT.Square, accum_out=m.ss[:, t:t + 1])
    last.then_inc(m.sq_ready, 1)
    act.wait_ge(m.x_normed, 1)
    for t in range(TT):
        last = A_(Y[:, t, :], X[:, t, :], ACT.Square, accum_out=m.ss[:, t:t + 1])
    last.then_inc(m.sq_ready, 1)
    for j in range(0, 8, 2):
        copy(m.HT[:, 2 * j:2 * j + 2, :], bank[6][:, :])
    copy(m.cwt[:, :], bank[6][:, 0:64])
    e = Tally(0)
    at = 0
    b_ready = [0, 0]
    rec = 0

    def delta(kind, t, n):
        nonlocal rec
        if kind == "gates":
            act.wait_ge(m.gc_copied, 1)
            A_(m.egc[:, :, :], m.gsum[:, :, :], ACT.Exp).then_inc(m.egc_ready, 1)
        elif kind == "expand":
            for b in (0, 1):
                act.wait_ge(m.dx_ready[b], t + 1)
                A_(m.egl[:, t, 4 * b:4 * b + 4, :], m.gl[:, t, 4 * b:4 * b + 4, :], ACT.Exp)
                A_(m.dt[b], m.dt[b], ACT.Exp).then_inc(m.d_ready[b], 1)
        elif kind == "new":
            rec += 1
        elif kind == "state":
            rec += 1
            c = slice(64 * n, 64 * n + 64)
            act.wait_ge(m.r_ready, rec)
            for i in (0, 1):
                last = A_(Y[c, t, U + i * U:U + (i + 1) * U], bank[6 + i][c, :], ACT.Copy)
            last.then_inc(m.oc_done, 1)

    for p, u in enumerate(ORDER2):
        width = min(U, N_IN - u * U)
        gaps = GAPS[at:at + PIECES] if p >= 5 else ()
        at += len(gaps)
        for g in gaps:
            delta(*g)
        act.wait_ge(m.hu_used, LAYERS * PER["hu"] + RING + 2 * (p + 1))
        for t in range(TT):
            last = A_(PROJ[:, t, u * U:u * U + width], bank[2 * (p % 2) + t][:, 0:width], ACT.Silu if u in (7, 8) else ACT.Copy)
        last.then_inc(m.pj_copied, 1)
        if p < 4:
            copy(m.raw[p % 2][:, 0:2, :], bank[6][:, :])
        if p >= 1 and p <= 4:
            act.wait_ge(m.cv_ready, p)
            A_(m.conv[(p - 1) % 2], m.conv[(p - 1) % 2], ACT.Silu).then_inc(m.conv_ready, 1)
            copy(PROJ[:, 0, BQ + (p - 1) * U:BQ + p * U], bank[6][:, :])
        if p == 4:
            act.wait_ge(m.pj_copied, LAYERS * PER["pja"] + 5)
            A_(m.beta[:, :, :], PROJ[:, :, BB:BB + 8], ACT.Sigmoid).then_inc(m.beta_ready, 1)
            act.wait_ge(m.z_ready, 1)
            A_(m.ea[:, :], m.sm2[:, 0:8], ACT.Exp)
            A_(m.ez[:, :, :], m.nz[:, :, :], ACT.Exp).then_inc(m.ez_ready, 1)
            act.wait_ge(m.ez_ready, 1)
            A_(m.ez[:, :, :], m.ez[:, :, :], ACT.Ln, bias=1.0).then_inc(m.ez_ready, 1)
    for g in GAPS[at:]:
        delta(*g)
    HT = m.HT
    for dst in (HT[:, 0:2, :], HT[:, 4:6, :], HT[:, 8:10, :], HT[:, 12:14, :]):
        copy(dst, bank[6][:, :])
    m_n, e_n = LAYERS * PER["m"], 0
    for kind, g in PAIRS2:
        for i in (0, 1):
            h = 2 * g + i
            m_n += 1
            act.wait_ge(m.m_ready, m_n)
            if kind == "C":
                A_(m.es[:, i, :], m.mm[:, i, :], ACT.Exp, bias=m.sm2[:, 16 + h:17 + h], scale=-1.0)
            for t in range(TT):
                kw = {} if kind == "A" else {"accum_out": m.den[:, i, t:t + 1]}
                last = A_(m.PB[:, i, t, :], m.PB[:, i, t, :], ACT.Exp, bias=m.nm[:, i, t:t + 1], scale=SC64, **kw)
            last.then_inc(m.e_ready, 1)
        for i in (0, 1):
            copy(m.PT[:, :, :, :], bank[6][:, :])
    for j in range(0, 8, 2):
        copy(HT[:, 2 * j:2 * j + 2, :], bank[6][:, :])


def second_vector(nc, m, dve, AX, steps0):
    V = nc.vector
    PROJ, bank, X, Y, HT = m.PROJ, m.bank, m.X, m.Y, m.HT
    steps = steps0
    td = Tally(LAYERS * PER["tdr"])

    def link(ins):
        nonlocal steps
        steps += 1
        ins.then_inc(m.dve_step, 1)
        dve.wait_ge(m.dve_step, steps)

    def copy(dst, src):
        dve.wait_ge(m.td_ready, td.next())
        V.tensor_copy(dst, src).then_inc(m.td_copied, 1)

    sq, rr = LAYERS * PER["q"], LAYERS * PER["rout"]

    dve.wait_ge(m.sq_ready, sq + 1)
    V.tensor_scalar(m.rin[:, 0:2], m.ss[:, 0:2], 1.0 / D, EPS, ALU.mult, ALU.add).then_inc(m.rin_ready, 1)
    dve.wait_ge(m.rows_in, 16 * 4)
    link(V.scalar_tensor_tensor(m.sc, m.sc, 1.0, m.gn, ALU.add, ALU.mult))
    dve.wait_ge(m.rms_ready, rr + 1)
    for t in range(TT):
        last = V.scalar_tensor_tensor(X[:, t, :], X[:, t, :], m.rms[:, t:t + 1], m.fn, ALU.mult, ALU.mult)
    last.then_inc(m.x_normed, 1)
    dve.wait_ge(m.sq_ready, sq + 2)
    V.tensor_scalar(m.rin[:, 0:2], m.ss[:, 0:2], 1.0 / D, EPS, ALU.mult, ALU.add).then_inc(m.rin_ready, 1)
    dve.wait_ge(m.rms_ready, rr + 2)
    for t in range(TT):
        last = V.scalar_tensor_tensor(Y[:, t, :], X[:, t, :], m.rms[:, t:t + 1], m.sc, ALU.mult, ALU.mult)
    link(last)
    for t in range(TT):
        last = V.tensor_tensor(Y[:, t, :], Y[:, t, :], m.sh, ALU.add)
    last.then_inc(m.h_ready, 1)
    for j in range(1, 8, 2):
        copy(HT[:, 2 * j:2 * j + 2, :], bank[7][:, :])
    dve.wait_ge(m.ta_copied, LAYERS * PER["ta"] + 1 + 5)
    dve.wait_ge(m.cst2_in, 16 * 11)

    stage = [0, 0]
    rec = 0
    bc_i = lambda x: x.unsqueeze(2).to_broadcast([P, 4, P])
    bc_h = lambda x: x.unsqueeze(1).to_broadcast([P, 4, P])
    flat = lambda x: x.rearrange("p h n -> p (h n)")
    v4 = lambda ps: ps[:, :].rearrange("p (h n) -> p h n", n=P)

    def columns(t, b):
        return V.tensor_tensor(m.x_[b], bc_h(m.uincl), bc_i(m.g[:, t, 4 * b:4 * b + 4]), ALU.mult)

    def delta(kind, t, n):
        nonlocal rec
        if kind == "gates":
            V.memset(flat(m.state), 0.0).then_inc(m.state_zero, 1)
            for b in (0, 1):
                columns(0, b).then_inc(m.bd_ready[b], 1)
            dve.wait_ge(m.gc_ready, 1)
            V.tensor_copy(m.gsum[:, :, :], bank[4][:, 0:16].rearrange("p (t h) -> p t h", t=TT)).then_inc(m.gc_copied, 1)
            dve.wait_ge(m.gc_copied, 1)
            dve.wait_ge(m.egc_ready, 1)
            link(V.tensor_tensor(m.beg[:, :, :], m.beta[:, :, :], m.egc[:, :, :], ALU.mult))
            return
        if kind in ("new", "state"):
            c = slice(64 * n, 64 * n + 64)
            rec += 1
            dve.wait_ge(m.r_ready, rec)
            if kind == "new":
                for b in (0, 1):
                    x = m.u[c, 4 * b:4 * b + 4, :]
                    last = V.tensor_tensor(x, x, bank[4 + b][c, :].rearrange("p (h n) -> p h n", n=P), ALU.subtract)
                last.then_inc(m.r_done, 1)
            else:
                for b in (0, 1):
                    x = m.state[:, 4 * b:4 * b + 4, :]
                    last = V.tensor_tensor(x, x, m.egl[:, t, 4 * b:4 * b + 4, n:n + 1].to_broadcast([P, 4, P]), ALU.mult)
                link(last)
                for b in (0, 1):
                    x = m.state[:, 4 * b:4 * b + 4, :]
                    last = V.tensor_tensor(x, x, v4(bank[4 + b]), ALU.add)
                last.then_inc(m.r_done, 1)
                if n == 1 and t == 0:
                    for b in (0, 1):
                        columns(1, b).then_inc(m.bd_ready[b], 1)
            return
        for b in (0, 1):
            A, B = bank[4 + 2 * b], bank[5 + 2 * b]
            hs = slice(4 * b, 4 * b + 4)
            stage[b] += 1
            dve.wait_ge(m.b_ready[b], stage[b])
            mask = lambda i: V.tensor_tensor(m.mt[b], m.lt[b], bc_h(m.level[i]), ALU.mult)
            if kind == "expand":
                V.tensor_copy(flat(m.kq[:, hs, :]), A[:, :])
                V.tensor_tensor(m.dt[b], v4(B), bc_i(m.gsum[:, t, hs]), ALU.subtract)
                link(V.tensor_copy(m.gl[:, t, hs, :], v4(B)[:, :, 63::64]))
                V.tensor_tensor(m.dt[b], m.dt[b], bc_h(m.neg), ALU.add).then_inc(m.dx_ready[b], 1)
                V.tensor_tensor(m.x_[b], bc_h(m.ident), bc_i(m.beta[:, t, hs]), ALU.mult)
                dve.wait_ge(m.d_ready[b], t + 1)
                kd = m.kd[:, hs]
                V.tensor_copy(kd[0:64, :], m.dt[b][0:64, :, 63])
                link(V.tensor_copy(kd[64:P, :], m.dt[b][64:P, :, 127]))
                k2 = PROJ[:, t, BK + 2 * b * P:BK + (2 * b + 2) * P].rearrange("p (h n) -> p h n", n=P)
                k4 = k2.unsqueeze(2).to_broadcast([P, 2, 2, P])
                V.tensor_tensor(m.kdec[:, hs, :].rearrange("p (h r) n -> p h r n", r=2), k4,
                                kd.rearrange("p (h r) -> p h r", r=2).unsqueeze(3).to_broadcast([P, 2, 2, P]), ALU.mult)\
                    .then_inc(m.b_done[b], 1)
            elif kind == "gram":
                link(V.tensor_tensor(m.lt[b], m.dt[b], v4(B), ALU.mult))
                r4 = lambda x: x.rearrange("p (h r) n -> p h r n", r=2)
                g4 = lambda i: v4(A)[:, 2 * i:2 * i + 2, :].unsqueeze(2).to_broadcast([P, 2, 2, P])
                link(V.tensor_tensor(r4(m.lt[b]), r4(m.lt[b]), g4(0), ALU.mult))
                V.tensor_tensor(r4(m.qkt[:, hs, :]), r4(m.dt[b]), g4(1), ALU.mult)
                link(mask(0))
                V.tensor_tensor(m.tt[b], bc_h(m.ident), m.mt[b], ALU.subtract).then_inc(m.b_done[b], 1)
            elif kind == "first":
                V.tensor_tensor(m.t_[b], bc_h(m.ident), v4(A), ALU.subtract)
                mask(1).then_inc(m.b_done[b], 1)
            elif kind == "x":
                V.tensor_copy(flat(m.x_[b]), A[:, :]).then_inc(m.b_done[b], 1)
            elif kind == "grow":
                if n < 5:
                    V.tensor_tensor(m.t_[b], m.t_[b], v4(A), ALU.subtract)
                    V.tensor_tensor(m.tt[b], m.tt[b], v4(B), ALU.subtract)
                    mask(n + 1).then_inc(m.b_done[b], 1)
                else:
                    V.tensor_tensor(m.tt[b], m.tt[b], v4(B), ALU.subtract)
                    V.tensor_tensor(m.x_[b], PROJ[:, t, BV + 4 * b * P:BV + (4 * b + 4) * P].rearrange("p (h n) -> p h n", n=P),
                                    bc_i(m.beta[:, t, hs]), ALU.mult)
                    r4 = lambda x: x.rearrange("p (h r) n -> p h r n", r=2)
                    for dst, src, s in ((m.mt[b], BK, m.beg), (m.t_[b], BQ, m.egc)):
                        x = PROJ[:, t, src + 2 * b * P:src + (2 * b + 2) * P].rearrange("p (h n) -> p h n", n=P)
                        last = V.tensor_tensor(r4(dst), x.unsqueeze(2).to_broadcast([P, 2, 2, P]),
                                               s[:, t, hs].rearrange("p (h r) -> p h r", r=2).unsqueeze(3).to_broadcast([P, 2, 2, P]), ALU.mult)
                    last.then_inc(m.b_done[b], 1)
            elif kind == "apply":
                V.tensor_copy(flat(m.u[:, hs, :]), A[:, :])
                V.tensor_copy(flat(m.wt[:, hs, :]), B[:, :]).then_inc(m.b_done[b], 1)
            elif kind == "qdec":
                V.tensor_copy(flat(m.qd[:, hs, :]), A[:, :]).then_inc(m.b_done[b], 1)

    at = 0
    for p, u in enumerate(ORDER2):
        gaps = GAPS[at:at + PIECES] if p >= 5 else ()
        at += len(gaps)
        for g in gaps:
            delta(*g)
        if p < 4:
            copy(m.raw[p % 2][:, 2:4, :], bank[7][:, :])
            dve.wait_ge(m.td_copied, LAYERS * PER["td"] + td.n + 1)
            dve.wait_ge(m.ta_copied, LAYERS * PER["ta"] + 1 + 5 + max(1, 2 * p))
            raw, out = m.raw[p % 2], m.conv[p % 2]
            for j in (3, 2, 1, 0):
                for b in range(4):
                    w = m.cwt[:, 16 * j + 4 * p + b:16 * j + 4 * p + b + 1]
                    d = 3 - j
                    if d == 0:
                        last = V.tensor_scalar(out[:, b, :], raw[:, b, :], w, None, ALU.mult)
                    else:
                        last = V.scalar_tensor_tensor(out[:, b, d:S], raw[:, b, 0:S - d], w, out[:, b, d:S], ALU.mult, ALU.add)
                if j:
                    link(last)
            last.then_inc(m.cv_ready, 1)
        if 1 <= p <= 4:
            copy(PROJ[:, 1, BQ + (p - 1) * U:BQ + p * U], bank[7][:, :])
        if p == 4:
            dve.wait_ge(m.beta_ready, 1)
            link(V.tensor_tensor(m.z[:, :, :], PROJ[:, :, BA:BA + 8], m.sm2[:, 8:16].unsqueeze(1).to_broadcast([P, TT, 8]), ALU.add))
            V.scalar_tensor_tensor(m.nz[:, :, :], m.z[:, :, :], -1.0, m.z[:, :, :], ALU.mult, ALU.min).then_inc(m.z_ready, 1)
            dve.wait_ge(m.ez_ready, 2)
            link(V.scalar_tensor_tensor(m.g[:, :, :], m.z[:, :, :], 0.0, m.ez[:, :, :], ALU.max, ALU.add))
            V.scalar_tensor_tensor(m.g[:, :, :], m.g[:, :, :], -1.0, m.ea[:, :].unsqueeze(1).to_broadcast([P, TT, 8]),
                                   ALU.mult, ALU.mult).then_inc(m.g_done, 1)
            dve.wait_ge(m.g_done, 1)
            dve.wait_ge(m.ta_copied, LAYERS * PER["ta"] + 1 + 5 + 8)
            dve.wait_ge(m.td_copied, LAYERS * PER["td"] + td.n + 1)
            qk = PROJ[:, :, BQ:BV].rearrange("p t (h n) -> p t h n", n=P)
            sq_ = m.sq2.rearrange("p t (h n) -> p t h n", n=P)
            link(V.tensor_tensor(sq_, qk, qk, ALU.mult))
            r16 = m.rin16[:, :].rearrange("p (t h) -> p t h", t=TT)
            link(V.tensor_reduce(r16, sq_, AX.X, ALU.add))
            V.tensor_scalar(m.rin16[:, :], m.rin16[:, :], EPS, None, ALU.add).then_inc(m.rin_ready, 1)
            dve.wait_ge(m.rms_ready, rr + 3)
            o16 = m.rms16[:, :].rearrange("p (t h) -> p t h", t=TT)
            link(V.tensor_scalar(o16[:, :, 0:4], o16[:, :, 0:4], SC128, None, ALU.mult))
            link(V.tensor_tensor(qk, qk, o16.unsqueeze(3).to_broadcast([P, TT, 8, P]), ALU.mult))
    for g in GAPS[at:]:
        delta(*g)
    dve.wait_ge(m.pj_copied, LAYERS * PER["pja"] + len(ORDER2))
    for t in range(TT):
        V.tensor_copy(m.ck4[:, t, :].rearrange("p (k r n) -> p k r n", k=2, r=2),
                      PROJ[:, t, C2K:C2K + P].rearrange("p (k n) -> p k n", k=2).unsqueeze(2).to_broadcast([P, 2, 2, 64]))\
            .then_inc(m.ck_half, 1)
    dve.wait_ge(m.ck_half, 2)
    dve.sem_inc(m.ck_ready, 1)
    for dst in (HT[:, 2:4, :], HT[:, 6:8, :], HT[:, 10:12, :]):
        copy(dst, bank[7][:, :])
    s_n, o_n = LAYERS * PER["s"], LAYERS * PER["o"]
    e_n = LAYERS * PER["e"]

    def normed(t):
        nonlocal rr
        o = Y[:, t, U:U + 1024].rearrange("p (h n) -> p h n", n=P)
        z = PROJ[:, t, BZ:BZ + 1024].rearrange("p (h n) -> p h n", n=P)
        sq_ = m.sqo.rearrange("p (h n) -> p h n", n=P)
        link(V.tensor_tensor(sq_, o, o, ALU.mult))
        link(V.tensor_reduce(m.rin16[:, 0:8], sq_, AX.X, ALU.add))
        V.tensor_scalar(m.rin16[:, 0:8], m.rin16[:, 0:8], 1.0 / P, EPS, ALU.mult, ALU.add).then_inc(m.rin_ready, 1)
        link(V.tensor_tensor(z, z, m.sm2[:, 24:152].unsqueeze(1).to_broadcast([P, 8, P]), ALU.mult))
        dve.wait_ge(m.rms_ready, LAYERS * PER["rout"] + 4 + t)
        link(V.tensor_tensor(o, o, m.rms16[:, 0:8].unsqueeze(2).to_broadcast([P, 8, P]), ALU.mult))
        V.tensor_tensor(o, o, z, ALU.mult).then_inc(m.on_done, 1)

    dve.wait_ge(m.oc_done, 2 * TT)
    for n, (kind, g) in enumerate(PAIRS2):
        for i in (0, 1):
            h = 2 * g + i
            s_n += 1
            dve.wait_ge(m.s_ready, s_n)
            pb, ps = m.PB[:, i, :, :], bank[4][:, :].rearrange("p (t n) -> p t n", t=TT)
            V.scalar_tensor_tensor(pb, m.rel[kind], -SLOPES8[h] / SC64, ps, ALU.mult, ALU.add).then_inc(m.s_used, 1)
            dve.wait_ge(m.s_used, s_n + 1)
            link(V.tensor_reduce(m.mx[:, i, :], pb, AX.X, ALU.max))
            if kind == "C":
                link(V.tensor_scalar(m.mm[:, i, :], m.mx[:, i, :], SC64, m.sm2[:, 16 + h:17 + h], ALU.mult, ALU.max))
                last = V.tensor_scalar(m.nm[:, i, :], m.mm[:, i, :], -1.0, None, ALU.mult)
            else:
                last = V.tensor_scalar(m.nm[:, i, :], m.mx[:, i, :], -SC64, None, ALU.mult)
            last.then_inc(m.m_ready, 1)
        if n < TT:
            normed(n)
        for i in (0, 1):
            h = 2 * g + i
            e_n += 1
            dve.wait_ge(m.e_ready, e_n)
            if kind == "A":
                pb = m.PB[:, i, :, :]
                for t in range(TT):
                    last = V.scalar_tensor_tensor(pb[:, t, :], pb[:, t, :], 1.0, m.cnt[:, t, :], ALU.mult, ALU.mult,
                                                  accum_out=m.den[:, i, t:t + 1])
                last.then_inc(m.c_ready, 1)
                dve.wait_ge(m.c_ready, LAYERS * PER["c"] + h + 1)
            else:
                link(V.tensor_tensor(m.den[:, i, :], m.den[:, i, :], m.es[:, i, :], ALU.add))
            link(V.reciprocal(m.rec[:, i, :], m.den[:, i, :]))
            o_n += 1
            dve.wait_ge(m.o_ready, o_n)
            to = (0 if kind == "A" else 1536) + h * 64
            for t in range(TT):
                last = V.tensor_scalar(Y[:, t, to:to + 64], bank[5][:, t * P:t * P + 64], m.rec[:, i, t:t + 1], None, ALU.mult)
            last.then_inc(m.o_used, 1)
    for j in range(1, 8, 2):
        copy(HT[:, 2 * j:2 * j + 2, :], bank[7][:, :])
    dve.wait_ge(m.rows_in, 16 * 5)
    for n in range(4):
        v = len(ORDER2) + n
        dve.wait_ge(m.hu_used, LAYERS * PER["hu"] + RING + 2 * (v + 1))
        for t in range(TT):
            last = V.tensor_tensor(m.tmp[:, t, :], bank[2 * (v % 2) + t][:, :], m.g1[:, n * U:(n + 1) * U], ALU.mult)
        link(last)
        for t in range(TT):
            x = X[:, t, n * U:(n + 1) * U]
            last = V.tensor_tensor(x, x, m.tmp[:, t, :], ALU.add)
        last.then_inc(m.xo, 1)
        dve.wait_ge(m.xo, 4 * LAYERS + 2 + n)
    return steps


def second_constants():
    i = np.arange(P)
    same = (i[:, None] // 64) == (i[None, :] // 64)
    c = np.zeros((P, 9 * P), np.float32)
    for l in range(6):
        s = 1 << l
        r, k = i[None, :] // s, i[:, None] // s
        c[:, l * P:(l + 1) * P] = (r % 2 == 1) & (k == r - 1)
    u = (i[:, None] <= i[None, :]) & same
    c[:, K_U:K_U + P] = u
    c[:, K_NEG:K_NEG + P] = np.where(u, 0.0, -1e30)
    c[:, K_ONE:K_ONE + P] = 1.0
    q, k = np.arange(S)[:, None], np.arange(S)[None, :]
    d = q - k
    cnt = ((d >= 0) & (d <= 128)).astype(np.float32) + ((d >= 0) & (d % 4 == 0)) + ((d >= 0) & (d % 16 == 0))
    rel_a = np.where(cnt > 0, d, BIG)
    rel_c = np.where((d >= 0) & (d <= 127), d, BIG)
    tile = lambda x: np.ascontiguousarray(x.reshape(TT, P, S).transpose(1, 0, 2).reshape(P, TT * S)).astype(np.float32)
    return {"cst2": c, "rel_a": tile(rel_a), "rel_c": tile(rel_c), "cnt_a": tile(cnt)}


EXPERTS, GROUPS, EPG, FF = 32, 4, 8, 512
SLOTS = 64
PAIRS = EXPERTS // 2
NS = 6
XR = EXPERTS + 2
TA2, TD2 = 37, 19
HU2 = LAYERS * PER["hu"] + RING + 30
PERP = dict(hu=12, tx=6, dn=4, dnr=2, sc=8, hid=1, gm=1, silu=1)
PREP = dict(tx=5, gm=1)
R_IOTA, R_I4, R_I32, R_UT, R_ONE, CR = 0, 64, 68, 100, 228, 356


def per_round(name):
    return PREP.get(name, 0) + PAIRS * PERP[name] + (8 if name == "sc" else 0)


def moe_buffers(m):
    flat = m.PROJ[:, :, :].rearrange("p t n -> p (t n)")
    m.slots = [m.ring[:, i, :] for i in range(4)] + [flat[:, 0:HALF], flat[:, HALF:2 * HALF]]
    qk = m.QK[:, :, :].rearrange("p k n -> p (k n)")
    m.gn2, m.sc2, m.sh2 = qk[:, 0:D], qk[:, D:2 * D], flat[:, 2 * HALF:2 * HALF + D]
    at = 2 * HALF + D
    m.rw = flat[:, at:at + 576].rearrange("p (k n) -> p k n", k=KB)
    m.rb = flat[:, at + 576:at + 612]
    m.cst3 = flat[:, at + 612:at + 612 + CR]
    m.xg = m.QK[:, 0:8, :].rearrange("p k n -> p (k n)").rearrange("p (k n) -> p k n", n=P)
    m.ye = qk[:, D:2 * D]
    m.acc = m.HT[:, :, :].rearrange("p k n -> p (k n)").rearrange("p (t n) -> p t n", t=TT)
    m.hid = m.dist[:, :, :].rearrange("p t n -> p (t n)")
    m.hs = m.distm[:, :, :].rearrange("p t n -> p (t n)")
    m.hidt = m.PT[:, :, :, :].rearrange("p a b c -> p (a b) c")
    pb = m.PB[:, :, :, :].rearrange("p a t n -> p (a t n)")
    m.gm, m.gg = (pb[:, i * S:(i + 1) * S].rearrange("p (t n) -> p t n", t=TT) for i in (0, 1))
    m.sca, m.scb = pb[:, 2 * S:3 * S], pb[:, 3 * S:4 * S]
    m.g2, m.fng = m.ring[:, 0, 0:D], m.ring[:, 0, D:2 * D]
    rq = m.ropeq[:, :, :, :].rearrange("p t h n -> p (t h n)")
    cbf = m.cb[:, :, :].rearrange("p k n -> p (k n)")
    tile = lambda x, n: x[:, 0:TT * n].rearrange("p (t n) -> p t n", t=TT)
    m.lg = tile(rq[:, 0:72], 36)
    m.em, m.cand, m.o1, m.o2, m.sel = (tile(rq[:, 80 + 64 * i:144 + 64 * i], 32) for i in range(5))
    m.ps, m.gt = tile(cbf[:, 0:68], XR), tile(cbf[:, 72:140], XR)
    m.ge, m.og = tile(cbf[:, 144:152], 4), tile(cbf[:, 152:160], 4)
    m.v = [cbf[:, 160 + 2 * i:162 + 2 * i] for i in range(10)]
    m.cmax = cbf[:, 180:184]
    m.yacc = m.tmp


def moe_sync(m, sp):
    a = m.a
    sp.wait_ge(m.o_used, LAYERS * PER["o"] + 16 + 1)
    sp.wait_ge(m.on_done, TT)
    for dst, src in ((m.gn2, a["norm2_g_2"]), (m.sc2, m.mod[:, 4 * D:5 * D]), (m.sh2, m.mod[:, 3 * D:4 * D]),
                     (m.rb[:, 0:4], a["router_group_b_2"]), (m.rb[:, 4:36], a["router_expert_b_2"])):
        sp.dma_start(dst, src.partition_broadcast(P)).then_inc(m.rows2_in, 16)
    sp.dma_start(m.rw[:, :, 0:4], a["router_group_w_2"][0].rearrange("(k p) n -> p k n", p=P)).then_inc(m.rows2_in, 16)
    sp.dma_start(m.rw[:, :, 4:36], a["router_expert_w_2"][0].rearrange("(k p) n -> p k n", p=P)).then_inc(m.rows2_in, 16)
    sp.dma_start(m.cst3, a["cst3"]).then_inc(m.rows2_in, 16)

    sp.wait_ge(m.hu_used, HU2)
    sp.wait_ge(m.xo, 4 * LAYERS + 1 + 4)

    def pair_loads(p):
        expert = lambda w, e: w[0, bass.ds(2 * p + e, 1)].rearrange("a k n -> (a k) n")
        for w in ("expert_w_gate_2", "expert_w_up_2"):
            for j in (0, 1):
                for e in (0, 1):
                    yield expert(a[w], e)[j * 1024:(j + 1) * 1024, :], 8
        for j in (0, 1):
            for e in (0, 1):
                yield expert(a["expert_w_down_2"], e)[:, j * 1024:(j + 1) * 1024], 4

    def load(n, src, k):
        sp.dma_start(m.slots[n % NS].rearrange("p (k n) -> p k n", k=k),
                     src.rearrange("(k p) n -> p k n", p=P)).then_inc(m.x_in[n % NS], 16)

    for n, (src, k) in enumerate(pair_loads(0)):
        if n == NS:
            sp.wait_ge(m.rounds_ready, 1)
            rounds = sp.value_load(m.rounds[0:1, 0:1], min_val=1, max_val=4)
        if n >= NS:
            sp.wait_ge(m.hu_used, HU2 + n - NS + 1)
        load(n, src, k)
    with sp.Fori(1, rounds * PAIRS) as pp:
        for n, (src, k) in enumerate(pair_loads(pp % PAIRS)):
            sp.wait_ge(m.hu_used, HU2 + pp * 12 + n - NS + 1)
            load(n, src, k)
    sp.wait_ge(m.moe_done, 1)
    sp.dma_start(m.g2, m.mod[:, 5 * D:6 * D].partition_broadcast(P)).then_inc(m.rows3_in, 16)
    sp.dma_start(m.fng, a["final_norm_g_2"].rearrange("(a n) -> a n", a=1).partition_broadcast(P)).then_inc(m.rows3_in, 16)


def moe_gpsimd(nc, m, pool):
    for n in range(2):
        pool.wait_ge(m.rin_ready, LAYERS * PER["rin"] + 5 + n + 1)
        nc.gpsimd.tensor_tensor(m.rms[:, 0:2], m.rin[:, 0:2], m.half[:, 0:2], ALU.pow).then_inc(m.rms_ready, 1)


def moe_tensor(nc, m, pe):
    mm = nc.tensor.matmul
    bank, H = m.bank, m.Y
    ta, td = Tally(LAYERS * PER["ta"] + TA2, 1), Tally(LAYERS * PER["td"] + TD2, 1)
    pe.wait_ge(m.h2_ready, 1)
    for j in range(8):
        t, ready, cop, ps = (ta, m.ta_ready, m.ta_copied, bank[6]) if j % 2 == 0 else (td, m.td_ready, m.td_copied, bank[7])
        pe.wait_ge(cop, t.now())
        for i, (b, tt) in enumerate([(b, tt) for b in (0, 1) for tt in range(TT)]):
            last = nc.tensor.transpose(ps[:, i * P:(i + 1) * P], H[:, tt, (2 * j + b) * P:(2 * j + b + 1) * P], m.ident)
        last.then_inc(ready, 1)
        t.next()
    pe.wait_ge(m.ta_copied, ta.now())
    pe.wait_ge(m.td_copied, td.now())
    pe.wait_ge(m.rows2_in, 16 * 8)
    for t in range(TT):
        for k in range(KB):
            last = mm(bank[0][:, t * 36:(t + 1) * 36], m.HT[:, k, t * P:(t + 1) * P], m.rw[:, k, :], start=k == 0, stop=k == KB - 1)
    last.then_inc(m.rt_ready, 1)
    ut, one = m.cst3[:, R_UT:R_UT + P], m.cst3[:, R_ONE:R_ONE + P]
    pe.wait_ge(m.sel_ready, 1)
    mm(bank[1][:, 0:32], ut, m.sel[:, 0, :], start=True, stop=True)
    mm(bank[1][:, 32:64], ut, m.sel[:, 1, :], start=True, stop=False)
    mm(bank[1][:, 32:64], one, m.sel[:, 0, :], start=False, stop=True)
    mm(bank[1][:, 64:96], one, m.sel[:, 0, :], start=True, stop=False)
    mm(bank[1][:, 64:96], one, m.sel[:, 1, :], start=False, stop=True).then_inc(m.rt_ready, 1)
    pe.sem_inc(m.moe_start, 1)
    pe.wait_ge(m.rounds_ready, 1)
    rounds = pe.value_load(m.rounds[0:1, 0:1], min_val=1, max_val=4)

    def gather(tx, gm):
        pe.wait_ge(m.gm_ready, gm)
        for q in range(4):
            pe.wait_ge(m.tx_copied, tx.now())
            ps = bank[2 + (tx.n - 1) % 2]
            for i in range(4):
                k = 4 * q + i
                for t in range(TT):
                    last = mm(ps[:, i * P:(i + 1) * P], H[:, t, k * P:(k + 1) * P], m.gm[:, t, :], start=t == 0, stop=t == TT - 1)
            last.then_inc(m.tx_ready, 1)
            tx.next()
        pe.wait_ge(m.tx_copied, tx.now())
        ps = bank[2 + (tx.n - 1) % 2]
        for t in range(TT):
            last = nc.tensor.transpose(ps[:, t * P:(t + 1) * P], m.gg[:, t, :], m.ident)
        last.then_inc(m.tx_ready, 1)
        tx.next()

    def scatter(sc):
        for t in range(TT):
            for c in range(4):
                pe.wait_ge(m.sc_used, sc.now())
                mm(bank[6 + c % 2][:, :], m.sca[:, t * P:(t + 1) * P], m.ye[:, c * U:(c + 1) * U], start=True, stop=True)\
                    .then_inc(m.sc_ready, 1)
                sc.next()

    with pe.Fori(0, rounds) as r:
        tx = Tally(r * per_round("tx"), 1)
        gather(tx, r * per_round("gm") + 1)
        with pe.Fori(0, PAIRS) as p:
            rp = r * PAIRS + p
            tx = Tally(r * per_round("tx") + PREP["tx"] + p * PERP["tx"], 1)
            load = [Tally(rp * 32) for _ in range(NS)]
            hu = 0

            def weights(n, k):
                return m.slots[n % NS].rearrange("p (k n) -> p k n", k=k)

            def arrived(n):
                pe.wait_ge(m.x_in[n % NS], load[n % NS].next(16))

            pe.wait_ge(m.tx_copied, tx.now() + 1)
            for side in (0, 1):
                for j in (0, 1):
                    arrived(hu)
                    arrived(hu + 1)
                    for k in range(8):
                        for e in (0, 1):
                            s = slice(64 * e, 64 * e + 64)
                            last = mm(bank[side][s, :], m.xg[:, 8 * j + k, s], weights(hu + e, 8)[:, k, :],
                                      start=j == 0 and k == 0, stop=j == 1 and k == 7)
                            if k == 7:
                                last.then_inc(m.hu_used, 1)
                    hu += 2
            pe.wait_ge(m.dn_copied, rp * 4 + 2)
            scatter(Tally(r * per_round("sc") + p * 8, 1))
            gather(tx, r * per_round("gm") + 2 + p)
            pe.wait_ge(m.hid_ready, rp + 1)
            pe.wait_ge(m.tx_copied, tx.now())
            ps = bank[2 + (tx.n - 1) % 2]
            for f in range(4):
                last = nc.tensor.transpose(ps[:, f * P:(f + 1) * P], m.hid[:, f * P:(f + 1) * P], m.ident)
            last.then_inc(m.tx_ready, 1)
            tx.next()
            pe.wait_ge(m.tx_copied, tx.now() + 1)
            for j in (0, 1):
                arrived(hu)
                arrived(hu + 1)
                for c in (0, 1):
                    n = 2 * j + c
                    pe.wait_ge(m.dn_copied, rp * 4 + n + 1)
                    for f in range(4):
                        for e in (0, 1):
                            s = slice(64 * e, 64 * e + 64)
                            last = mm(bank[4 + n % 2][s, :], m.hidt[:, f, s], weights(hu + e, 4)[:, f, c * U:(c + 1) * U],
                                      start=f == 0, stop=f == 3)
                            if f == 3 and c == 1:
                                last.then_inc(m.hu_used, 1)
                    if c == 0:
                        last.then_inc(m.dn_ready, 1)
                hu += 2
        pe.wait_ge(m.dn_copied, (r + 1) * (PAIRS * 4) + 2)
        scatter(Tally(r * per_round("sc") + PAIRS * 8, 1))
        pe.wait_ge(m.sc_used, (r + 1) * per_round("sc") + 2)
    pe.sem_inc(m.moe_done, 1)


def moe_scalar(nc, m, act, ACT):
    A_ = nc.scalar.activation
    X, Y, bank = m.X, m.Y, m.bank
    act.wait_ge(m.xo, 4 * LAYERS + 1 + 4)
    for t in range(TT):
        last = A_(Y[:, t, :], X[:, t, :], ACT.Square, accum_out=m.ss[:, t:t + 1])
    last.then_inc(m.sq_ready, 1)
    for i, j in enumerate(range(0, 8, 2)):
        act.wait_ge(m.ta_ready, LAYERS * PER["ta"] + TA2 + i + 1)
        A_(m.HT[:, 2 * j:2 * j + 2, :], bank[6][:, :], ACT.Copy).then_inc(m.ta_copied, 1)
    act.wait_ge(m.gd_ready, 1)
    A_(m.ge[:, :, :], m.ge[:, :, :], ACT.Exp).then_inc(m.rexp_ready, 1)
    act.wait_ge(m.vd_ready, 1)
    A_(m.v[3], m.v[3], ACT.Exp).then_inc(m.rexp_ready, 1)
    act.wait_ge(m.rounds_ready, 1)
    rounds = act.value_load(m.rounds[0:1, 0:1], min_val=1, max_val=4)
    act.sem_inc(m.tx_copied, 2)
    act.sem_inc(m.dn_copied, 2)

    def gathered(tx, keep):
        for q in range(4):
            act.wait_ge(m.tx_ready, tx.next())
            if q == 0 and keep:
                A_(m.sca, m.scb, ACT.Copy).then_inc(m.sca_ready, 1)
            A_(m.xg[:, 4 * q:4 * q + 4, :], bank[2 + (tx.n - 1) % 2][:, :], ACT.Copy).then_inc(m.tx_copied, 1)
        act.wait_ge(m.tx_ready, tx.next())
        A_(m.scb, bank[2 + (tx.n - 1) % 2][:, 0:S], ACT.Copy).then_inc(m.tx_copied, 1)

    with act.Fori(0, rounds) as r:
        gathered(Tally(r * per_round("tx")), False)
        with act.Fori(0, PAIRS) as p:
            rp = r * PAIRS + p
            tx = Tally(r * per_round("tx") + PREP["tx"] + p * PERP["tx"])
            act.wait_ge(m.hu_used, HU2 + rp * 12 + 4)
            A_(m.hs, bank[0][:, :], ACT.Silu).then_inc(m.silu_ready, 1)
            act.wait_ge(m.tx_copied, tx.now() + 2)
            gathered(tx, True)
            act.wait_ge(m.tx_ready, tx.next())
            A_(m.hidt[:, :, :], bank[2 + (tx.n - 1) % 2][:, :], ACT.Copy).then_inc(m.tx_copied, 1)
            for n in range(4):
                if n % 2 == 0:
                    act.wait_ge(m.dn_ready, rp * 2 + n // 2 + 1)
                else:
                    act.wait_ge(m.hu_used, HU2 + rp * 12 + 8 + 2 * (n // 2 + 1))
                A_(m.ye[:, n * U:(n + 1) * U], bank[4 + n % 2][:, :], ACT.Copy).then_inc(m.dn_copied, 1)
    act.wait_ge(m.x_final, 1)
    for t in range(TT):
        last = A_(Y[:, t, :], X[:, t, :], ACT.Square, accum_out=m.ss[:, t:t + 1])
    last.then_inc(m.sq_ready, 1)


def moe_vector(nc, m, dve, AX, steps0):
    V = nc.vector
    X, Y, bank = m.X, m.Y, m.bank
    steps = steps0

    def link(ins):
        nonlocal steps
        steps += 1
        ins.then_inc(m.dve_step, 1)
        dve.wait_ge(m.dve_step, steps)

    sq, rr = LAYERS * PER["q"] + 2, LAYERS * PER["rout"] + 5
    dve.wait_ge(m.sq_ready, sq + 1)
    V.tensor_scalar(m.rin[:, 0:2], m.ss[:, 0:2], 1.0 / D, EPS, ALU.mult, ALU.add).then_inc(m.rin_ready, 1)
    dve.wait_ge(m.rows2_in, 16 * 8)
    link(V.scalar_tensor_tensor(m.sc2, m.sc2, 1.0, m.gn2, ALU.add, ALU.mult))
    dve.wait_ge(m.rms_ready, rr + 1)
    for t in range(TT):
        last = V.scalar_tensor_tensor(Y[:, t, :], X[:, t, :], m.rms[:, t:t + 1], m.sc2, ALU.mult, ALU.mult)
    link(last)
    for t in range(TT):
        last = V.tensor_tensor(Y[:, t, :], Y[:, t, :], m.sh2, ALU.add)
    last.then_inc(m.h2_ready, 1)
    for i, j in enumerate(range(1, 8, 2)):
        dve.wait_ge(m.td_ready, LAYERS * PER["tdr"] + TD2 + i + 1)
        V.tensor_copy(m.HT[:, 2 * j:2 * j + 2, :], bank[7][:, :]).then_inc(m.td_copied, 1)

    lg, em, cand, o1, o2, sel = m.lg, m.em, m.cand, m.o1, m.o2, m.sel
    gmax, gi, pg, dv, v1, i1, v2, i2, g1, g2 = m.v
    over = lambda x, n: x.unsqueeze(2).to_broadcast([P, TT, n])
    both = lambda at, n: m.cst3[:, at:at + n].unsqueeze(1).to_broadcast([P, TT, n])
    i4, i32 = both(R_I4, 4), both(R_I32, 32)
    dve.wait_ge(m.rt_ready, 1)
    link(V.tensor_tensor(lg, bank[0][:, 0:72].rearrange("p (t n) -> p t n", t=TT), m.rb.unsqueeze(1).to_broadcast([P, TT, 36]), ALU.add))
    gl = lg[:, :, 0:4]

    def first_max(x, n, iota, top, index, onehot, tmp):
        link(V.tensor_reduce(top, x, AX.X, ALU.max))
        link(V.tensor_tensor(tmp, x, over(top, n), ALU.is_equal))
        link(V.scalar_tensor_tensor(tmp, tmp, -1000.0, iota, ALU.mult, ALU.add))
        link(V.tensor_reduce(index, tmp, AX.X, ALU.min))
        link(V.tensor_scalar(index, index, 1000.0, None, ALU.add))
        link(V.tensor_tensor(onehot, iota, over(index, n), ALU.is_equal))

    first_max(gl, 4, i4, gmax, gi, m.og, cand[:, :, 0:4])
    V.tensor_tensor(m.ge, gl, over(gmax, 4), ALU.subtract).then_inc(m.gd_ready, 1)
    link(V.tensor_scalar(m.og, m.og, 1e30, -1e30, ALU.mult, ALU.add))
    link(V.tensor_tensor(em.rearrange("p t (g n) -> p t g n", g=GROUPS), lg[:, :, 4:36].rearrange("p t (g n) -> p t g n", g=GROUPS),
                         m.og.unsqueeze(3).to_broadcast([P, TT, GROUPS, EPG]), ALU.add))
    first_max(em, 32, i32, v1, i1, o1, cand)
    link(V.scalar_tensor_tensor(em, o1, -1e32, em, ALU.mult, ALU.add))
    first_max(em, 32, i32, v2, i2, o2, cand)
    V.tensor_tensor(dv, v2, v1, ALU.subtract).then_inc(m.vd_ready, 1)
    V.tensor_tensor(sel, o1, o2, ALU.add).then_inc(m.sel_ready, 1)
    dve.wait_ge(m.rexp_ready, 2)
    link(V.tensor_reduce(pg, m.ge, AX.X, ALU.add))
    link(V.reciprocal(pg, pg))
    link(V.tensor_scalar(g1, dv, 1.0, None, ALU.add))
    link(V.reciprocal(g1, g1))
    link(V.tensor_tensor(g1, g1, pg, ALU.mult))
    link(V.tensor_tensor(g2, g1, dv, ALU.mult))
    V.memset(m.gt, 0.0)
    V.memset(m.ps, -1e6)
    V.memset(m.ye, 0.0)
    link(V.memset(m.sca, 0.0))
    link(V.tensor_tensor(cand, o1, over(g1, 32), ALU.mult))
    link(V.tensor_tensor(m.gt[:, :, 0:32], o2, over(g2, 32), ALU.mult))
    link(V.tensor_tensor(m.gt[:, :, 0:32], m.gt[:, :, 0:32], cand, ALU.add))
    dve.wait_ge(m.sel_ready, 1)
    dve.wait_ge(m.rt_ready, 2)
    link(V.tensor_scalar(cand, bank[1][:, 0:64].rearrange("p (t n) -> p t n", t=TT), 1e6 + SLOTS, None, ALU.add))
    link(V.tensor_tensor(cand, cand, sel, ALU.mult))
    link(V.tensor_scalar(m.ps[:, :, 0:32], cand, -1e6, None, ALU.add))
    V.memset(m.acc, 0.0)
    link(V.tensor_reduce(m.cmax[:, 0:1], bank[1][:, 64:96], AX.X, ALU.max))
    for i in (1, 2, 3):
        last = V.tensor_scalar(m.cmax[:, i:i + 1], m.cmax[:, 0:1], float(SLOTS * i), None, ALU.is_gt)
    link(last)
    link(V.tensor_reduce(m.cmax[:, 0:1], m.cmax[:, 1:4], AX.X, ALU.add))
    V.tensor_scalar(m.rounds[:, :], m.cmax[:, 0:1], 1.0, None, ALU.add).then_inc(m.rounds_ready, 1)
    dve.wait_ge(m.rounds_ready, 1)
    rounds = dve.value_load(m.rounds[0:1, 0:1], min_val=1, max_val=4)
    dve.sem_inc(m.sc_used, 2)
    iota = m.cst3[:, R_IOTA:R_IOTA + 64].unsqueeze(1).unsqueeze(1).to_broadcast([P, TT, 2, 64])

    def one_hot(at, value):
        wide = lambda x: x[:, :, at].unsqueeze(3).to_broadcast([P, TT, 2, 64])
        g4 = lambda x: x.rearrange("p t (e n) -> p t e n", e=2)
        V.tensor_tensor(g4(m.gm), iota, wide(m.ps), ALU.is_equal).then_inc(m.oh_ready, 1)
        dve.wait_ge(m.oh_ready, value)
        V.tensor_tensor(g4(m.gg), g4(m.gm), wide(m.gt), ALU.mult).then_inc(m.gm_ready, 1)

    def scattered(sc):
        for t in range(TT):
            for c in range(4):
                dve.wait_ge(m.sc_ready, sc.next())
                x = m.acc[:, t, c * U:(c + 1) * U]
                V.tensor_tensor(x, x, bank[6 + c % 2][:, :], ALU.add).then_inc(m.sc_used, 1)

    with dve.Fori(0, rounds) as r:
        V.tensor_scalar(m.ps[:, :, 0:32], m.ps[:, :, 0:32], -float(SLOTS), None, ALU.add).then_inc(m.ps_ready, 1)
        V.memset(m.sca, 0.0).then_inc(m.ps_ready, 1)
        dve.wait_ge(m.ps_ready, 2 * r + 2)
        one_hot(slice(0, 2), r * per_round("gm") + 1)
        with dve.Fori(0, PAIRS) as p:
            rp = r * PAIRS + p
            dve.wait_ge(m.hu_used, HU2 + rp * 12 + 2)
            one_hot(bass.ds(2 * p + 2, 2), r * per_round("gm") + 2 + p)
            dve.wait_ge(m.silu_ready, rp + 1)
            dve.wait_ge(m.hu_used, HU2 + rp * 12 + 8)
            V.tensor_tensor(m.hid, m.hs, bank[1][:, :], ALU.mult).then_inc(m.hid_ready, 1)
            scattered(Tally(r * per_round("sc") + p * 8))
        scattered(Tally(r * per_round("sc") + PAIRS * 8))
    dve.wait_ge(m.rows3_in, 32)
    for t in range(TT):
        last = V.tensor_tensor(m.acc[:, t, :], m.acc[:, t, :], m.g2, ALU.mult)
    link(last)
    for t in range(TT):
        last = V.tensor_tensor(X[:, t, :], X[:, t, :], m.acc[:, t, :], ALU.add)
    last.then_inc(m.x_final, 1)
    dve.wait_ge(m.sq_ready, sq + 2)
    V.tensor_scalar(m.rin[:, 0:2], m.ss[:, 0:2], 1.0 / D, EPS, ALU.mult, ALU.add).then_inc(m.rin_ready, 1)
    dve.wait_ge(m.rms_ready, rr + 2)
    for t in range(TT):
        V.scalar_tensor_tensor(X[:, t, :], X[:, t, :], m.rms[:, t:t + 1], m.fng, ALU.mult, ALU.mult).then_inc(m.out_ready, 1)


def moe_constants():
    i = np.arange(P)
    c = np.zeros((P, CR), np.float32)
    c[:, R_IOTA:R_IOTA + 64] = np.arange(64)
    c[:, R_I4:R_I4 + 4] = np.arange(4)
    c[:, R_I32:R_I32 + 32] = np.arange(32)
    c[:, R_UT:R_UT + P] = i[:, None] < i[None, :]
    c[:, R_ONE:R_ONE + P] = 1.0
    return {"cst3": c}


def program(nc, ctx, a, out):
    f32, i32 = mybir.dt.float32, mybir.dt.int32
    ACT = mybir.ActivationFunctionType
    AX = mybir.AxisListType

    def sb(name, shape, dt=f32):
        return ctx.enter_context(nc.sbuf_tensor(name, shape, dt))

    def sem(name):
        return ctx.enter_context(nc.semaphore(name))

    ring = sb("weight_ring", [P, RING, HALF])
    X = sb("x_res", [P, TT, D])
    HT = sb("h_t", [P, KB, S])
    PROJ = sb("proj", [P, TT, D_IN])
    Y = sb("y", [P, TT, D])
    QK = sb("qk_t", [P, 16, S])
    PB = sb("p_buf", [P, 2, TT, S])
    PT = sb("p_t", [P, TT, TT, P])
    cst = sb("cst", [P, C1])
    small_all = sb("small_all", [P, LAYERS * SMALL])
    cur = sb("small_cur", [P, SMALL])
    cosT = sb("cos_t", [P, TT, 32])
    sinT = sb("sin_t", [P, TT, 32])
    dist = sb("dist", [P, TT, S])
    distm = sb("dist_masked", [P, TT, S])
    cb = sb("c_bcast", [P, KB, 32])
    ccol = sb("c_col", [P, KB])
    ada_part = sb("ada_part", [P, U])
    ada_row = sb("ada_row", [1, U])
    ada_b = sb("ada_b_row", [1, U])
    ropeq = sb("rope_q", [P, TT, 4, 64])
    ropet = sb("rope_tmp", [P, TT, 4, 32])
    kr2 = sb("rope_k", [P, TT, 2, 64])
    posi = sb("pos_int", [P, TT], i32)
    posp = sb("pos_col", [P, TT])
    ss = sb("sum_sq", [P, 8])
    rin = sb("rms_in", [P, 8])
    rms = sb("rms_out", [P, 8])
    half = sb("minus_half", [P, 8])
    mx = sb("row_max", [P, 2, TT])
    mm = sb("row_max_scaled", [P, 2, TT])
    nm = sb("row_max_neg", [P, 2, TT])
    den = sb("row_sum", [P, 2, TT])
    es = sb("sink_exp", [P, 2, TT])
    rec = sb("row_rec", [P, 2, TT])
    lam = sb("lam", [P, 4])
    bank = [ctx.enter_context(nc.psum_tensor(f"bank{i}", [P, U], f32)) for i in range(8)]
    psS, psO, psTA, psTD = bank[4], bank[5], bank[6], bank[7]
    ident = cst[:, C_ID:C_ID + P]

    w_in = [sem(f"weights_in{i}") for i in range(RING)]
    loading = sem("first_columns_loading")
    hu_used = sem("half_unit_used")
    in_x, in_small, in_pos, half_ready, cb_ready, angles_ready, setup_a, row_b, mod_out = (
        sem(n) for n in ("x_in", "small_in", "pos_in", "half_ready", "c_bcast_ready", "angles_ready", "setup_a", "ada_b_in", "mod_out"))
    h_ready, pj_ready, pj_copied, xo = (sem(n) for n in ("h_ready", "sums_ready", "proj_copied", "x_added"))
    ta_ready, ta_copied, td_ready, td_copied = (sem(n) for n in ("ta_ready", "ta_copied", "td_ready", "td_copied"))
    s_ready, s_used, m_ready, e_ready, c_ready = (
        sem(n) for n in ("scores_ready", "scores_used", "max_ready", "exp_ready", "diff_ready"))
    o_ready, o_used, sq_ready, rin_ready, rms_ready, row_ready = (
        sem(n) for n in ("o_ready", "y_ready", "squares_ready", "rms_in_ready", "rms_ready", "ada_row_ready"))
    cn_ready, rope_ready, lam_in, lam_ready, cur_ready = (
        sem(n) for n in ("c_normed", "rope_ready", "lam_in", "lam_exp", "small_cur_ready"))
    dve_step, act_step = sem("dve_step"), sem("act_step")

    m = Parts()
    m.a, m.ring, m.X, m.HT, m.PROJ, m.Y, m.QK, m.PB, m.PT, m.dist = (
        a, ring, X, HT, PROJ, Y, QK, PB, PT, dist)
    m.distm, m.cb, m.ada_part, m.ropeq, m.ropet, m.kr2, m.ss, m.rin, m.rms, m.half = (
        distm, cb, ada_part, ropeq, ropet, kr2, ss, rin, rms, half)
    m.mx, m.mm, m.nm, m.den, m.es, m.rec, m.bank, m.ident, m.w_in, m.hu_used = (
        mx, mm, nm, den, es, rec, bank, ident, w_in, hu_used)
    m.xo, m.mod_out, m.h_ready, m.pj_copied, m.ta_ready, m.ta_copied, m.td_ready, m.td_copied, m.s_ready, m.s_used = (
        xo, mod_out, h_ready, pj_copied, ta_ready, ta_copied, td_ready, td_copied, s_ready, s_used)
    m.m_ready, m.e_ready, m.c_ready, m.o_ready, m.o_used, m.sq_ready, m.rin_ready, m.rms_ready, m.dve_step, m.half_ready = (
        m_ready, e_ready, c_ready, o_ready, o_used, sq_ready, rin_ready, rms_ready, dve_step, half_ready)
    m.beta, m.g, m.z, m.nz, m.ez, m.gsum, m.egc, m.beg = (
        sb(n, [P, TT, 8]) for n in ("beta", "g_log", "z", "minus_abs_z", "exp_z", "g_sum", "g_sum_exp", "beta_g"))
    m.gl, m.egl = (sb(n, [P, TT, 8, 2]) for n in ("g_last", "g_last_exp"))
    m.ea, m.kd, m.sm2, m.cwt = sb("exp_a", [P, 8]), sb("key_decay", [P, 8]), sb("small2", [P, 152]), sb("conv_w_t", [P, 64])
    m.rin16, m.rms16, m.half16 = (sb(n, [P, 16]) for n in ("rms_in16", "rms_out16", "minus_half16"))
    m.rounds = sb("rounds", [P, 1], i32)
    m.x_in = [sem(f"expert_weights_in{i}") for i in range(NS)]
    (m.rows2_in, m.rows3_in, m.h2_ready, m.rt_ready, m.sel_ready, m.moe_start, m.rounds_ready, m.gm_ready, m.oh_ready, m.tx_ready,
     m.tx_copied, m.sc_used, m.sc_ready, m.dn_copied, m.dn_ready, m.hid_ready, m.silu_ready, m.sca_ready, m.moe_done, m.gd_ready,
     m.rexp_ready, m.vd_ready, m.ps_ready, m.x_final, m.out_ready, m.stored) = (
        sem(n) for n in ("rows2_in", "rows3_in", "h2_ready", "router_ready", "selected", "moe_start", "rounds_ready", "one_hot_gated",
                         "one_hot", "gather_ready", "gather_copied", "scatter_added", "scatter_ready", "down_copied", "down_ready",
                         "hidden_ready", "silu_ready", "gates_moved", "moe_done", "group_diff", "router_exp", "expert_diff",
                         "places_ready", "x_final", "out_ready", "stored"))
    for_batches = lambda n: [sem(f"{n}{b}") for b in (0, 1)]
    m.b_ready, m.b_done, m.bd_ready, m.dx_ready, m.d_ready = (
        for_batches(n) for n in ("delta_ready", "delta_done", "g_columns", "decay_log", "decay_exp"))
    (m.rows_in, m.cst2_in, m.x_normed, m.r_ready, m.r_done, m.oc_done, m.gc_ready, m.gc_copied, m.egc_ready, m.state_zero,
     m.conv_ready, m.cv_ready, m.beta_ready, m.z_ready, m.ez_ready, m.g_done, m.ck_ready, m.ck_half, m.on_done) = (
        sem(n) for n in ("rows_in", "cst2_in", "x_normed", "chunk_ready", "chunk_done", "chunk_out", "g_sum_ready", "g_sum_copied",
                         "g_sum_exp_ready", "state_zero", "conv_silu", "conv_done", "beta_ready", "z_ready", "ez_ready", "g_done",
                         "ck_ready", "ck_half", "delta_normed"))

    block = ctx.enter_context(nc.Block())
    w_in_d, w_out_d = a["w_in"], a["w_out"]
    mod = m.mod = nc.dram_tensor("mod_scratch", [1, 6 * D], f32).ap()

    def half_rows(w, j):
        return w[j * 1024:(j + 1) * 1024, :].rearrange("(k p) n -> p k n", p=P)

    m.half_rows = half_rows
    second_buffers(m)
    moe_buffers(m)

    def slot(i):
        return ring[:, i % RING, :]

    uq = ring[:, 1, 0:QR_K * UQ].rearrange("p (k n) -> p k n", k=QR_K)
    ukv = [ring[:, 0, 16 * REST:16 * REST + UKV], ring[:, 1, QR_K * UQ:QR_K * UQ + UKV]]
    rest = ring[:, 0, 0:16 * REST].rearrange("p (k n) -> p k n", k=KB)
    mlaq, mlakv = PROJ[:, :, 0:UQ], PROJ[:, :, AG:AG + UKV]

    def heads(group):
        kind, g = group[0], int(group[1])
        return [(kind, g, c) for c in (0, 1)] if kind == "D" else [(kind, 2 * g + c, None) for c in (0, 1)]

    @block.sync
    def _(sp):
        sp.dma_start(X[:, :, :], a["x"][0].rearrange("(t p) d -> p t d", p=P)).then_inc(in_x, 16)
        with sp.Fori(0, LAYERS) as l:
            n = 0

            def load(dst, src, apart=False):
                sp.wait_ge(hu_used, l * PER["hu"] + n + 1)
                if n == 0:
                    sp.wait_ge(in_x, 16)
                if apart:
                    sp.sem_inc(loading, 1)
                sp.dma_start(dst, src).then_inc(w_in[n % RING], 16)

            wl = w_in_d[bass.ds(l, 1)].rearrange("a k n -> (a k) n")
            wo = w_out_d[bass.ds(l, 1)].rearrange("a k n -> (a k) n")
            for p, u in enumerate(ORDER):
                if u == 11:
                    load(rest, wl[:, 11 * U:D_IN].rearrange("(k p) n -> p k n", p=P))
                    ukv_d = a["mla_w_ukv"][bass.ds(l, 1)].rearrange("a k n -> (a k) n")
                    load(ukv[0], ukv_d[0:P, :])
                    n += 1
                    load(uq, a["mla_w_uq"][bass.ds(l, 1)].rearrange("a (k p) n -> p (a k) n", p=P))
                    load(ukv[1], ukv_d[P:2 * P, :])
                    n += 1
                else:
                    for j in (0, 1):
                        load(slot(n).rearrange("p (k n) -> p k n", k=8), half_rows(wl[:, u * U:(u + 1) * U], j),
                             apart=u + j == 0)
                        n += 1
                for j in (0, 1):
                    src = a["ada_w_2"][0, j * 1024:(j + 1) * 1024, bass.ds(l * 12 * U + p * U, U)]
                    load(slot(n).rearrange("p (k n) -> p k n", k=8), src.rearrange("(k p) n -> p k n", p=P))
                    n += 1
            for u in range(4):
                for j in (0, 1):
                    load(slot(n).rearrange("p (k n) -> p k n", k=8), half_rows(wo[:, u * U:(u + 1) * U], j))
                    n += 1
            assert n == PER["hu"]
        second_sync(m, sp)
        moe_sync(m, sp)
        for t in range(TT):
            sp.wait_ge(m.out_ready, t + 1)
            sp.dma_start(out[0, t * P:(t + 1) * P, :], X[:, t, :]).then_inc(m.stored, 16)
        sp.wait_ge(m.stored, 16 * TT)

    @block.gpsimd
    def _(pool):
        nc.gpsimd.memset(half[:, :], -0.5).then_inc(half_ready, 1)
        pool.dma_start(cst[:, :], a["cst1"]).then_inc(in_small, 16)
        pool.dma_start(posi[:, :], a["positions"].rearrange("(t p) -> p t", p=P),
                       allow_slow_non_contiguous=True).then_inc(in_pos, 16)
        pool.dma_start(PT[:, :, :, :].rearrange("p a b c -> p (a b c)").bitcast(i32)[:, 0:S],
                       a["positions"].rearrange("(a n) -> a n", a=1).partition_broadcast(P)).then_inc(in_pos, 16)
        pool.dma_start(ccol[:, :], a["c_2"][0].rearrange("(k p) -> p k", p=P),
                       allow_slow_non_contiguous=True).then_inc(in_pos, 16)
        for l in range(LAYERS):
            at = l * SMALL
            for dst, src in ((small_all[:, at + G_:at + G_ + KB], a["norm_g"][l].rearrange("(k p) -> p k", p=P)),
                             (small_all[:, at + QN_:at + QN_ + 3], a["mla_q_norm"][l].rearrange("(k p) -> p k", p=P)),
                             (small_all[:, at + QN_ + 3:at + QN_ + 5], a["mla_kv_norm"][l].rearrange("(k p) -> p k", p=P)),
                             (small_all[:, at + SK_:at + SK_ + 8], a["swa_sink"][l:l + 1, :].partition_broadcast(P)),
                             (small_all[:, at + LP_:at + LP_ + 256], a["diff_lambda"][l:l + 1].rearrange("a b c -> a (b c)").partition_broadcast(P)),
                             (small_all[:, at + SB_:at + SB_ + 128], a["diff_subln"][l:l + 1, :].partition_broadcast(P)),
                             (small_all[:, at + LC_:at + LC_ + 2], a["lam_init"][l:l + 1, :].partition_broadcast(P))):
                pool.dma_start(dst, src, allow_slow_non_contiguous=True).then_inc(in_small, 16)
        pool.wait_ge(half_ready, 1)
        with pool.Fori(0, LAYERS) as l:
            r_in = Tally(l * PER["rin"])

            def root(i, j):
                pool.wait_ge(rin_ready, r_in.next())
                nc.gpsimd.tensor_tensor(rms[:, i:j], rin[:, i:j], half[:, i:j], ALU.pow).then_inc(rms_ready, 1)

            root(0, 2)
            for p in range(12):
                for kind, arg in TASKS.get(p, ()):
                    if kind == "mla_norm":
                        root(2, 6)
                    if kind == "out" and arg[0] == "D":
                        root(6, 8)

        second_gpsimd(nc, m, pool)
        moe_gpsimd(nc, m, pool)

    @block.tensor
    def _(pe):
        pe.sem_inc(hu_used, RING)
        pe.wait_ge(in_small, 16 * 15)
        pe.wait_ge(cb_ready, 1)
        with pe.Fori(0, LAYERS) as l:
            load = [Tally(l * (15 if i < 2 else 14) * 16) for i in range(RING)]
            ta, td = Tally(l * PER["ta"], 1), Tally(l * PER["td"], 1)
            pjc, xoc = Tally(l * PER["pja"]), Tally(l * PER["xo"], 1)
            s, o, e, c = Tally(l * PER["s"], 1), Tally(l * PER["o"], 1), Tally(l * PER["e"]), Tally(l * PER["c"])
            hu = 0

            def transposes(by_act, sources):
                t, ready, copied, ps = (ta, ta_ready, ta_copied, psTA) if by_act else (td, td_ready, td_copied, psTD)
                pe.wait_ge(copied, t.now())
                for i, src in enumerate(sources):
                    last = nc.tensor.transpose(ps[:, i * P:(i + 1) * P], src, ident)
                last.then_inc(ready, 1)
                t.next()

            def copied():
                pe.wait_ge(ta_copied, ta.now())
                pe.wait_ge(td_copied, td.now())

            def proj(v, lhs, width, chunk, blocks, signal, by=1):
                for k in range(blocks):
                    for t in range(TT):
                        last = nc.tensor.matmul(bank[2 * (v % 2) + t][:, 0:width], lhs[:, k, t * P:(t + 1) * P],
                                                chunk(k), start=k == 0, stop=k == blocks - 1)
                last.then_inc(signal, by)

            def halves(v):
                nonlocal hu
                for j in (0, 1):
                    pe.wait_ge(w_in[hu % RING], load[hu % RING].next(16))
                    w = slot(hu).rearrange("p (k n) -> p k n", k=8)
                    for k in range(8):
                        for t in range(TT):
                            last = nc.tensor.matmul(bank[2 * (v % 2) + t][:, :], HT[:, 8 * j + k, t * P:(t + 1) * P],
                                                    w[:, k, :], start=j == 0 and k == 0, stop=j == 1 and k == 7)
                    last.then_inc(hu_used, 1)
                    hu += 1

            def scores(kind, h, comp):
                pe.wait_ge(s_used, s.now())
                s.next()
                copied()
                for t in range(TT):
                    out = psS[:, t * S:(t + 1) * S]
                    tok = slice(t * P, (t + 1) * P)
                    if kind == "M":
                        q = slice(64 * (h % 2), 64 * (h % 2) + 64)
                        nc.tensor.matmul(out, QK[:, 5 + h, tok], QK[:, 9 + h, :], start=True, stop=False)
                        last = nc.tensor.matmul(out, QK[q, 13 + h // 2, tok], QK[q, 15, :], start=False, stop=True)
                    elif kind == "D":
                        q = slice(64 * comp, 64 * comp + 64)
                        last = nc.tensor.matmul(out, QK[q, h, tok], QK[q, 4 + h, :], start=True, stop=True)
                    else:
                        last = nc.tensor.matmul(out, QK[:, 8 + h if h < 4 else h - 4, tok], QK[:, 12 + h // 4, :],
                                                start=True, stop=True)
                last.then_inc(s_ready, 1)

            def weighted(pb, value):
                transposes(True, [PB[:, pb, qt, kt * P:(kt + 1) * P] for kt in range(TT) for qt in range(TT)])
                pe.wait_ge(o_used, o.now())
                ob = psO
                o.next()
                pe.wait_ge(ta_copied, ta.now())
                for t in range(TT):
                    for kt in range(TT):
                        last = nc.tensor.matmul(ob[:, t * P:(t + 1) * P], PT[:, kt, t, :], value(kt),
                                                start=kt == 0, stop=kt == TT - 1)
                last.then_inc(o_ready, 1)

            def step(kind, arg):
                if kind == "mla_norm":
                    pe.wait_ge(cn_ready, l + 1)
                    cq = lambda b, t: PROJ[:, t, CQ + b * P:CQ + (b + 1) * P]
                    for b in ((0, 1), (2, 3), (4,)):
                        transposes(False, [cq(i, t) for i in b for t in range(TT)])
                elif kind == "mla_up":
                    copied()
                    for n, (lo, hi) in enumerate(((0, 512), (512, 768))):
                        if n == 0:
                            pe.wait_ge(pj_copied, pjc.base + 2)
                        else:
                            pe.wait_ge(pj_copied, pjc.base + 3)
                        proj(3 + n, QK[:, 0:3, :], hi - lo, lambda k: uq[:, k, lo:hi], QR_K, pj_ready)
                    for n in range(2):
                        pe.wait_ge(pj_copied, pjc.base + 4 + n)
                        proj(5 + n, QK[:, 3:5, :], U, lambda k: ukv[k][:, n * U:(n + 1) * U], KVR_K,
                             hu_used if n else pj_ready, 2 if n else 1)
                elif kind == "mla_rope":
                    pe.wait_ge(pj_copied, pjc.base + 8)
                    for h in (0, 2):
                        transposes(h == 0, [mlaq[:, t, (h + i) * 192:(h + i) * 192 + P] for i in (0, 1) for t in range(TT)])
                    for h in (0, 2):
                        transposes(h == 0, [mlakv[:, t, (h + i) * S:(h + i) * S + P] for i in (0, 1) for t in range(TT)])
                    pe.wait_ge(rope_ready, l + 1)
                    transposes(True, [ropeq[:, t, 2 * i:2 * i + 2, :] for i in (0, 1) for t in range(TT)])
                    transposes(False, [kr2[:, t, :, :] for t in range(TT)])
                elif kind == "prep_d":
                    for i, at in enumerate((DQ, DQ + 2 * P, DK, DK + 2 * P)):
                        transposes(i % 2 == 0, [PROJ[:, t, at + b * P:at + (b + 1) * P] for b in (0, 1) for t in range(TT)])
                elif kind == "prep_w":
                    for i, at in enumerate(((AQ, AQ + 2 * P, AK), (AQ + 4 * P, AQ + 6 * P))[arg]):
                        transposes(i % 2 == 0, [PROJ[:, t, at + b * P:at + (b + 1) * P] for b in (0, 1) for t in range(TT)])
                elif kind == "soft":
                    for h in heads(arg):
                        scores(*h)
                elif kind == "out":
                    if arg[0] == "D":
                        h = int(arg[1])
                        pe.wait_ge(c_ready, c.next())
                        weighted(0, lambda kt: PROJ[:, kt, DV + h * P:DV + (h + 1) * P])
                    else:
                        for i, (k, h, _) in enumerate(heads(arg)):
                            if i == 0:
                                pe.wait_ge(e_ready, e_of[arg] - 1)
                            else:
                                pe.wait_ge(e_ready, e_of[arg])
                            at = AG + h * S + P if k == "M" else AV + (h // 4) * P
                            weighted(i, lambda kt: PROJ[:, kt, at:at + P])

            pe.wait_ge(h_ready, l + 1)
            for j in range(8):
                transposes(j % 2 == 0, [Y[:, t, (2 * j + b) * P:(2 * j + b + 1) * P] for b in (0, 1) for t in range(TT)])
            copied()
            e_of = {}
            v = 0
            for p, u in enumerate(ORDER):
                if v >= 2:
                    pe.wait_ge(pj_copied, pjc.base + v - 1)
                if u == 11:
                    pe.wait_ge(w_in[0], load[0].next(32))
                    pe.wait_ge(w_in[1], load[1].next(32))
                    proj(v, HT, REST, lambda k: rest[:, k, :], KB, pj_ready)
                else:
                    halves(v)
                v += 1
                for kind, arg in TASKS.get(p, ()):
                    if kind == "soft":
                        e_of[arg] = e.next(2)
                    if kind in ("prep_d", "prep_w"):
                        pe.wait_ge(pj_copied, pjc.base + v)
                    step(kind, arg)
                    if kind == "mla_up":
                        v += 4
                        hu += 2
                pe.wait_ge(td_copied, td.now())
                for j in (0, 1):
                    pe.wait_ge(w_in[hu % RING], load[hu % RING].next(16))
                    w = slot(hu).rearrange("p (k n) -> p k n", k=8)
                    for k in range(8):
                        g = k % 4
                        last = nc.tensor.matmul(psTD[32 * g:32 * g + 32, :], cb[:, 8 * j + k, :], w[:, k, :],
                                                start=j == 0 and k < 4, stop=j == 1 and k >= 4)
                    last.then_inc(hu_used, 1)
                    hu += 1
                td.next()
                pe.wait_ge(td_copied, td.now())
                nc.tensor.matmul(psTD[0:1, :], cst[:, C_SEL:C_SEL + 1], ada_part[:, :], start=True, stop=True)\
                    .then_inc(td_ready, 1)
                td.next()
            for kind, arg in TASKS[12]:
                if kind == "soft":
                    e_of[arg] = e.next(2)
                step(kind, arg)
            pe.wait_ge(o_used, o.now())
            for j in range(8):
                transposes(j % 2 == 0, [Y[:, t, (2 * j + b) * P:(2 * j + b + 1) * P] for b in (0, 1) for t in range(TT)])
            copied()
            for n in range(4):
                if n >= 2:
                    pe.wait_ge(xo, xoc.base + n)
                halves(v)
                v += 1
            assert hu == PER["hu"] and ta.n - 1 == PER["ta"] and td.n - 1 == PER["td"], (hu, ta.n, td.n)
            assert s.n - 1 == PER["s"] and e.n == PER["e"] and o.n - 1 == PER["o"] and c.n == PER["c"], (s.n, e.n, o.n, c.n)

        second_tensor(nc, m, pe)
        moe_tensor(nc, m, pe)

    @block.scalar
    def _(act):
        A_ = nc.scalar.activation
        steps = 0
        act.sem_inc(ta_copied, 1)
        act.wait_ge(in_pos, 48)
        A_(ccol[:, :], ccol[:, :], ACT.Silu).then_inc(setup_a, 1)
        act.wait_ge(angles_ready, 1)
        A_(sinT[:, :, :], dist[:, 0, 0:64].rearrange("p (t n) -> p t n", t=TT), ACT.Sin).then_inc(setup_a, 1)
        A_(cosT[:, :, :], dist[:, 1, 0:64].rearrange("p (t n) -> p t n", t=TT), ACT.Sin).then_inc(setup_a, 1)
        act.wait_ge(in_x, 16)
        with act.Fori(0, LAYERS) as l:
            pj, ta = Tally(l * PER["pj"]), Tally(l * PER["ta"])
            mr, o, hu_at = Tally(l * PER["m"]), Tally(l * PER["o"]), 0
            pjc = Tally(l * PER["pja"])
            rr = Tally(l * PER["rout"])
            o_count = 0

            def copy(dst, src):
                act.wait_ge(ta_ready, ta.next())
                A_(dst, src, ACT.Copy).then_inc(ta_copied, 1)

            def evac(v, out, width, silu):
                for t in range(TT):
                    src = bank[2 * (v % 2) + t]
                    cuts = [(0, silu[0], ACT.Copy), (silu[0], silu[1], ACT.Silu), (silu[1], width, ACT.Copy)]
                    for lo, hi, f in cuts:
                        if hi > lo:
                            last = A_(out(t, lo, hi), src[:, lo:hi], f)
                last.then_inc(pj_copied, 1)
                pjc.next()

            def step(kind, arg):
                nonlocal o_count
                if kind == "mla_norm":
                    act.wait_ge(pj_copied, pjc.now())
                    for i, (at, w) in enumerate(((CQ, 384), (CKV, 256))):
                        for t in range(TT):
                            junk = PB[:, :, :, :].rearrange("p a t n -> p (a t n)")[:, t * 384:t * 384 + w] if i == 0 else \
                                (ropeq[:, 0, :, :].rearrange("p h n -> p (h n)") if t else PB[:, 1, 1, :])
                            last = A_(junk, PROJ[:, t, at:at + w], ACT.Square, accum_out=ss[:, 2 + 2 * i + t:3 + 2 * i + t])
                    last.then_inc(sq_ready, 1)
                elif kind == "mla_up":
                    for n, (lo, hi) in enumerate(((0, 512), (512, 768))):
                        act.wait_ge(pj_ready, pj.next())
                        evac(3 + n, lambda t, x, y: mlaq[:, t, lo + x:lo + y], hi - lo, (0, 0))
                    act.wait_ge(pj_ready, pj.next())
                    evac(5, lambda t, x, y: mlakv[:, t, x:y], U, (0, 0))
                    act.wait_ge(hu_used, l * PER["hu"] + RING + 10)
                    evac(6, lambda t, x, y: mlakv[:, t, U + x:U + y], U, (0, 0))
                elif kind == "mla_rope":
                    copy(QK[:, 5:7, :], psTA[:, :])
                    copy(QK[:, 9:11, :], psTA[:, :])
                    copy(QK[:, 13:15, :], psTA[:, :])
                elif kind == "prep_d":
                    copy(QK[:, 0:2, :], psTA[:, :])
                    copy(QK[:, 4:6, :], psTA[:, :])
                elif kind == "prep_w" and arg == 0:
                    copy(QK[:, 8:10, :], psTA[:, :])
                    copy(QK[:, 12:14, :], psTA[:, :])
                elif kind == "prep_w":
                    copy(QK[:, 0:2, :], psTA[:, :])
                elif kind == "soft":
                    for i, (k, h, _) in enumerate(heads(arg)):
                        act.wait_ge(m_ready, mr.next())
                        if k == "W":
                            A_(es[:, i, :], mm[:, i, :], ACT.Exp, bias=cur[:, SK_ + h:SK_ + h + 1], scale=-1.0)
                        sc = {"M": SC192, "D": SC64, "W": SC128}[k]
                        for t in range(TT):
                            last = A_(PB[:, i, t, :], PB[:, i, t, :], ACT.Exp, bias=nm[:, i, t:t + 1], scale=sc,
                                      accum_out=den[:, i, t:t + 1])
                        last.then_inc(e_ready, 1)
                elif kind == "out":
                    for _ in range(1 if arg[0] == "D" else 2):
                        copy(PT[:, :, :, :], psTA[:, :])
                        n = o.next()
                        o_count += 1
                        if arg[0] == "D":
                            act.wait_ge(o_ready, n)
                            for t in range(TT):
                                at = t * P
                                last = A_(ropeq[:, t, 0:2, :].rearrange("p h n -> p (h n)"), psO[:, at:at + P], ACT.Square,
                                          accum_out=ss[:, 6 + t:7 + t])
                            last.then_inc(sq_ready, 1)

            def load_b(p):
                act.dma_start(ada_b[:, :], a["ada_b_2"][0:1, bass.ds(l * 12 * U + p * U, U)]).then_inc(row_b, 16)

            act.wait_ge(xo, l * PER["xo"] + 1)
            load_b(0)
            for t in range(TT):
                last = A_(Y[:, t, :], X[:, t, :], ACT.Square, accum_out=ss[:, t:t + 1])
            last.then_inc(sq_ready, 1)
            act.wait_ge(lam_in, l + 1)
            A_(lam[:, 2:4], lam[:, 0:2], ACT.Exp).then_inc(lam_ready, 1)
            act.wait_ge(rms_ready, l * PER["rout"] + 1)
            for t in range(TT):
                last = A_(Y[:, t, :], X[:, t, :], ACT.Copy, scale=rms[:, t:t + 1])
            last.then_inc(h_ready, 1)
            for j in range(0, 8, 2):
                act.wait_ge(ta_ready, ta.next())
                for b in (0, 1):
                    last = A_(HT[:, 2 * j + b, :], psTA[:, b * S:(b + 1) * S], ACT.Copy, scale=cur[:, G_ + 2 * j + b:G_ + 2 * j + b + 1])
                last.then_inc(ta_copied, 1)
            v = 0
            for p, u in enumerate(ORDER):
                if u == 11:
                    act.wait_ge(pj_ready, pj.next())
                else:
                    hu_at += 2
                    act.wait_ge(hu_used, l * PER["hu"] + RING + hu_at)
                silu = {3: (0, 512), 4: (0, 512), 6: (192, 512), 7: (0, 192), 10: (192, 512), 11: (0, 192)}.get(u, (0, 0))
                evac(v, lambda t, x, y: PROJ[:, t, u * U + x:u * U + y], REST if u == 11 else U, silu)
                v += 1
                for kind, arg in TASKS.get(p, ()):
                    step(kind, arg)
                    if kind == "mla_up":
                        v += 4
                        hu_at += 2
                hu_at += 2
                act.wait_ge(row_ready, l * 12 + p + 1)
                act.dma_start(mod[0:1, bass.ds(l * 12 * U + p * U, U)], ada_row[:, :]).then_inc(mod_out, 16)
                if p < 11:
                    load_b(p + 1)
            act.wait_ge(mod_out, l * 12 * 16 + 12 * 16)
            for kind, arg in TASKS[12]:
                step(kind, arg)
            for j in range(0, 8, 2):
                copy(HT[:, 2 * j:2 * j + 2, :], psTA[:, :])
            assert ta.n == PER["ta"] and pj.n == PER["pj"] and pjc.n == PER["pja"] and mr.n == PER["m"], (ta.n, pj.n, pjc.n, mr.n)

        second_scalar(nc, m, act, ACT)
        moe_scalar(nc, m, act, ACT)

    @block.vector
    def _(dve):
        V = nc.vector
        steps = 0
        base = 0

        def link(ins):
            nonlocal steps
            steps += 1
            ins.then_inc(dve_step, 1)
            dve.wait_ge(dve_step, base + steps)

        dve.sem_inc(td_copied, 1)
        dve.sem_inc(s_used, 1)
        dve.sem_inc(o_used, 1)
        dve.sem_inc(xo, 1)
        dve.wait_ge(in_small, 16 * 15)
        dve.wait_ge(in_pos, 48)
        prow = PB[:, 0, 0, :]
        pint = PT[:, :, :, :].rearrange("p a b c -> p (a b c)").bitcast(i32)[:, 0:S]
        V.tensor_copy(prow, pint)
        link(V.tensor_copy(posp[:, :], posi[:, :]))
        ang, k_, r_, w_ = (PB[:, 1, 0, i * 64:(i + 1) * 64] for i in range(4))
        for t in range(TT):
            last = V.tensor_scalar(ang[:, t * 32:(t + 1) * 32], cst[:, C_FREQ:C_FREQ + 32], posp[:, t:t + 1], None, ALU.mult)
        link(last)
        link(V.tensor_scalar(k_, ang, 1 / (2 * math.pi), MAGIC, ALU.mult, ALU.add))
        link(V.tensor_scalar(k_, k_, -MAGIC, None, ALU.add))
        for part in (TWO_PI_A, TWO_PI_B, TWO_PI_C):
            link(V.scalar_tensor_tensor(ang, k_, -part, ang, ALU.mult, ALU.add))
        link(V.tensor_scalar(dist[:, 0, 0:64], ang, -3.1415925, 3.1415925, ALU.max, ALU.min))
        link(V.tensor_scalar(r_, ang, math.pi / 2, None, ALU.add))
        link(V.tensor_scalar(w_, r_, math.pi, -2 * math.pi, ALU.is_gt, ALU.mult))
        link(V.tensor_tensor(r_, r_, w_, ALU.add))
        dve.wait_ge(setup_a, 1)
        V.tensor_copy(cb[:, :, :], ccol[:, :].unsqueeze(2).to_broadcast([P, KB, 32])).then_inc(cb_ready, 1)
        V.tensor_scalar(dist[:, 1, 0:64], r_, -3.1415925, 3.1415925, ALU.max, ALU.min).then_inc(angles_ready, 1)
        dve.wait_ge(setup_a, 3)
        for t in range(TT):
            last = V.tensor_scalar(dist[:, t, :], prow, posp[:, t:t + 1], None, ALU.subtract)
        link(last)
        link(V.scalar_tensor_tensor(dist[:, :, :], dist[:, :, :], -1.0, dist[:, :, :], ALU.mult, ALU.max))
        link(V.tensor_scalar(distm[:, :, :], dist[:, :, :], float(P), BIG, ALU.is_gt, ALU.mult))
        link(V.tensor_tensor(distm[:, :, :], distm[:, :, :], dist[:, :, :], ALU.add))
        setup_steps = steps
        with dve.Fori(0, LAYERS) as l:
            base, steps = l * PER["dve"] + setup_steps, 0
            td, s, o, q, e = Tally(l * PER["td"]), Tally(l * PER["s"]), Tally(l * PER["o"]), Tally(l * PER["q"]), Tally(l * PER["e"])
            rr, row = Tally(l * PER["rout"]), Tally(l * 12)
            td_c, s_c, o_c = Tally(l * PER["td"], 1), Tally(l * PER["s"], 1), Tally(l * PER["o"], 1)
            pjc = Tally(l * PER["pja"])
            td_w = 0
            hu_at = 0

            def copy(dst, src):
                dve.wait_ge(td_ready, l * PER["tdr"] + tdr.next())
                V.tensor_copy(dst, src).then_inc(td_copied, 1)

            tdr = Tally(0)

            def copy_gain(pairs):
                dve.wait_ge(td_ready, l * PER["tdr"] + tdr.next())
                for dst, src, g in pairs:
                    last = V.tensor_scalar(dst, src, g, None, ALU.mult)
                last.then_inc(td_copied, 1)

            def mean(i, j, n):
                return V.tensor_scalar(rin[:, i:j], ss[:, i:j], 1.0 / n, EPS, ALU.mult, ALU.add)

            link(V.tensor_copy(cur[:, :], small_all[:, bass.ds(l * SMALL, SMALL)]))
            dve.wait_ge(sq_ready, q.next())
            mean(0, 2, D).then_inc(rin_ready, 1)
            rr.next()
            lp = cur[:, LP_:LP_ + 256].rearrange("p (a b n) -> p a b n", a=2, b=2)
            prod = ropet[:, :, :, :].rearrange("p t h n -> p (t h n)")[:, 0:P].rearrange("p (a n) -> p a n", a=2)
            link(V.tensor_tensor(prod, lp[:, :, 0, :], lp[:, :, 1, :], ALU.mult))
            V.tensor_reduce(lam[:, 0:2], prod, AX.X, ALU.add).then_inc(lam_in, 1)
            link(V.tensor_scalar(cur[:, SB_:SB_ + P], cur[:, SB_:SB_ + P], cur[:, LC_ + 1:LC_ + 2], None, ALU.mult))
            for j in range(1, 8, 2):
                copy_gain([(HT[:, 2 * j + b, :], psTD[:, b * S:(b + 1) * S], cur[:, G_ + 2 * j + b:G_ + 2 * j + b + 1]) for b in (0, 1)])
            dve.wait_ge(lam_ready, l + 1)
            link(V.tensor_tensor(lam[:, 0:1], lam[:, 3:4], lam[:, 2:3], ALU.subtract))
            link(V.tensor_tensor(lam[:, 1:2], lam[:, 0:1], cur[:, LC_:LC_ + 1], ALU.subtract))

            def rotate(dst, x1, x2, heads_):
                shape = [P, TT, heads_, 32]
                cos, sin = (x[:, :, :].unsqueeze(2).to_broadcast(shape) for x in (cosT, sinT))
                tmp = ropet[:, :, 0:heads_, :]
                for lo, f, g, op in ((0, cos, sin, ALU.subtract), (32, sin, cos, ALU.add)):
                    V.tensor_tensor(dst[:, :, :, lo:lo + 32], x1, f, ALU.mult)
                    link(V.tensor_tensor(tmp, x2, g, ALU.mult))
                    last = V.tensor_tensor(dst[:, :, :, lo:lo + 32], dst[:, :, :, lo:lo + 32], tmp, op)
                    if lo == 0:
                        link(last)
                return last

            def step(kind, arg):
                if kind == "mla_norm":
                    dve.wait_ge(sq_ready, q.next())
                    mean(2, 4, 384)
                    mean(4, 6, 256).then_inc(rin_ready, 1)
                    dve.wait_ge(rms_ready, rr.next())
                    for i, (at, w) in enumerate(((CQ, 384), (CKV, 256))):
                        for t in range(TT):
                            x = PROJ[:, t, at:at + w]
                            last = V.tensor_scalar(x, x, rms[:, 2 + 2 * i + t:3 + 2 * i + t], None, ALU.mult)
                    last.then_inc(cn_ready, 1)
                    for bs in ((0, 1), (2, 3), (4,)):
                        copy_gain([(QK[:, b, :], psTD[:, i * S:(i + 1) * S], cur[:, QN_ + b:QN_ + b + 1]) for i, b in enumerate(bs)])
                elif kind == "mla_rope":
                    dve.wait_ge(pj_copied, pjc.base + 7)
                    copy(QK[:, 7:9, :], psTD[:, :])
                    copy(QK[:, 11:13, :], psTD[:, :])
                    xq = mlaq.rearrange("p t (h n) -> p t h n", h=4)
                    link(rotate(ropeq, xq[:, :, :, 128:160], xq[:, :, :, 160:192], 4))
                    x1, x2 = (PROJ[:, :, at:at + 32].unsqueeze(2).to_broadcast([P, TT, 2, 32]) for at in (KR, KR + 32))
                    rotate(kr2, x1, x2, 2).then_inc(rope_ready, 1)
                    dve.wait_ge(td_ready, l * PER["tdr"] + tdr.next())
                    V.tensor_copy(QK[:, 15, :], psTD[:, 0:S]).then_inc(td_copied, 1)
                elif kind == "prep_d":
                    dve.wait_ge(pj_copied, pjc.base + v)
                    g = PROJ[:, :, DG:D_IN].rearrange("p t (h n) -> p t h n", h=4)
                    link(V.tensor_tensor(g, g, cur[:, SB_:SB_ + P].unsqueeze(1).unsqueeze(1).to_broadcast([P, TT, 4, P]), ALU.mult))
                    copy(QK[:, 2:4, :], psTD[:, :])
                    copy(QK[:, 6:8, :], psTD[:, :])
                elif kind == "prep_w":
                    copy(QK[:, 2:4, :] if arg else QK[:, 10:12, :], psTD[:, :])
                elif kind == "soft":
                    for i, (k, h, _) in enumerate(heads(arg)):
                        dve.wait_ge(s_ready, s.next())
                        pb, ps = PB[:, i, :, :], psS[:, :].rearrange("p (t n) -> p t n", t=TT)
                        if k == "M":
                            ins = V.tensor_copy(pb, ps)
                        elif k == "D":
                            ins = V.scalar_tensor_tensor(pb, dist[:, :, :], -SLOPES4[h] / SC64, ps, ALU.mult, ALU.add)
                        else:
                            ins = V.scalar_tensor_tensor(pb, distm[:, :, :], -SLOPES8[h] / SC128, ps, ALU.mult, ALU.add)
                        ins.then_inc(s_used, 1)
                        dve.wait_ge(s_used, s_c.next())
                        link(V.tensor_reduce(mx[:, i, :], pb, AX.X, ALU.max))
                        if k == "W":
                            link(V.tensor_scalar(mm[:, i, :], mx[:, i, :], SC128, cur[:, SK_ + h:SK_ + h + 1], ALU.mult, ALU.max))
                            last = V.tensor_scalar(nm[:, i, :], mm[:, i, :], -1.0, None, ALU.mult)
                        else:
                            last = V.tensor_scalar(nm[:, i, :], mx[:, i, :], -(SC192 if k == "M" else SC64), None, ALU.mult)
                        last.then_inc(m_ready, 1)
                elif kind == "out" and arg[0] == "D":
                    h = int(arg[1])
                    dve.wait_ge(e_ready, e.next(2))
                    link(V.reciprocal(rec[:, :, :], den[:, :, :]))
                    link(V.tensor_scalar(rec[:, 1, :], rec[:, 1, :], lam[:, 1:2], None, ALU.mult))
                    for t in range(TT):
                        last = V.tensor_scalar(PB[:, 0, t, :], PB[:, 0, t, :], rec[:, 0, t:t + 1], None, ALU.mult)
                    link(last)
                    for t in range(TT):
                        last = V.scalar_tensor_tensor(PB[:, 0, t, :], PB[:, 1, t, :], rec[:, 1, t:t + 1], PB[:, 0, t, :], ALU.mult, ALU.add)
                    last.then_inc(c_ready, 1)
                    dve.wait_ge(sq_ready, q.next())
                    mean(6, 8, P).then_inc(rin_ready, 1)
                    dve.wait_ge(rms_ready, rr.next())
                    dve.wait_ge(o_ready, o.next())
                    for t in range(TT):
                        at = t * P
                        last = V.scalar_tensor_tensor(Y[:, t, 1536 + h * P:1536 + (h + 1) * P], psO[:, at:at + P], rms[:, 6 + t:7 + t],
                                                      PROJ[:, t, DG + h * P:DG + (h + 1) * P], ALU.mult, ALU.mult)
                    last.then_inc(o_used, 1)
                elif kind == "out":
                    dve.wait_ge(pj_copied, pjc.base + v)
                    for i, (k, h, _) in enumerate(heads(arg)):
                        dve.wait_ge(e_ready, e.next())
                        if k == "W":
                            link(V.tensor_tensor(den[:, i, :], den[:, i, :], es[:, i, :], ALU.add))
                        link(V.reciprocal(rec[:, i, :], den[:, i, :]))
                        dve.wait_ge(o_ready, o.next())
                        gate, to = (BG, 1024) if k == "M" else (AG, 0)
                        for t in range(TT):
                            at = t * P
                            last = V.scalar_tensor_tensor(Y[:, t, to + h * P:to + (h + 1) * P], psO[:, at:at + P], rec[:, i, t:t + 1],
                                                          PROJ[:, t, gate + h * P:gate + (h + 1) * P], ALU.mult, ALU.mult)
                        last.then_inc(o_used, 1)

            td_c.next(4)
            v = 0
            for p, u in enumerate(ORDER):
                v += 1
                for kind, arg in TASKS.get(p, ()):
                    step(kind, arg)
                    td_c.next({"mla_norm": 3, "mla_rope": 3, "prep_d": 2, "prep_w": 1}.get(kind, 0))
                    if kind == "mla_up":
                        v += 4
                hu_at += 4
                dve.wait_ge(hu_used, l * PER["hu"] + RING + hu_at)
                V.tensor_copy(ada_part[:, :], psTD[:, :]).then_inc(td_copied, 1)
                td_c.next()
                dve.wait_ge(td_ready, l * PER["tdr"] + tdr.next())
                dve.wait_ge(row_b, l * 12 * 16 + (p + 1) * 16)
                if p > 0:
                    dve.wait_ge(mod_out, l * 12 * 16 + p * 16)
                V.tensor_tensor(ada_row[:, :], psTD[0:1, :], ada_b[:, :], ALU.add).then_inc(td_copied, 1)
                dve.wait_ge(td_copied, td_c.next())
                dve.sem_inc(row_ready, 1)
            for kind, arg in TASKS[12]:
                step(kind, arg)
            for j in range(1, 8, 2):
                copy(HT[:, 2 * j:2 * j + 2, :], psTD[:, :])
            for n in range(4):
                dve.wait_ge(hu_used, l * PER["hu"] + RING + 50 + 2 * n)
                for t in range(TT):
                    x = X[:, t, n * U:(n + 1) * U]
                    last = V.tensor_tensor(x, x, bank[2 * (v % 2) + t][:, :], ALU.add)
                last.then_inc(xo, 1)
                v += 1
            assert tdr.n == PER["tdr"] and steps == PER["dve"] and q.n == PER["q"] and rr.n == PER["rout"], (tdr.n, steps, q.n, rr.n)
        steps2 = second_vector(nc, m, dve, AX, LAYERS * PER["dve"] + setup_steps)
        moe_vector(nc, m, dve, AX, steps2)


def host_constants():
    c = np.zeros((P, C1), np.float32)
    c[:, C_ID:C_ID + P] = np.eye(P, dtype=np.float32)
    c[:, C_FREQ:C_FREQ + 32] = np.float32(10000.0) ** (-np.arange(0, 64, 2, dtype=np.float32) / np.float32(64))
    c[0:P:32, C_SEL] = 1.0
    lam = [0.8 - 0.6 * math.exp(-0.3 * l) for l in range(LAYERS)]
    return {"cst1": c, "lam_init": np.array([[x, 1.0 - x] for x in lam], np.float32), **second_constants(), **moe_constants()}


def kernel(**inputs):
    import numpy as _np
    import concourse.bacc as _bacc
    from concourse import mybir as _mybir
    from concourse.bass_utils import run_bass_kernel_spmd as _run

    nc = _bacc.Bacc("TRN2", target_bir_lowering=False, num_devices=1)
    arrays, a = {}, {}
    for name, x in {**inputs, **host_constants()}.items():
        x = _np.ascontiguousarray(x)
        arrays[f"in_{name}_dram"] = x
        a[name] = nc.dram_tensor(f"in_{name}_dram", x.shape, _mybir.dt.from_np(x.dtype), kind="ExternalInput").ap()
    out = nc.dram_tensor("out_0_dram", (1, S, D), _mybir.dt.float32, kind="ExternalOutput").ap()
    with ExitStack() as ctx:
        program(nc, ctx, a, out)
    return _run(nc, [arrays], core_ids=[0]).results[0]["out_0_dram"]
```

```python
import math
from contextlib import ExitStack

import numpy as np

import concourse.bass as bass
from concourse import mybir
from concourse.alu_op_type import AluOpType as ALU

P = 128
S = 256
TT = S // P
D = 2048
KB = D // P
LAYERS = 2
U = 512
HALF = 8 * U
RING = 4

AQ, AK, AV, AG, CQ, CKV, KR, BG, DQ, DK, DV, DG, D_IN = 0, 1024, 1280, 1536, 2560, 2944, 3200, 3264, 3776, 4288, 4800, 5312, 5824
REST = D_IN - 11 * U
QR_K, KVR_K = 3, 2
UQ, UKV = 768, 1024
EPS = 1e-6
BIG = 1e32

A2Q, A2K, A2V, BQ, BK, BV, BZ, BB, BA, C2Q, C2K, C2V, N_IN = 0, 512, 1024, 1536, 2048, 2560, 3584, 4608, 4616, 4624, 5136, 5264, 5392

ORDER = (5, 6, 11, 7, 8, 9, 10, 0, 2, 3, 1, 4)
SLOPES8 = [2.0 ** -(i + 1) for i in range(8)]
SLOPES4 = [2.0 ** -(2 * (i + 1)) for i in range(4)]
SC128, SC64, SC192 = 128 ** -0.5, 64 ** -0.5, 192 ** -0.5
MAGIC = 12582912.0
TWO_PI_A = 6.28125
TWO_PI_B = float(np.float32(2 * math.pi - 6.28125))
TWO_PI_C = 2 * math.pi - 6.28125 - TWO_PI_B

G_, QN_, SK_, LP_, SB_, LC_, SMALL = 0, 16, 21, 29, 285, 413, 415

C_ID, C_FREQ, C_SEL, C1 = 0, 128, 160, 161


class Parts:
    pass


class Tally:

    def __init__(self, base=0, first=0):
        self.base, self.n = base, first

    def next(self, by=1):
        self.n += by
        return self.base + self.n

    def now(self):
        return self.base + self.n


PER = dict(hu=56, pj=4, ta=32, td=42, tdr=30, pja=16, xo=4, s=20, m=20, e=20, c=4, o=16, q=6, rin=6, rout=6, dve=77)

TASKS = {1: [("mla_norm", 0)], 2: [("mla_up", 0)], 3: [("mla_rope", 0)], 4: [("soft", "M0")],
         5: [("out", "M0"), ("soft", "M1")], 6: [("out", "M1"), ("prep_d", 0), ("soft", "D0")],
         7: [("out", "D0"), ("soft", "D1"), ("out", "D1"), ("soft", "D2")],
         8: [("out", "D2"), ("soft", "D3"), ("out", "D3"), ("prep_w", 0), ("soft", "W0")],
         9: [("out", "W0"), ("soft", "W1")], 10: [("out", "W1"), ("prep_w", 1), ("soft", "W2")],
         11: [("out", "W2"), ("soft", "W3")], 12: [("out", "W3")]}
DIRECT = (1, 2, 11)


K_LEV, K_U, K_NEG, K_ONE = 0, 6 * P, 7 * P, 8 * P
ORDER2 = (3, 4, 5, 6, 9, 0, 1, 2, 10, 7, 8)
PIECES = 8
GAPS = [("gates", 0, 0)] + [(kind, t, n) for t in range(TT) for kind, n in
        [("expand", 0), ("gram", 0), ("first", 0)] + [(x, i) for i in range(1, 6) for x in ("x", "grow")] +
        [("apply", 0), ("qdec", 0)] + [(x, c) for c in (0, 1) for x in ("new", "state")]]
PAIRS2 = [("A", g) for g in range(4)] + [("C", g) for g in range(4)]


def levels_of(m):
    return [m.cb[:, :, :].rearrange("p k n -> p (k n)")[:, i * P:(i + 1) * P] for i in range(4)] + \
           [m.ropeq[:, :, :, :].rearrange("p t h n -> p (t h n)")[:, i * P:(i + 1) * P] for i in range(2)]


def second_buffers(m):
    rq = m.ropeq[:, :, :, :].rearrange("p t h n -> p (t h n)")
    m.level = levels_of(m)
    m.uincl, m.neg = rq[:, 2 * P:3 * P], rq[:, 3 * P:4 * P]
    m.ones = m.ropet[:, :, :, :].rearrange("p t h n -> p (t h n)")[:, 0:P]
    m.rel = {"A": m.dist[:, :, :], "C": m.distm[:, :, :]}
    m.cnt = m.ada_part[:, :].rearrange("p (t n) -> p t n", t=TT)
    h4 = lambda x: x.rearrange("p (h n) -> p h n", n=P)
    qk = m.QK[:, :, :].rearrange("p k n -> p (k n)")
    m.raw = [m.QK[:, 8 * i:8 * i + 4, :] for i in range(2)]
    m.conv = [m.QK[:, 8 * i + 4:8 * i + 8, :] for i in range(2)]
    m.u, m.wt, m.qkt, m.qd = (h4(qk[:, i * 1024:(i + 1) * 1024]) for i in range(4))
    r2, r3 = m.ring[:, 2, :], m.ring[:, 3, :]
    m.kdec, m.kq, m.state = h4(r2[:, 0:1024]), h4(r2[:, 1024:2048]), h4(r2[:, 2048:3072])
    m.lt = [h4(r2[:, 3072:3584]), h4(r2[:, 3584:4096])]
    m.mt, m.t_, m.tt, m.x_ = ([h4(r3[:, (2 * i + b) * U:(2 * i + b + 1) * U]) for b in (0, 1)] for i in range(4))
    m.dt = [h4(m.PB[:, b, :, :].rearrange("p t n -> p (t n)")) for b in (0, 1)]
    m.sq2 = m.ring[:, 2, 0:2048].rearrange("p (t n) -> p t n", t=TT)
    m.g1 = m.Y[:, 0, :]
    parts = m.PROJ_r[:, :, :].rearrange("p t n -> p (t n)")
    m.w_hi = [parts[:, i * HALF:(i + 1) * HALF].rearrange("p (k n) -> p k n", k=8) for i in (0, 1)]
    m.fn, m.gn, m.sc, m.sh = m.PROJ[:, :, D:D + 1024], m.Y[:, 0, :], m.Y[:, 1, :], m.ring[:, 2, 0:D]
    m.h = m.PROJ[:, :, 0:D]
    m.cw_rows = m.kr2[:, :, :, :].rearrange("p t h n -> p (t h n)")[0:64, 0:P]
    m.pbs = [m.PB[:, :, :, :], qk[:, 0:1024].rearrange("p (a t n) -> p a t n", a=2, t=TT)]
    m.pts = [m.PT[:, :, :, :], qk[:, 1024:1536].rearrange("p (a b c) -> p a b c", a=TT, b=TT)]
    m.stats = [(m.mx, m.mm, m.nm, m.den, m.es, m.rec),
               [qk[:, 1536 + 4 * i:1540 + 4 * i].rearrange("p (a t) -> p a t", a=2) for i in range(6)]]
    m.ck4 = m.PT[:, :, :, :].rearrange("p a b c -> p a (b c)")
    m.tmp = m.PB[:, :, :, :].rearrange("p a t n -> p (a t n)").rearrange("p (t n) -> p t n", t=TT)
    m.sqo = qk[:, 2048:3072]


def second_sync(m, sp):
    a, ring = m.a, m.ring
    load = 0
    w, wo = a["w_in_2"][0], a["w_out_2"][0]

    def half(src, width, j):
        nonlocal load
        sp.wait_ge(m.hu_used, LAYERS * PER["hu"] + RING + load - (3 if load < 2 else 1))
        sp.dma_start(ring[:, load % 2, 0:8 * width].rearrange("p (k n) -> p k n", k=8),
                     m.half_rows(src, j)).then_inc(m.w_in[load % 2], 16)
        load += 1

    sp.wait_ge(m.ta_copied, LAYERS * PER["ta"] + 1)
    sp.wait_ge(m.td_copied, LAYERS * PER["td"] + 1)
    sp.wait_ge(m.mod_out, 16 * 24)
    sp.dma_start(m.gn, a["norm1_g_2"].partition_broadcast(P)).then_inc(m.rows_in, 16)
    sp.dma_start(m.sc, m.mod[:, D:2 * D].partition_broadcast(P)).then_inc(m.rows_in, 16)
    sp.dma_start(m.fn, a["final_norm"].rearrange("(a t n) -> a t n", a=1, t=TT).partition_broadcast(P)).then_inc(m.rows_in, 16)
    for p, u in enumerate(ORDER2):
        hi = min((u + 1) * U, N_IN)
        for j in (0, 1):
            half(w[:, u * U:hi], hi - u * U, j)
        if p == 0:
            sp.wait_ge(m.hu_used, LAYERS * PER["hu"] + RING - 1)
            sp.dma_start(m.sh, m.mod[:, 0:D].partition_broadcast(P)).then_inc(m.shift_in, 16)
    used = LAYERS * PER["hu"] + RING
    for n in range(8):
        if n < 2:
            sp.wait_ge(m.hu_used, used + 20 + n + 1)
        elif n == 2:
            sp.wait_ge(m.r_done, 4 * TT)
            sp.wait_ge(m.oc_done, 2 * TT)
        elif n >= 4:
            sp.wait_ge(m.hu_used, used + 22 + n - 4 + 1)
        sp.dma_start(ring[:, n % RING, :].rearrange("p (k n) -> p k n", k=8),
                     m.half_rows(wo[:, n // 2 * U:(n // 2 + 1) * U], n % 2)).then_inc(m.w_in[n % RING], 16)
        if n == 3:
            sp.wait_ge(m.ta_copied, LAYERS * PER["ta"] + TA2 + 1)
            sp.wait_ge(m.td_copied, LAYERS * PER["td"] + TD2 + 1)
            sp.dma_start(m.g1, m.mod[:, 2 * D:3 * D].partition_broadcast(P)).then_inc(m.rows_in, 16)


def second_gpsimd(nc, m, pool):
    a = m.a
    pool.wait_ge(m.o_used, LAYERS * PER["o"] + 1)
    lev = m.cb[:, :, :].rearrange("p k n -> p (k n)")
    rq = m.ropeq[:, :, :, :].rearrange("p t h n -> p (t h n)")
    for dst, src in ((lev, a["cst2"][:, 0:4 * P]), (rq, a["cst2"][:, 4 * P:8 * P]), (m.ones, a["cst2"][:, 8 * P:9 * P]),
                     (m.dist[:, :, :].rearrange("p t n -> p (t n)"), a["rel_a"]),
                     (m.distm[:, :, :].rearrange("p t n -> p (t n)"), a["rel_c"]), (m.ada_part[:, :], a["cnt_a"]),
                     (m.cw_rows, a["dn_conv_w_2"][0].rearrange("j (b c) -> (j b) c", c=P)),
                     (m.sm2[:, 0:8], a["dn_a_log_2"].partition_broadcast(P)), (m.sm2[:, 8:16], a["dn_dt_bias_2"].partition_broadcast(P)),
                     (m.sm2[:, 16:24], a["attn_sinks_2"].partition_broadcast(P)), (m.sm2[:, 24:152], a["dn_norm_g_2"].partition_broadcast(P))):
        pool.dma_start(dst, src).then_inc(m.cst2_in, 16)
    n = LAYERS * PER["rin"]
    for _ in (0, 1):
        n += 1
        pool.wait_ge(m.rin_ready, n)
        nc.gpsimd.tensor_tensor(m.rms[:, 0:2], m.rin[:, 0:2], m.half[:, 0:2], ALU.pow).then_inc(m.rms_ready, 1)
    nc.gpsimd.memset(m.half16[:, :], -0.5).then_inc(m.half_ready, 1)
    pool.wait_ge(m.half_ready, 2)
    for _ in range(1 + TT):
        n += 1
        pool.wait_ge(m.rin_ready, n)
        nc.gpsimd.tensor_tensor(m.rms16[:, :], m.rin16[:, :], m.half16[:, :], ALU.pow).then_inc(m.rms_ready, 1)


def second_tensor(nc, m, pe):
    PROJ, HT, QK, Y, bank, ident = m.PROJ, m.HT, m.QK, m.Y, m.bank, m.ident
    mm = nc.tensor.matmul
    ta, td = Tally(LAYERS * PER["ta"], 1), Tally(LAYERS * PER["td"], 1)
    load = [Tally(LAYERS * 15 * 16) for _ in (0, 1)]
    pjc = LAYERS * PER["pja"]
    hu = 0

    def transposes(by_act, sources):
        t, ready, copied, ps = (ta, m.ta_ready, m.ta_copied, bank[6]) if by_act else (td, m.td_ready, m.td_copied, bank[7])
        pe.wait_ge(copied, t.now())
        for i, src in enumerate(sources):
            last = nc.tensor.transpose(ps[:, i * P:(i + 1) * P], src, ident)
        last.then_inc(ready, 1)
        t.next()

    def copied():
        pe.wait_ge(m.ta_copied, ta.now())
        pe.wait_ge(m.td_copied, td.now())

    def halves(v, width, gaps=()):
        nonlocal hu
        gaps = list(gaps)
        for j in (0, 1):
            pe.wait_ge(m.w_in[hu % 2], load[hu % 2].next(16))
            w = m.ring[:, hu % 2, 0:8 * width].rearrange("p (k n) -> p k n", k=8)
            for k in range(8):
                if k % 2 == 0 and gaps:
                    delta(*gaps.pop(0))
                for t in range(TT):
                    last = mm(bank[2 * (v % 2) + t][:, 0:width], HT[:, 8 * j + k, t * P:(t + 1) * P],
                              w[:, k, :], start=j == 0 and k == 0, stop=j == 1 and k == 7)
            last.then_inc(m.hu_used, 1)
            hu += 1

    stage = [0, 0]
    rec = 0

    def delta(kind, t, n):
        nonlocal rec
        if kind == "gates":
            pe.wait_ge(m.g_done, 1)
            for i in range(TT):
                last = mm(bank[4][:, i * 8:i * 8 + 8], m.uincl, m.g[:, i, :], start=True, stop=True)
            last.then_inc(m.gc_ready, 1)
            return
        if kind in ("new", "state"):
            c = slice(64 * n, 64 * n + 64)
            rec += 1
            if kind == "new":
                pe.wait_ge(m.b_done[0], stage[0])
                pe.wait_ge(m.b_done[1], stage[1])
                pe.wait_ge(m.r_done, rec - 1) if rec > 1 else pe.wait_ge(m.state_zero, 1)
                for h in range(8):
                    last = mm(bank[4 + h // 4][c, (h % 4) * P:(h % 4 + 1) * P], m.wt[:, h, c], m.state[:, h, :], start=True, stop=True)
                last.then_inc(m.r_ready, 1)
            else:
                pe.wait_ge(m.r_done, rec - 1)
                pe.wait_ge(m.oc_done, 2 * t + n) if 2 * t + n else None
                for h in range(8):
                    kt = m.kdec[c, h, :]
                    last = mm(bank[4 + h // 4][:, (h % 4) * P:(h % 4 + 1) * P], kt, m.u[c, h, :], start=True, stop=True)
                for h in range(8):
                    out = bank[6 + h // 4][c, (h % 4) * P:(h % 4 + 1) * P]
                    mm(out, m.qd[:, h, c], m.state[:, h, :], start=True, stop=False)
                    last = mm(out, m.qkt[c, h, c], m.u[c, h, :], start=False, stop=True)
                last.then_inc(m.r_ready, 1)
            return
        for b in (0, 1):
            A, B = bank[4 + 2 * b], bank[5 + 2 * b]
            s4 = lambda ps, i: ps[:, i * P:(i + 1) * P]
            pe.wait_ge(m.b_done[b], stage[b]) if stage[b] else pe.wait_ge(m.bd_ready[b], 1)
            if kind == "expand":
                if t == 0:
                    pe.wait_ge(m.gc_copied, 1)
                if t:
                    pe.wait_ge(m.r_done, rec)
                    pe.wait_ge(m.oc_done, 2 * t)
                    pe.wait_ge(m.bd_ready[b], t + 1)
                for i in (0, 1):
                    kh = 2 * b + i
                    nc.tensor.transpose(s4(A, i), PROJ[:, t, BK + kh * P:BK + (kh + 1) * P], ident)
                    nc.tensor.transpose(s4(A, 2 + i), PROJ[:, t, BQ + kh * P:BQ + (kh + 1) * P], ident)
                last = mm(B[:, :], m.ones, m.x_[b].rearrange("p h n -> p (h n)"), start=True, stop=True)
            elif kind == "gram":
                for i in (0, 1):
                    k, q = m.kq[:, 4 * b + i, :], m.kq[:, 4 * b + 2 + i, :]
                    mm(s4(A, i), k, k, start=True, stop=True)
                    mm(s4(A, 2 + i), k, q, start=True, stop=True)
                last = mm(B[:, :], m.ones, m.x_[b].rearrange("p h n -> p (h n)"), start=True, stop=True)
            elif kind == "first":
                for h in range(4):
                    last = nc.tensor.transpose(s4(A, h), m.mt[b][:, h, :], ident)
            elif kind == "x":
                for h in range(4):
                    last = mm(s4(A, h), m.mt[b][:, h, :], m.t_[b][:, h, :], start=True, stop=True)
            elif kind == "grow":
                if n < 5:
                    for h in range(4):
                        mm(s4(A, h), m.tt[b][:, h, :], m.x_[b][:, h, :], start=True, stop=True)
                for h in range(4):
                    last = mm(s4(B, h), m.x_[b][:, h, :], m.tt[b][:, h, :], start=True, stop=True)
            elif kind == "apply":
                for h in range(4):
                    mm(s4(A, h), m.tt[b][:, h, :], m.x_[b][:, h, :], start=True, stop=True)
                for h in range(4):
                    last = mm(s4(B, h), m.mt[b][:, h, :], m.tt[b][:, h, :], start=True, stop=True)
            elif kind == "qdec":
                for h in range(4):
                    last = nc.tensor.transpose(s4(A, h), m.t_[b][:, h, :], ident)
            last.then_inc(m.b_ready[b], 1)
            stage[b] += 1

    for j in range(8):
        if j % 2 == 0:
            pe.wait_ge(m.h_ready, LAYERS + 1 + j // 2)
        transposes(j % 2 == 0, [m.h[:, t, (2 * j + b) * P:(2 * j + b + 1) * P] for b in (0, 1) for t in range(TT)])
    pe.wait_ge(m.cst2_in, 16 * 11)
    pe.wait_ge(m.ta_copied, ta.now())
    nc.tensor.transpose(bank[6][:, 0:64], m.cw_rows, ident[0:64, 0:64]).then_inc(m.ta_ready, 1)
    ta.next()
    copied()
    at = 0
    for p, u in enumerate(ORDER2):
        width = min(U, N_IN - u * U)
        if p >= 2:
            pe.wait_ge(m.pj_copied, pjc + p - 1)
        gaps = GAPS[at:at + PIECES] if p >= 5 else ()
        at += len(gaps)
        if p == 5:
            copied()
        halves(p, width, gaps)
        if p < 4:
            pe.wait_ge(m.pj_copied, pjc + p + 1)
            for i in (0, 1):
                transposes(i == 0, [PROJ[:, t, BQ + p * U + (2 * i + b) * P:BQ + p * U + (2 * i + b + 1) * P] for b in (0, 1) for t in range(TT)])
        if 1 <= p <= 4:
            pe.wait_ge(m.conv_ready, p)
            src = m.conv[(p - 1) % 2]
            for t in range(TT):
                transposes(t == 0, [src[:, b, t * P:(t + 1) * P] for b in range(4)])
    for g in GAPS[at:]:
        delta(*g)
    pe.wait_ge(m.oc_done, 2 * TT)
    pe.wait_ge(m.r_done, 4 * TT)
    pe.wait_ge(m.pj_copied, pjc + len(ORDER2))
    cols = [A2Q, A2Q + 2 * P, A2K, A2K + 2 * P, C2Q, C2Q + 2 * P]
    for i, c in enumerate(cols):
        transposes(i % 2 == 0, [PROJ[:, t, c + b * P:c + (b + 1) * P] for b in (0, 1) for t in range(TT)])
    pe.wait_ge(m.ck_ready, 1)
    transposes(True, [m.ck4[:, t, i * P:(i + 1) * P] for i in (0, 1) for t in range(TT)])
    copied()
    s_n, o_n, e_n = LAYERS * PER["s"], LAYERS * PER["o"], LAYERS * PER["e"]

    def scores(kind, h):
        nonlocal s_n
        pe.wait_ge(m.s_used, s_n)
        q = slice(64 * (h % 2), 64 * (h % 2) + 64)
        qb, kb = (h // 2, 4 + h // 2) if kind == "A" else (8 + h // 2, 12 + h // 4)
        for t in range(TT):
            last = mm(bank[(4, 3)[h % 2]][:, t * S:(t + 1) * S], HT[q, qb, t * P:(t + 1) * P], HT[q, kb, :], start=True, stop=True)
        last.then_inc(m.s_ready, 1)
        s_n += 1

    def flip(kind, h, n):
        nonlocal e_n
        e_n += 1
        i = h % 2
        pe.wait_ge(m.c_ready if kind == "A" else m.e_ready, (LAYERS * PER["c"] + h + 1) if kind == "A" else e_n)
        pe.wait_ge(m.ta_copied, ta.now() - 1)
        for k, (kt, qt) in enumerate([(kt, qt) for kt in range(TT) for qt in range(TT)]):
            last = nc.tensor.transpose(bank[(6, 1)[i]][:, k * P:(k + 1) * P], m.pbs[n % 2][:, i, qt, kt * P:(kt + 1) * P], ident)
        last.then_inc(m.ta_ready, 1)
        ta.next()

    def out(kind, h):
        nonlocal o_n
        i = h % 2
        pe.wait_ge(m.o_used, o_n)
        pe.wait_ge(m.ta_copied, ta.now() - 1 + i)
        v = A2V + h * 64 if kind == "A" else C2V + (h // 4) * 64
        for t in range(TT):
            for kt in range(TT):
                last = mm(bank[(5, 2)[i]][:, t * P:t * P + 64], m.pts[i][:, kt, t, :], PROJ[:, kt, v:v + 64], start=kt == 0, stop=kt == TT - 1)
        last.then_inc(m.o_ready, 1)
        o_n += 1

    for n in range(len(PAIRS2) + 1):
        if n < len(PAIRS2):
            for i in (0, 1):
                scores(PAIRS2[n][0], 2 * PAIRS2[n][1] + i)
        if n:
            kind, g = PAIRS2[n - 1]
            for i in (0, 1):
                flip(kind, 2 * g + i, n - 1)
            for i in (0, 1):
                out(kind, 2 * g + i)
    pe.wait_ge(m.ta_copied, ta.now())
    pe.wait_ge(m.o_used, o_n + 1)
    pe.wait_ge(m.on_done, TT)
    for j in range(8):
        transposes(j % 2 == 0, [Y[:, t, (2 * j + b) * P:(2 * j + b + 1) * P] for b in (0, 1) for t in range(TT)])
    copied()
    for n in range(4):
        v = len(ORDER2) + n
        if n >= 2:
            pe.wait_ge(m.xo, 4 * LAYERS + n)
        else:
            pe.wait_ge(m.pj_copied, pjc + v - 1)
        for j in (0, 1):
            i = 2 * n + j
            hi, lo = m.w_hi[i % 2], m.ring_r[:, i % RING, :].rearrange("p (k n) -> p k n", k=8)
            pe.wait_ge(m.w_hi_ready, LAYERS * 8 + i + 1)
            for k in range(8):
                for part in (m.y_hi, m.y_lo):
                    for t in range(TT):
                        mm(bank[2 * (v % 2) + t][:, :], part[:, 8 * j + k, t * P:(t + 1) * P], hi[:, k, :],
                           start=j == 0 and k == 0 and part is m.y_hi, stop=False)
            pe.wait_ge(m.w_lo_ready, LAYERS * 8 + i + 1)
            for k in range(8):
                for t in range(TT):
                    last = mm(bank[2 * (v % 2) + t][:, :], m.y_hi[:, 8 * j + k, t * P:(t + 1) * P], lo[:, k, :],
                              start=False, stop=j == 1 and k == 7)
            last.then_inc(m.hu_used, 1)
            hu += 1


def second_scalar(nc, m, act, ACT):
    A_ = nc.scalar.activation
    PROJ, bank, X, Y = m.PROJ, m.bank, m.X, m.Y
    ta = Tally(LAYERS * PER["ta"])

    def copy(dst, src):
        act.wait_ge(m.ta_ready, ta.next())
        A_(dst, src, ACT.Copy).then_inc(m.ta_copied, 1)

    act.wait_ge(m.xo, 4 * LAYERS + 1)
    for t in range(TT):
        last = A_(m.h[:, t, :], X[:, t, :], ACT.Square, accum_out=m.ss[:, t:t + 1])
    last.then_inc(m.sq_ready, 1)
    for t in range(TT):
        act.wait_ge(m.x_normed, t + 1)
        last = A_(m.h[:, t, :], X[:, t, :], ACT.Square, accum_out=m.ss[:, t:t + 1])
    last.then_inc(m.sq_ready, 1)
    for j in range(0, 8, 2):
        copy(m.HT[:, 2 * j:2 * j + 2, :], bank[6][:, :])
    copy(m.cwt[:, :], bank[6][:, 0:64])
    e = Tally(0)
    at = 0
    b_ready = [0, 0]
    rec = 0

    def delta(kind, t, n):
        nonlocal rec
        if kind == "gates":
            act.wait_ge(m.gc_copied, 1)
            A_(m.egc[:, :, :], m.gsum[:, :, :], ACT.Exp).then_inc(m.egc_ready, 1)
        elif kind == "expand":
            for b in (0, 1):
                act.wait_ge(m.dx_ready[b], t + 1)
                A_(m.egl[:, t, 4 * b:4 * b + 4, :], m.gl[:, t, 4 * b:4 * b + 4, :], ACT.Exp)
                A_(m.dt[b], m.dt[b], ACT.Exp).then_inc(m.d_ready[b], 1)
        elif kind == "new":
            rec += 1
        elif kind == "state":
            rec += 1
            c = slice(64 * n, 64 * n + 64)
            act.wait_ge(m.r_ready, rec)
            for i in (0, 1):
                last = A_(Y[c, t, U + i * U:U + (i + 1) * U], bank[6 + i][c, :], ACT.Copy)
            last.then_inc(m.oc_done, 1)

    for p, u in enumerate(ORDER2):
        width = min(U, N_IN - u * U)
        gaps = GAPS[at:at + PIECES] if p >= 5 else ()
        at += len(gaps)
        for g in gaps:
            delta(*g)
        act.wait_ge(m.hu_used, LAYERS * PER["hu"] + RING + 2 * (p + 1))
        for t in range(TT):
            last = A_(PROJ[:, t, u * U:u * U + width], bank[2 * (p % 2) + t][:, 0:width], ACT.Silu if u in (7, 8) else ACT.Copy)
        last.then_inc(m.pj_copied, 1)
        if p < 4:
            copy(m.raw[p % 2][:, 0:2, :], bank[6][:, :])
        if p >= 1 and p <= 4:
            act.wait_ge(m.cv_ready, p)
            A_(m.conv[(p - 1) % 2], m.conv[(p - 1) % 2], ACT.Silu).then_inc(m.conv_ready, 1)
            copy(PROJ[:, 0, BQ + (p - 1) * U:BQ + p * U], bank[6][:, :])
        if p == 4:
            act.wait_ge(m.pj_copied, LAYERS * PER["pja"] + 5)
            A_(m.beta[:, :, :], PROJ[:, :, BB:BB + 8], ACT.Sigmoid).then_inc(m.beta_ready, 1)
            act.wait_ge(m.z_ready, 1)
            A_(m.ea[:, :], m.sm2[:, 0:8], ACT.Exp)
            A_(m.ez[:, :, :], m.nz[:, :, :], ACT.Exp).then_inc(m.ez_ready, 1)
            act.wait_ge(m.ez_ready, 1)
            A_(m.ez[:, :, :], m.ez[:, :, :], ACT.Ln, bias=1.0).then_inc(m.ez_ready, 1)
    for g in GAPS[at:]:
        delta(*g)
    HT = m.HT
    for dst in (HT[:, 0:2, :], HT[:, 4:6, :], HT[:, 8:10, :], HT[:, 12:14, :]):
        copy(dst, bank[6][:, :])
    m_n, e_n = LAYERS * PER["m"], 0
    for n in range(len(PAIRS2) + 1):
        if n:
            for i in (0, 1):
                copy(m.pts[i], bank[(6, 1)[i]][:, :])
        if n < len(PAIRS2):
            kind, g = PAIRS2[n]
            _, mm_, nm, den, es, _ = m.stats[n % 2]
            for i in (0, 1):
                h = 2 * g + i
                m_n += 1
                act.wait_ge(m.m_ready, m_n)
                if kind == "C":
                    A_(es[:, i, :], mm_[:, i, :], ACT.Exp, bias=m.sm2[:, 16 + h:17 + h], scale=-1.0)
                for t in range(TT):
                    kw = {} if kind == "A" else {"accum_out": den[:, i, t:t + 1]}
                    x = m.pbs[n % 2][:, i, t, :]
                    last = A_(x, x, ACT.Exp, bias=nm[:, i, t:t + 1], scale=SC64, **kw)
                last.then_inc(m.e_ready, 1)

    def round_weights(n, ks=slice(0, 8)):
        return A_(m.w_hi[n % 2][:, ks, :], m.ring[:, n % RING, :].rearrange("p (k n) -> p k n", k=8)[:, ks, :], ACT.Copy)

    def arrived(n):
        act.wait_ge(m.w_in[n % RING], (LAYERS * 15 + 11 if n % RING < 2 else LAYERS * 14) * 16 + (n // RING + 1) * 16)

    act.wait_ge(m.o_used, LAYERS * PER["o"] + 16 + 1)
    act.wait_ge(m.on_done, TT)
    arrived(0)
    for j in range(0, 8, 2):
        act.wait_ge(m.ta_ready, ta.next())
        A_(m.y_hi[:, 2 * j:2 * j + 2, :], bank[6][:, :], ACT.Copy).then_inc(m.y_hi_ready, 1)
        last = round_weights(0, slice(j, j + 2))
    last.then_inc(m.w_hi_ready, 1)
    for n in range(1, 8):
        arrived(n)
        if n >= 2:
            act.wait_ge(m.hu_used, LAYERS * PER["hu"] + RING + 22 + n - 1)
        round_weights(n).then_inc(m.w_hi_ready, 1)


def second_vector(nc, m, dve, AX, steps0):
    V = nc.vector
    PROJ, bank, X, Y, HT = m.PROJ, m.bank, m.X, m.Y, m.HT
    steps = steps0
    td = Tally(LAYERS * PER["tdr"])

    def link(ins):
        nonlocal steps
        steps += 1
        ins.then_inc(m.dve_step, 1)
        dve.wait_ge(m.dve_step, steps)

    def copy(dst, src):
        dve.wait_ge(m.td_ready, td.next())
        V.tensor_copy(dst, src).then_inc(m.td_copied, 1)

    sq, rr = LAYERS * PER["q"], LAYERS * PER["rout"]

    dve.wait_ge(m.rows_in, 16 * 3)
    link(V.scalar_tensor_tensor(m.sc, m.sc, 1.0, m.gn, ALU.add, ALU.mult))
    dve.wait_ge(m.sq_ready, sq + 1)
    V.tensor_scalar(m.rin[:, 0:2], m.ss[:, 0:2], 1.0 / D, EPS, ALU.mult, ALU.add).then_inc(m.rin_ready, 1)
    dve.wait_ge(m.rms_ready, rr + 1)
    for t in range(TT):
        x = X[:, t, :].rearrange("p (a n) -> p a n", a=TT)
        V.scalar_tensor_tensor(x, x, m.rms[:, t:t + 1], m.fn, ALU.mult, ALU.mult).then_inc(m.x_normed, 1)
    dve.wait_ge(m.sq_ready, sq + 2)
    V.tensor_scalar(m.rin[:, 0:2], m.ss[:, 0:2], 1.0 / D, EPS, ALU.mult, ALU.add).then_inc(m.rin_ready, 1)
    dve.wait_ge(m.rms_ready, rr + 2)
    dve.wait_ge(m.shift_in, 16)
    for q in range(4):
        c = slice(q * U, (q + 1) * U)
        for t in range(TT):
            last = V.scalar_tensor_tensor(m.h[:, t, c], X[:, t, c], m.rms[:, t:t + 1], m.sc[:, c], ALU.mult, ALU.mult)
        link(last)
        V.tensor_tensor(m.h[:, :, c], m.h[:, :, c], m.sh[:, c].unsqueeze(1).to_broadcast([P, TT, U]), ALU.add).then_inc(m.h_ready, 1)
    for j in range(1, 8, 2):
        copy(HT[:, 2 * j:2 * j + 2, :], bank[7][:, :])
    dve.wait_ge(m.ta_copied, LAYERS * PER["ta"] + 1 + 5)
    dve.wait_ge(m.cst2_in, 16 * 11)

    stage = [0, 0]
    rec = 0
    bc_i = lambda x: x.unsqueeze(2).to_broadcast([P, 4, P])
    bc_h = lambda x: x.unsqueeze(1).to_broadcast([P, 4, P])
    flat = lambda x: x.rearrange("p h n -> p (h n)")
    v4 = lambda ps: ps[:, :].rearrange("p (h n) -> p h n", n=P)

    def columns(t, b):
        return V.tensor_tensor(m.x_[b], bc_h(m.uincl), bc_i(m.g[:, t, 4 * b:4 * b + 4]), ALU.mult)

    def delta(kind, t, n):
        nonlocal rec
        if kind == "gates":
            V.memset(flat(m.state), 0.0).then_inc(m.state_zero, 1)
            for b in (0, 1):
                columns(0, b).then_inc(m.bd_ready[b], 1)
            dve.wait_ge(m.gc_ready, 1)
            V.tensor_copy(m.gsum[:, :, :], bank[4][:, 0:16].rearrange("p (t h) -> p t h", t=TT)).then_inc(m.gc_copied, 1)
            dve.wait_ge(m.gc_copied, 1)
            dve.wait_ge(m.egc_ready, 1)
            link(V.tensor_tensor(m.beg[:, :, :], m.beta[:, :, :], m.egc[:, :, :], ALU.mult))
            return
        if kind in ("new", "state"):
            c = slice(64 * n, 64 * n + 64)
            rec += 1
            dve.wait_ge(m.r_ready, rec)
            if kind == "new":
                for b in (0, 1):
                    x = m.u[c, 4 * b:4 * b + 4, :]
                    last = V.tensor_tensor(x, x, bank[4 + b][c, :].rearrange("p (h n) -> p h n", n=P), ALU.subtract)
                last.then_inc(m.r_done, 1)
            else:
                for b in (0, 1):
                    x = m.state[:, 4 * b:4 * b + 4, :]
                    last = V.tensor_tensor(x, x, m.egl[:, t, 4 * b:4 * b + 4, n:n + 1].to_broadcast([P, 4, P]), ALU.mult)
                link(last)
                for b in (0, 1):
                    x = m.state[:, 4 * b:4 * b + 4, :]
                    last = V.tensor_tensor(x, x, v4(bank[4 + b]), ALU.add)
                last.then_inc(m.r_done, 1)
                if n == 1 and t == 0:
                    for b in (0, 1):
                        columns(1, b).then_inc(m.bd_ready[b], 1)
            return
        for b in (0, 1):
            A, B = bank[4 + 2 * b], bank[5 + 2 * b]
            hs = slice(4 * b, 4 * b + 4)
            stage[b] += 1
            dve.wait_ge(m.b_ready[b], stage[b])
            mask = lambda i: V.tensor_tensor(m.mt[b], m.lt[b], bc_h(m.level[i]), ALU.mult)
            if kind == "expand":
                V.tensor_copy(flat(m.kq[:, hs, :]), A[:, :])
                V.tensor_tensor(m.dt[b], v4(B), bc_i(m.gsum[:, t, hs]), ALU.subtract)
                link(V.tensor_copy(m.gl[:, t, hs, :], v4(B)[:, :, 63::64]))
                V.tensor_tensor(m.dt[b], m.dt[b], bc_h(m.neg), ALU.add).then_inc(m.dx_ready[b], 1)
                V.tensor_tensor(m.x_[b], bc_h(m.ident), bc_i(m.beta[:, t, hs]), ALU.mult)
                dve.wait_ge(m.d_ready[b], t + 1)
                kd = m.kd[:, hs]
                V.tensor_copy(kd[0:64, :], m.dt[b][0:64, :, 63])
                link(V.tensor_copy(kd[64:P, :], m.dt[b][64:P, :, 127]))
                k2 = PROJ[:, t, BK + 2 * b * P:BK + (2 * b + 2) * P].rearrange("p (h n) -> p h n", n=P)
                k4 = k2.unsqueeze(2).to_broadcast([P, 2, 2, P])
                V.tensor_tensor(m.kdec[:, hs, :].rearrange("p (h r) n -> p h r n", r=2), k4,
                                kd.rearrange("p (h r) -> p h r", r=2).unsqueeze(3).to_broadcast([P, 2, 2, P]), ALU.mult)\
                    .then_inc(m.b_done[b], 1)
            elif kind == "gram":
                link(V.tensor_tensor(m.lt[b], m.dt[b], v4(B), ALU.mult))
                r4 = lambda x: x.rearrange("p (h r) n -> p h r n", r=2)
                g4 = lambda i: v4(A)[:, 2 * i:2 * i + 2, :].unsqueeze(2).to_broadcast([P, 2, 2, P])
                link(V.tensor_tensor(r4(m.lt[b]), r4(m.lt[b]), g4(0), ALU.mult))
                V.tensor_tensor(r4(m.qkt[:, hs, :]), r4(m.dt[b]), g4(1), ALU.mult)
                link(mask(0))
                V.tensor_tensor(m.tt[b], bc_h(m.ident), m.mt[b], ALU.subtract).then_inc(m.b_done[b], 1)
            elif kind == "first":
                V.tensor_tensor(m.t_[b], bc_h(m.ident), v4(A), ALU.subtract)
                mask(1).then_inc(m.b_done[b], 1)
            elif kind == "x":
                V.tensor_copy(flat(m.x_[b]), A[:, :]).then_inc(m.b_done[b], 1)
            elif kind == "grow":
                if n < 5:
                    V.tensor_tensor(m.t_[b], m.t_[b], v4(A), ALU.subtract)
                    V.tensor_tensor(m.tt[b], m.tt[b], v4(B), ALU.subtract)
                    mask(n + 1).then_inc(m.b_done[b], 1)
                else:
                    V.tensor_tensor(m.tt[b], m.tt[b], v4(B), ALU.subtract)
                    V.tensor_tensor(m.x_[b], PROJ[:, t, BV + 4 * b * P:BV + (4 * b + 4) * P].rearrange("p (h n) -> p h n", n=P),
                                    bc_i(m.beta[:, t, hs]), ALU.mult)
                    r4 = lambda x: x.rearrange("p (h r) n -> p h r n", r=2)
                    for dst, src, s in ((m.mt[b], BK, m.beg), (m.t_[b], BQ, m.egc)):
                        x = PROJ[:, t, src + 2 * b * P:src + (2 * b + 2) * P].rearrange("p (h n) -> p h n", n=P)
                        last = V.tensor_tensor(r4(dst), x.unsqueeze(2).to_broadcast([P, 2, 2, P]),
                                               s[:, t, hs].rearrange("p (h r) -> p h r", r=2).unsqueeze(3).to_broadcast([P, 2, 2, P]), ALU.mult)
                    last.then_inc(m.b_done[b], 1)
            elif kind == "apply":
                V.tensor_copy(flat(m.u[:, hs, :]), A[:, :])
                V.tensor_copy(flat(m.wt[:, hs, :]), B[:, :]).then_inc(m.b_done[b], 1)
            elif kind == "qdec":
                V.tensor_copy(flat(m.qd[:, hs, :]), A[:, :]).then_inc(m.b_done[b], 1)

    at = 0
    for p, u in enumerate(ORDER2):
        gaps = GAPS[at:at + PIECES] if p >= 5 else ()
        at += len(gaps)
        for g in gaps:
            delta(*g)
        if p < 4:
            copy(m.raw[p % 2][:, 2:4, :], bank[7][:, :])
            dve.wait_ge(m.td_copied, LAYERS * PER["td"] + td.n + 1)
            dve.wait_ge(m.ta_copied, LAYERS * PER["ta"] + 1 + 5 + max(1, 2 * p))
            raw, out = m.raw[p % 2], m.conv[p % 2]
            for j in (3, 2, 1, 0):
                for b in range(4):
                    w = m.cwt[:, 16 * j + 4 * p + b:16 * j + 4 * p + b + 1]
                    d = 3 - j
                    if d == 0:
                        last = V.tensor_scalar(out[:, b, :], raw[:, b, :], w, None, ALU.mult)
                    else:
                        last = V.scalar_tensor_tensor(out[:, b, d:S], raw[:, b, 0:S - d], w, out[:, b, d:S], ALU.mult, ALU.add)
                if j:
                    link(last)
            last.then_inc(m.cv_ready, 1)
        if 1 <= p <= 4:
            copy(PROJ[:, 1, BQ + (p - 1) * U:BQ + p * U], bank[7][:, :])
        if p == 4:
            dve.wait_ge(m.beta_ready, 1)
            link(V.tensor_tensor(m.z[:, :, :], PROJ[:, :, BA:BA + 8], m.sm2[:, 8:16].unsqueeze(1).to_broadcast([P, TT, 8]), ALU.add))
            V.scalar_tensor_tensor(m.nz[:, :, :], m.z[:, :, :], -1.0, m.z[:, :, :], ALU.mult, ALU.min).then_inc(m.z_ready, 1)
            dve.wait_ge(m.ez_ready, 2)
            link(V.scalar_tensor_tensor(m.g[:, :, :], m.z[:, :, :], 0.0, m.ez[:, :, :], ALU.max, ALU.add))
            V.scalar_tensor_tensor(m.g[:, :, :], m.g[:, :, :], -1.0, m.ea[:, :].unsqueeze(1).to_broadcast([P, TT, 8]),
                                   ALU.mult, ALU.mult).then_inc(m.g_done, 1)
            dve.wait_ge(m.g_done, 1)
            dve.wait_ge(m.ta_copied, LAYERS * PER["ta"] + 1 + 5 + 8)
            dve.wait_ge(m.td_copied, LAYERS * PER["td"] + td.n + 1)
            qk = PROJ[:, :, BQ:BV].rearrange("p t (h n) -> p t h n", n=P)
            sq_ = m.sq2.rearrange("p t (h n) -> p t h n", n=P)
            link(V.tensor_tensor(sq_, qk, qk, ALU.mult))
            r16 = m.rin16[:, :].rearrange("p (t h) -> p t h", t=TT)
            link(V.tensor_reduce(r16, sq_, AX.X, ALU.add))
            V.tensor_scalar(m.rin16[:, :], m.rin16[:, :], EPS, None, ALU.add).then_inc(m.rin_ready, 1)
            dve.wait_ge(m.rms_ready, rr + 3)
            o16 = m.rms16[:, :].rearrange("p (t h) -> p t h", t=TT)
            link(V.tensor_scalar(o16[:, :, 0:4], o16[:, :, 0:4], SC128, None, ALU.mult))
            link(V.tensor_tensor(qk, qk, o16.unsqueeze(3).to_broadcast([P, TT, 8, P]), ALU.mult))
    for g in GAPS[at:]:
        delta(*g)
    dve.wait_ge(m.pj_copied, LAYERS * PER["pja"] + len(ORDER2))
    for t in range(TT):
        V.tensor_copy(m.ck4[:, t, :].rearrange("p (k r n) -> p k r n", k=2, r=2),
                      PROJ[:, t, C2K:C2K + P].rearrange("p (k n) -> p k n", k=2).unsqueeze(2).to_broadcast([P, 2, 2, 64]))\
            .then_inc(m.ck_half, 1)
    dve.wait_ge(m.ck_half, 2)
    dve.sem_inc(m.ck_ready, 1)
    for dst in (HT[:, 2:4, :], HT[:, 6:8, :], HT[:, 10:12, :]):
        copy(dst, bank[7][:, :])
    s_n, o_n = LAYERS * PER["s"], LAYERS * PER["o"]
    e_n = LAYERS * PER["e"]

    def normed(t):
        nonlocal rr
        o = Y[:, t, U:U + 1024].rearrange("p (h n) -> p h n", n=P)
        z = PROJ[:, t, BZ:BZ + 1024].rearrange("p (h n) -> p h n", n=P)
        sq_ = m.sqo.rearrange("p (h n) -> p h n", n=P)
        link(V.tensor_tensor(sq_, o, o, ALU.mult))
        link(V.tensor_reduce(m.rin16[:, 0:8], sq_, AX.X, ALU.add))
        V.tensor_scalar(m.rin16[:, 0:8], m.rin16[:, 0:8], 1.0 / P, EPS, ALU.mult, ALU.add).then_inc(m.rin_ready, 1)
        link(V.tensor_tensor(z, z, m.sm2[:, 24:152].unsqueeze(1).to_broadcast([P, 8, P]), ALU.mult))
        dve.wait_ge(m.rms_ready, LAYERS * PER["rout"] + 4 + t)
        link(V.tensor_tensor(o, o, m.rms16[:, 0:8].unsqueeze(2).to_broadcast([P, 8, P]), ALU.mult))
        V.tensor_tensor(o, o, z, ALU.mult).then_inc(m.on_done, 1)

    dve.wait_ge(m.oc_done, 2 * TT)

    def soft(n):
        nonlocal s_n
        kind, g = PAIRS2[n]
        mx, mm_, nm, _, _, _ = m.stats[n % 2]
        for i in (0, 1):
            h = 2 * g + i
            s_n += 1
            dve.wait_ge(m.s_ready, s_n)
            pb, ps = m.pbs[n % 2][:, i, :, :], bank[(4, 3)[i]][:, :].rearrange("p (t n) -> p t n", t=TT)
            V.scalar_tensor_tensor(pb, m.rel[kind], -SLOPES8[h] / SC64, ps, ALU.mult, ALU.add).then_inc(m.s_used, 1)
            dve.wait_ge(m.s_used, s_n + 1)
            link(V.tensor_reduce(mx[:, i, :], pb, AX.X, ALU.max))
            if kind == "C":
                link(V.tensor_scalar(mm_[:, i, :], mx[:, i, :], SC64, m.sm2[:, 16 + h:17 + h], ALU.mult, ALU.max))
                last = V.tensor_scalar(nm[:, i, :], mm_[:, i, :], -1.0, None, ALU.mult)
            else:
                last = V.tensor_scalar(nm[:, i, :], mx[:, i, :], -SC64, None, ALU.mult)
            last.then_inc(m.m_ready, 1)

    for n in range(len(PAIRS2) + 1):
        if n:
            kind, g = PAIRS2[n - 1]
            _, _, _, den, es, rec_ = m.stats[(n - 1) % 2]
        for i in (0, 1) if n else ():
            h = 2 * g + i
            e_n += 1
            dve.wait_ge(m.e_ready, e_n)
            if kind == "A":
                pb = m.pbs[(n - 1) % 2][:, i, :, :]
                for t in range(TT):
                    last = V.scalar_tensor_tensor(pb[:, t, :], pb[:, t, :], 1.0, m.cnt[:, t, :], ALU.mult, ALU.mult,
                                                  accum_out=den[:, i, t:t + 1])
                last.then_inc(m.c_ready, 1)
                dve.wait_ge(m.c_ready, LAYERS * PER["c"] + h + 1)
            else:
                link(V.tensor_tensor(den[:, i, :], den[:, i, :], es[:, i, :], ALU.add))
            link(V.reciprocal(rec_[:, i, :], den[:, i, :]))
        if n < len(PAIRS2):
            soft(n)
        if n in (1, 3):
            normed(n // 2)
        if n == 0:
            continue
        for i in (0, 1):
            o_n += 1
            dve.wait_ge(m.o_ready, o_n)
            to = (0 if kind == "A" else 1536) + (2 * g + i) * 64
            for t in range(TT):
                last = V.tensor_scalar(Y[:, t, to:to + 64], bank[(5, 2)[i]][:, t * P:t * P + 64], rec_[:, i, t:t + 1], None, ALU.mult)
            last.then_inc(m.o_used, 1)

    def remainders(n):
        dve.wait_ge(m.w_hi_ready, LAYERS * 8 + n + 1)
        lo, w = (x[:, n % RING, :].rearrange("p (k n) -> p k n", k=8) for x in (m.ring_r, m.ring))
        V.tensor_tensor(lo, w, m.w_hi[n % 2].bitcast(m.f32), ALU.subtract).then_inc(m.w_lo_ready, 1)

    for j in range(8):
        dst = slice(2 * j, 2 * j + 2)
        if j % 2 == 0:
            dve.wait_ge(m.y_hi_ready, LAYERS * 4 + j // 2 + 1)
        else:
            dve.wait_ge(m.td_ready, td.next())
            link(V.tensor_copy(m.y_hi[:, dst, :], bank[7][:, :]))
        V.tensor_tensor(m.y_lo[:, dst, :], bank[6 + j % 2][:, :].rearrange("p (a n) -> p a n", a=2),
                        m.y_hi[:, dst, :].bitcast(m.f32), ALU.subtract).then_inc(m.td_copied if j % 2 else m.ta_copied, 1)
    for n in range(4):
        remainders(n)
    dve.wait_ge(m.rows_in, 16 * 4)
    for n in range(4):
        v = len(ORDER2) + n
        dve.wait_ge(m.hu_used, LAYERS * PER["hu"] + RING + 2 * (v + 1))
        for t in range(TT):
            last = V.tensor_tensor(m.tmp[:, t, :], bank[2 * (v % 2) + t][:, :], m.g1[:, n * U:(n + 1) * U], ALU.mult)
        link(last)
        for t in range(TT):
            x = X[:, t, n * U:(n + 1) * U]
            last = V.tensor_tensor(x, x, m.tmp[:, t, :], ALU.add)
        last.then_inc(m.xo, 1)
        dve.wait_ge(m.xo, 4 * LAYERS + 2 + n)
        if n < 2:
            remainders(4 + 2 * n)
            remainders(5 + 2 * n)
    return steps


def second_constants():
    i = np.arange(P)
    same = (i[:, None] // 64) == (i[None, :] // 64)
    c = np.zeros((P, 9 * P), np.float32)
    for l in range(6):
        s = 1 << l
        r, k = i[None, :] // s, i[:, None] // s
        c[:, l * P:(l + 1) * P] = (r % 2 == 1) & (k == r - 1)
    u = (i[:, None] <= i[None, :]) & same
    c[:, K_U:K_U + P] = u
    c[:, K_NEG:K_NEG + P] = np.where(u, 0.0, -1e30)
    c[:, K_ONE:K_ONE + P] = 1.0
    q, k = np.arange(S)[:, None], np.arange(S)[None, :]
    d = q - k
    cnt = ((d >= 0) & (d <= 128)).astype(np.float32) + ((d >= 0) & (d % 4 == 0)) + ((d >= 0) & (d % 16 == 0))
    rel_a = np.where(cnt > 0, d, BIG)
    rel_c = np.where((d >= 0) & (d <= 127), d, BIG)
    tile = lambda x: np.ascontiguousarray(x.reshape(TT, P, S).transpose(1, 0, 2).reshape(P, TT * S)).astype(np.float32)
    return {"cst2": c, "rel_a": tile(rel_a), "rel_c": tile(rel_c), "cnt_a": tile(cnt)}


EXPERTS, GROUPS, EPG, FF = 32, 4, 8, 512
SLOTS = 64
PAIRS = EXPERTS // 2
NS = 6
XR = EXPERTS + 2
TA2, TD2 = 37, 19
HU2 = LAYERS * PER["hu"] + RING + 30
PERP = dict(hu=12, tx=6, dn=4, dnr=2, sc=8, hid=1, gm=1, silu=1)
PREP = dict(tx=5, gm=1)
R_IOTA, R_I4, R_I32, R_UT, R_ONE, CR = 0, 64, 68, 100, 228, 356


def per_round(name):
    return PREP.get(name, 0) + PAIRS * PERP[name] + (8 if name == "sc" else 0)


def moe_buffers(m):
    flat = m.PROJ[:, :, :].rearrange("p t n -> p (t n)")
    m.slots = [m.ring[:, i, :] for i in range(4)] + [flat[:, 0:HALF], flat[:, HALF:2 * HALF]]
    qk = m.QK[:, :, :].rearrange("p k n -> p (k n)")
    m.gn2, m.junk2 = m.Y[:, 1, :], (qk[:, 0:D], m.Y[:, 0, :])
    m.sc2, m.sh2 = qk[:, D:2 * D], flat[:, 2 * HALF:2 * HALF + D]
    at = 2 * HALF + D
    m.rw = flat[:, at:at + 576].rearrange("p (k n) -> p k n", k=KB)
    m.rb = flat[:, at + 576:at + 612]
    m.cst3 = flat[:, at + 612:at + 612 + CR]
    m.xg = m.QK[:, 0:8, :].rearrange("p k n -> p (k n)").rearrange("p (k n) -> p k n", n=P)
    m.ye = qk[:, D:2 * D]
    m.acc = m.HT[:, :, :].rearrange("p k n -> p (k n)").rearrange("p (t n) -> p t n", t=TT)
    m.hid = m.dist[:, :, :].rearrange("p t n -> p (t n)")
    m.hs = m.distm[:, :, :].rearrange("p t n -> p (t n)")
    m.hidt = m.PT[:, :, :, :].rearrange("p a b c -> p (a b) c")
    pb = m.PB[:, :, :, :].rearrange("p a t n -> p (a t n)")
    m.gm, m.gg = (pb[:, i * S:(i + 1) * S].rearrange("p (t n) -> p t n", t=TT) for i in (0, 1))
    m.sca, m.scb = pb[:, 2 * S:3 * S], pb[:, 3 * S:4 * S]
    m.g2, m.fng = m.sh2, m.ring[:, 0, 0:D]
    rq = m.ropeq[:, :, :, :].rearrange("p t h n -> p (t h n)")
    cbf = m.cb[:, :, :].rearrange("p k n -> p (k n)")
    tile = lambda x, n: x[:, 0:TT * n].rearrange("p (t n) -> p t n", t=TT)
    m.lg = tile(rq[:, 0:72], 36)
    m.em, m.cand, m.o1, m.o2, m.sel = (tile(rq[:, 80 + 64 * i:144 + 64 * i], 32) for i in range(5))
    m.ps, m.gt = tile(cbf[:, 0:68], XR), tile(cbf[:, 72:140], XR)
    m.ge, m.og = tile(cbf[:, 144:152], 4), tile(cbf[:, 152:160], 4)
    m.v = [cbf[:, 160 + 2 * i:162 + 2 * i] for i in range(10)]
    m.cmax = cbf[:, 180:184]
    m.yacc = m.tmp


def moe_sync(m, sp):
    a = m.a
    sp.wait_ge(m.o_used, LAYERS * PER["o"] + 16 + 1)
    sp.wait_ge(m.on_done, TT)
    for dst, src in ((m.gn2, a["norm2_g_2"]), (m.sh2, m.mod[:, 3 * D:4 * D]),
                     (m.rb[:, 0:4], a["router_group_b_2"]), (m.rb[:, 4:36], a["router_expert_b_2"])):
        sp.dma_start(dst, src.partition_broadcast(P)).then_inc(m.rows2_in, 16)
    sp.dma_start(m.rw[:, :, 0:4], a["router_group_w_2"][0].rearrange("(k p) n -> p k n", p=P)).then_inc(m.rows2_in, 16)
    sp.dma_start(m.rw[:, :, 4:36], a["router_expert_w_2"][0].rearrange("(k p) n -> p k n", p=P)).then_inc(m.rows2_in, 16)
    sp.dma_start(m.cst3, a["cst3"]).then_inc(m.rows2_in, 16)

    def pair_loads(p):
        expert = lambda w, e: w[0, bass.ds(2 * p + e, 1)].rearrange("a k n -> (a k) n")
        for w in ("expert_w_gate_2", "expert_w_up_2"):
            for j in (0, 1):
                for e in (0, 1):
                    yield expert(a[w], e)[j * 1024:(j + 1) * 1024, :], 8
        for j in (0, 1):
            for e in (0, 1):
                yield expert(a["expert_w_down_2"], e)[:, j * 1024:(j + 1) * 1024], 4

    def load(n, src, k):
        sp.dma_start(m.slots[n % NS].rearrange("p (k n) -> p k n", k=k),
                     src.rearrange("(k p) n -> p k n", p=P)).then_inc(m.x_in[n % NS], 16)

    for n, (src, k) in enumerate(pair_loads(0)):
        if n == NS:
            sp.wait_ge(m.h2_ready, 4)
            sp.dma_start(m.g2, m.mod[:, 5 * D:6 * D].partition_broadcast(P)).then_inc(m.g2_in, 16)
            sp.wait_ge(m.rounds_ready, 1)
            rounds = sp.value_load(m.rounds[0:1, 0:1], min_val=1, max_val=4)
        if n < 4:
            sp.wait_ge(m.hu_used, HU2 - 4 + n + 1)
        if n == 3:
            sp.dma_start(m.sc2, m.mod[:, 4 * D:5 * D].partition_broadcast(P)).then_inc(m.rows2_in, 16)
        if n >= NS:
            sp.wait_ge(m.hu_used, HU2 + n - NS + 1)
        load(n, src, k)
    with sp.Fori(1, rounds * PAIRS) as pp:
        for n, (src, k) in enumerate(pair_loads(pp % PAIRS)):
            sp.wait_ge(m.hu_used, HU2 + pp * 12 + n - NS + 1)
            load(n, src, k)
    sp.wait_ge(m.moe_done, 1)
    sp.dma_start(m.fng, a["final_norm_g_2"].rearrange("(a n) -> a n", a=1).partition_broadcast(P)).then_inc(m.rows3_in, 16)


def moe_gpsimd(nc, m, pool):
    def root(n, lo, hi):
        pool.wait_ge(m.rin_ready, LAYERS * PER["rin"] + 5 + n)
        nc.gpsimd.tensor_tensor(m.rms[:, lo:hi], m.rin[:, lo:hi], m.half[:, lo:hi], ALU.pow).then_inc(m.rms_ready, 1)

    root(1, 0, 2)
    pool.wait_ge(m.rt_ready, 1)
    nc.gpsimd.memset(m.acc, 0.0).then_inc(m.zeroed, 1)
    nc.gpsimd.memset(m.ye, 0.0).then_inc(m.zeroed, 1)
    for t in range(TT):
        root(2 + t, t, t + 1)


def moe_tensor(nc, m, pe):
    mm = nc.tensor.matmul
    bank, H = m.bank, m.Y
    ta, td = Tally(LAYERS * PER["ta"] + TA2, 1), Tally(LAYERS * PER["td"] + TD2, 1)

    def route(j):
        for k in (2 * j, 2 * j + 1):
            for t in range(TT):
                last = mm(bank[t][:, 0:36], m.HT[:, k, t * P:(t + 1) * P], m.rw[:, k, :], start=k == 0, stop=k == KB - 1)
        return last

    for j in range(8):
        if j % 2 == 0:
            pe.wait_ge(m.h2_ready, 1 + j // 2)
        t, ready, cop, ps = (ta, m.ta_ready, m.ta_copied, bank[6]) if j % 2 == 0 else (td, m.td_ready, m.td_copied, bank[7])
        pe.wait_ge(cop, t.now())
        for i, (b, tt) in enumerate([(b, tt) for b in (0, 1) for tt in range(TT)]):
            last = nc.tensor.transpose(ps[:, i * P:(i + 1) * P], H[:, tt, (2 * j + b) * P:(2 * j + b + 1) * P], m.ident)
        last.then_inc(ready, 1)
        t.next()
        if j == 2:
            pe.wait_ge(m.rows2_in, 16 * 8)
        if j >= 2:
            route(j - 2)
    pe.wait_ge(m.ta_copied, ta.now())
    pe.wait_ge(m.td_copied, td.now())
    route(6)
    route(7).then_inc(m.rt_ready, 1)
    ut, one = m.cst3[:, R_UT:R_UT + P], m.cst3[:, R_ONE:R_ONE + P]
    pe.wait_ge(m.sel_ready, 1)
    mm(bank[2][:, 0:32], ut, m.sel[:, 0, :], start=True, stop=True)
    mm(bank[2][:, 32:64], ut, m.sel[:, 1, :], start=True, stop=False)
    mm(bank[2][:, 32:64], one, m.sel[:, 0, :], start=False, stop=True)
    mm(bank[2][:, 64:96], one, m.sel[:, 0, :], start=True, stop=False)
    mm(bank[2][:, 64:96], one, m.sel[:, 1, :], start=False, stop=True).then_inc(m.rt_ready, 1)
    pe.sem_inc(m.moe_start, 1)
    pe.wait_ge(m.rounds_ready, 1)
    rounds = pe.value_load(m.rounds[0:1, 0:1], min_val=1, max_val=4)
    pe.wait_ge(m.zeroed, 2)

    def gather(tx, gm):
        pe.wait_ge(m.gm_ready, gm)
        for q in range(4):
            pe.wait_ge(m.tx_copied, tx.now())
            ps = bank[2 + (tx.n - 1) % 2]
            for i in range(4):
                k = 4 * q + i
                for t in range(TT):
                    last = mm(ps[:, i * P:(i + 1) * P], H[:, t, k * P:(k + 1) * P], m.gm[:, t, :], start=t == 0, stop=t == TT - 1)
            last.then_inc(m.tx_ready, 1)
            tx.next()
        pe.wait_ge(m.tx_copied, tx.now())
        ps = bank[2 + (tx.n - 1) % 2]
        for t in range(TT):
            last = nc.tensor.transpose(ps[:, t * P:(t + 1) * P], m.gg[:, t, :], m.ident)
        last.then_inc(m.tx_ready, 1)
        tx.next()

    def scatter(sc):
        for t in range(TT):
            for c in range(4):
                pe.wait_ge(m.sc_used, sc.now())
                mm(bank[6 + c % 2][:, :], m.sca[:, t * P:(t + 1) * P], m.ye[:, c * U:(c + 1) * U], start=True, stop=True)\
                    .then_inc(m.sc_ready, 1)
                sc.next()

    with pe.Fori(0, rounds) as r:
        tx = Tally(r * per_round("tx"), 1)
        gather(tx, r * per_round("gm") + 1)
        with pe.Fori(0, PAIRS) as p:
            rp = r * PAIRS + p
            tx = Tally(r * per_round("tx") + PREP["tx"] + p * PERP["tx"], 1)
            load = [Tally(rp * 32) for _ in range(NS)]
            hu = 0

            def weights(n, k):
                return m.slots[n % NS].rearrange("p (k n) -> p k n", k=k)

            def arrived(n):
                pe.wait_ge(m.x_in[n % NS], load[n % NS].next(16))

            pe.wait_ge(m.tx_copied, tx.now() + 1)
            for side in (0, 1):
                for j in (0, 1):
                    arrived(hu)
                    arrived(hu + 1)
                    for k in range(8):
                        for e in (0, 1):
                            s = slice(64 * e, 64 * e + 64)
                            last = mm(bank[side][s, :], m.xg[:, 8 * j + k, s], weights(hu + e, 8)[:, k, :],
                                      start=j == 0 and k == 0, stop=j == 1 and k == 7)
                            if k == 7:
                                last.then_inc(m.hu_used, 1)
                    hu += 2
            pe.wait_ge(m.dn_copied, rp * 4 + 2)
            scatter(Tally(r * per_round("sc") + p * 8, 1))
            gather(tx, r * per_round("gm") + 2 + p)
            pe.wait_ge(m.hid_ready, rp + 1)
            pe.wait_ge(m.tx_copied, tx.now())
            ps = bank[2 + (tx.n - 1) % 2]
            for f in range(4):
                last = nc.tensor.transpose(ps[:, f * P:(f + 1) * P], m.hid[:, f * P:(f + 1) * P], m.ident)
            last.then_inc(m.tx_ready, 1)
            tx.next()
            pe.wait_ge(m.tx_copied, tx.now() + 1)
            for j in (0, 1):
                arrived(hu)
                arrived(hu + 1)
                for c in (0, 1):
                    n = 2 * j + c
                    pe.wait_ge(m.dn_copied, rp * 4 + n + 1)
                    for f in range(4):
                        for e in (0, 1):
                            s = slice(64 * e, 64 * e + 64)
                            last = mm(bank[4 + n % 2][s, :], m.hidt[:, f, s], weights(hu + e, 4)[:, f, c * U:(c + 1) * U],
                                      start=f == 0, stop=f == 3)
                            if f == 3 and c == 1:
                                last.then_inc(m.hu_used, 1)
                    if c == 0:
                        last.then_inc(m.dn_ready, 1)
                hu += 2
        pe.wait_ge(m.dn_copied, (r + 1) * (PAIRS * 4) + 2)
        scatter(Tally(r * per_round("sc") + PAIRS * 8, 1))
        pe.wait_ge(m.sc_used, (r + 1) * per_round("sc") + 2)
    pe.sem_inc(m.moe_done, 1)


def moe_scalar(nc, m, act, ACT):
    A_ = nc.scalar.activation
    X, Y, bank = m.X, m.Y, m.bank
    act.wait_ge(m.xo, 4 * LAYERS + 1 + 4)
    for t in range(TT):
        last = A_(m.junk2[t], X[:, t, :], ACT.Square, accum_out=m.ss[:, t:t + 1])
    last.then_inc(m.sq_ready, 1)
    for i, j in enumerate(range(0, 8, 2)):
        act.wait_ge(m.ta_ready, LAYERS * PER["ta"] + TA2 + i + 1)
        A_(m.HT[:, 2 * j:2 * j + 2, :], bank[6][:, :], ACT.Copy).then_inc(m.ta_copied, 1)
    act.wait_ge(m.gd_ready, 1)
    A_(m.ge[:, :, :], m.ge[:, :, :], ACT.Exp).then_inc(m.rexp_ready, 1)
    act.wait_ge(m.vd_ready, 1)
    A_(m.v[3], m.v[3], ACT.Exp).then_inc(m.rexp_ready, 1)
    act.wait_ge(m.rounds_ready, 1)
    rounds = act.value_load(m.rounds[0:1, 0:1], min_val=1, max_val=4)
    act.sem_inc(m.tx_copied, 2)
    act.sem_inc(m.dn_copied, 2)

    def gathered(tx, keep):
        for q in range(4):
            act.wait_ge(m.tx_ready, tx.next())
            if q == 0 and keep:
                A_(m.sca, m.scb, ACT.Copy).then_inc(m.sca_ready, 1)
            A_(m.xg[:, 4 * q:4 * q + 4, :], bank[2 + (tx.n - 1) % 2][:, :], ACT.Copy).then_inc(m.tx_copied, 1)
        act.wait_ge(m.tx_ready, tx.next())
        A_(m.scb, bank[2 + (tx.n - 1) % 2][:, 0:S], ACT.Copy).then_inc(m.tx_copied, 1)

    with act.Fori(0, rounds) as r:
        gathered(Tally(r * per_round("tx")), False)
        with act.Fori(0, PAIRS) as p:
            rp = r * PAIRS + p
            tx = Tally(r * per_round("tx") + PREP["tx"] + p * PERP["tx"])
            act.wait_ge(m.hu_used, HU2 + rp * 12 + 4)
            A_(m.hs, bank[0][:, :], ACT.Silu).then_inc(m.silu_ready, 1)
            act.wait_ge(m.tx_copied, tx.now() + 2)
            gathered(tx, True)
            act.wait_ge(m.tx_ready, tx.next())
            A_(m.hidt[:, :, :], bank[2 + (tx.n - 1) % 2][:, :], ACT.Copy).then_inc(m.tx_copied, 1)
            for n in range(4):
                if n % 2 == 0:
                    act.wait_ge(m.dn_ready, rp * 2 + n // 2 + 1)
                else:
                    act.wait_ge(m.hu_used, HU2 + rp * 12 + 8 + 2 * (n // 2 + 1))
                A_(m.ye[:, n * U:(n + 1) * U], bank[4 + n % 2][:, :], ACT.Copy).then_inc(m.dn_copied, 1)
    for t in range(TT):
        act.wait_ge(m.x_final, t + 1)
        A_(Y[:, t, :], X[:, t, :], ACT.Square, accum_out=m.ss[:, t:t + 1]).then_inc(m.sq_ready, 1)


def moe_vector(nc, m, dve, AX, steps0):
    V = nc.vector
    X, Y, bank = m.X, m.Y, m.bank
    steps = steps0

    def link(ins):
        nonlocal steps
        steps += 1
        ins.then_inc(m.dve_step, 1)
        dve.wait_ge(m.dve_step, steps)

    sq, rr = LAYERS * PER["q"] + 2, LAYERS * PER["rout"] + 5
    dve.wait_ge(m.sq_ready, sq + 1)
    V.tensor_scalar(m.rin[:, 0:2], m.ss[:, 0:2], 1.0 / D, EPS, ALU.mult, ALU.add).then_inc(m.rin_ready, 1)
    dve.wait_ge(m.rows2_in, 16 * 8)
    link(V.scalar_tensor_tensor(m.sc2, m.sc2, 1.0, m.gn2, ALU.add, ALU.mult))
    dve.wait_ge(m.rms_ready, rr + 1)
    for q in range(4):
        c = slice(q * U, (q + 1) * U)
        for t in range(TT):
            last = V.scalar_tensor_tensor(Y[:, t, c], X[:, t, c], m.rms[:, t:t + 1], m.sc2[:, c], ALU.mult, ALU.mult)
        link(last)
        V.tensor_tensor(Y[:, :, c], Y[:, :, c], m.sh2[:, c].unsqueeze(1).to_broadcast([P, TT, U]), ALU.add).then_inc(m.h2_ready, 1)
    for i, j in enumerate(range(1, 8, 2)):
        dve.wait_ge(m.td_ready, LAYERS * PER["tdr"] + TD2 + i + 1)
        V.tensor_copy(m.HT[:, 2 * j:2 * j + 2, :], bank[7][:, :]).then_inc(m.td_copied, 1)

    lg, em, cand, o1, o2, sel = m.lg, m.em, m.cand, m.o1, m.o2, m.sel
    gmax, gi, pg, dv, v1, i1, v2, i2, g1, g2 = m.v
    over = lambda x, n: x.unsqueeze(2).to_broadcast([P, TT, n])
    both = lambda at, n: m.cst3[:, at:at + n].unsqueeze(1).to_broadcast([P, TT, n])
    i4, i32 = both(R_I4, 4), both(R_I32, 32)
    dve.wait_ge(m.rt_ready, 1)
    for t in range(TT):
        last = V.tensor_tensor(lg[:, t, :], bank[t][:, 0:36], m.rb, ALU.add)
    link(last)
    gl = lg[:, :, 0:4]

    def first_max(x, n, iota, top, index, onehot, tmp):
        link(V.tensor_reduce(top, x, AX.X, ALU.max))
        link(V.tensor_tensor(tmp, x, over(top, n), ALU.is_equal))
        link(V.scalar_tensor_tensor(tmp, tmp, -1000.0, iota, ALU.mult, ALU.add))
        link(V.tensor_reduce(index, tmp, AX.X, ALU.min))
        link(V.tensor_scalar(index, index, 1000.0, None, ALU.add))
        link(V.tensor_tensor(onehot, iota, over(index, n), ALU.is_equal))

    first_max(gl, 4, i4, gmax, gi, m.og, cand[:, :, 0:4])
    V.tensor_tensor(m.ge, gl, over(gmax, 4), ALU.subtract).then_inc(m.gd_ready, 1)
    link(V.tensor_scalar(m.og, m.og, 1e30, -1e30, ALU.mult, ALU.add))
    link(V.tensor_tensor(em.rearrange("p t (g n) -> p t g n", g=GROUPS), lg[:, :, 4:36].rearrange("p t (g n) -> p t g n", g=GROUPS),
                         m.og.unsqueeze(3).to_broadcast([P, TT, GROUPS, EPG]), ALU.add))
    first_max(em, 32, i32, v1, i1, o1, cand)
    link(V.scalar_tensor_tensor(em, o1, -1e32, em, ALU.mult, ALU.add))
    first_max(em, 32, i32, v2, i2, o2, cand)
    V.tensor_tensor(dv, v2, v1, ALU.subtract).then_inc(m.vd_ready, 1)
    V.tensor_tensor(sel, o1, o2, ALU.add).then_inc(m.sel_ready, 1)
    dve.wait_ge(m.rexp_ready, 2)
    link(V.tensor_reduce(pg, m.ge, AX.X, ALU.add))
    link(V.reciprocal(pg, pg))
    link(V.tensor_scalar(g1, dv, 1.0, None, ALU.add))
    link(V.reciprocal(g1, g1))
    link(V.tensor_tensor(g1, g1, pg, ALU.mult))
    link(V.tensor_tensor(g2, g1, dv, ALU.mult))
    V.memset(m.gt, 0.0)
    link(V.memset(m.ps, -1e6))
    link(V.tensor_tensor(cand, o1, over(g1, 32), ALU.mult))
    link(V.tensor_tensor(m.gt[:, :, 0:32], o2, over(g2, 32), ALU.mult))
    link(V.tensor_tensor(m.gt[:, :, 0:32], m.gt[:, :, 0:32], cand, ALU.add))
    dve.wait_ge(m.sel_ready, 1)
    dve.wait_ge(m.rt_ready, 2)
    link(V.tensor_scalar(cand, bank[2][:, 0:64].rearrange("p (t n) -> p t n", t=TT), 1e6 + SLOTS, None, ALU.add))
    link(V.tensor_tensor(cand, cand, sel, ALU.mult))
    link(V.tensor_scalar(m.ps[:, :, 0:32], cand, -1e6, None, ALU.add))
    link(V.tensor_reduce(m.cmax[:, 0:1], bank[2][:, 64:96], AX.X, ALU.max))
    for i in (1, 2, 3):
        last = V.tensor_scalar(m.cmax[:, i:i + 1], m.cmax[:, 0:1], float(SLOTS * i), None, ALU.is_gt)
    link(last)
    link(V.tensor_reduce(m.cmax[:, 0:1], m.cmax[:, 1:4], AX.X, ALU.add))
    V.tensor_scalar(m.rounds[:, :], m.cmax[:, 0:1], 1.0, None, ALU.add).then_inc(m.rounds_ready, 1)
    dve.wait_ge(m.rounds_ready, 1)
    rounds = dve.value_load(m.rounds[0:1, 0:1], min_val=1, max_val=4)
    dve.wait_ge(m.zeroed, 2)
    dve.sem_inc(m.sc_used, 2)
    iota = m.cst3[:, R_IOTA:R_IOTA + 64].unsqueeze(1).unsqueeze(1).to_broadcast([P, TT, 2, 64])

    def one_hot(at, value):
        wide = lambda x: x[:, :, at].unsqueeze(3).to_broadcast([P, TT, 2, 64])
        g4 = lambda x: x.rearrange("p t (e n) -> p t e n", e=2)
        V.tensor_tensor(g4(m.gm), iota, wide(m.ps), ALU.is_equal).then_inc(m.oh_ready, 1)
        dve.wait_ge(m.oh_ready, value)
        V.tensor_tensor(g4(m.gg), g4(m.gm), wide(m.gt), ALU.mult).then_inc(m.gm_ready, 1)

    def scattered(sc):
        for t in range(TT):
            for c in range(4):
                dve.wait_ge(m.sc_ready, sc.next())
                x = m.acc[:, t, c * U:(c + 1) * U]
                V.tensor_tensor(x, x, bank[6 + c % 2][:, :], ALU.add).then_inc(m.sc_used, 1)

    with dve.Fori(0, rounds) as r:
        V.tensor_scalar(m.ps[:, :, 0:32], m.ps[:, :, 0:32], -float(SLOTS), None, ALU.add).then_inc(m.ps_ready, 1)
        V.memset(m.sca, 0.0).then_inc(m.ps_ready, 1)
        dve.wait_ge(m.ps_ready, 2 * r + 2)
        one_hot(slice(0, 2), r * per_round("gm") + 1)
        with dve.Fori(0, PAIRS) as p:
            rp = r * PAIRS + p
            dve.wait_ge(m.hu_used, HU2 + rp * 12 + 2)
            one_hot(bass.ds(2 * p + 2, 2), r * per_round("gm") + 2 + p)
            dve.wait_ge(m.silu_ready, rp + 1)
            dve.wait_ge(m.hu_used, HU2 + rp * 12 + 8)
            V.tensor_tensor(m.hid, m.hs, bank[1][:, :], ALU.mult).then_inc(m.hid_ready, 1)
            scattered(Tally(r * per_round("sc") + p * 8))
        scattered(Tally(r * per_round("sc") + PAIRS * 8))
    dve.wait_ge(m.g2_in, 16)
    for t in range(TT):
        link(V.tensor_tensor(m.acc[:, t, :], m.acc[:, t, :], m.g2, ALU.mult))
        V.tensor_tensor(X[:, t, :], X[:, t, :], m.acc[:, t, :], ALU.add).then_inc(m.x_final, 1)
    for t in range(TT):
        dve.wait_ge(m.sq_ready, sq + 2 + t)
        V.tensor_scalar(m.rin[:, t:t + 1], m.ss[:, t:t + 1], 1.0 / D, EPS, ALU.mult, ALU.add).then_inc(m.rin_ready, 1)
    dve.wait_ge(m.rows3_in, 16)
    for t in range(TT):
        dve.wait_ge(m.rms_ready, rr + 2 + t)
        V.scalar_tensor_tensor(X[:, t, :], X[:, t, :], m.rms[:, t:t + 1], m.fng, ALU.mult, ALU.mult).then_inc(m.out_ready, 1)


def moe_constants():
    i = np.arange(P)
    c = np.zeros((P, CR), np.float32)
    c[:, R_IOTA:R_IOTA + 64] = np.arange(64)
    c[:, R_I4:R_I4 + 4] = np.arange(4)
    c[:, R_I32:R_I32 + 32] = np.arange(32)
    c[:, R_UT:R_UT + P] = i[:, None] < i[None, :]
    c[:, R_ONE:R_ONE + P] = 1.0
    return {"cst3": c}


def program(nc, ctx, a, out):
    f32, i32 = mybir.dt.float32, mybir.dt.int32
    ACT = mybir.ActivationFunctionType
    AX = mybir.AxisListType

    def sb(name, shape, dt=f32):
        return ctx.enter_context(nc.sbuf_tensor(name, shape, dt))

    def sem(name):
        return ctx.enter_context(nc.semaphore(name))

    def both(name, shape):
        with nc.sbuf_tensor(name, shape, f32) as whole:
            pass
        return whole, sb(name + "_parts", shape, mybir.dt.float32r)

    ring, ring_r = both("weight_ring", [P, RING, HALF])
    X = sb("x_res", [P, TT, D])
    HT, HT_r = both("h_t", [P, KB, S])
    PROJ, PROJ_r = both("proj", [P, TT, D_IN])
    Y = sb("y", [P, TT, D])
    QK, QK_r = both("qk_t", [P, 16, S])
    PB = sb("p_buf", [P, 2, TT, S])
    PT = sb("p_t", [P, TT, TT, P])
    cst = sb("cst", [P, C1])
    small_all = sb("small_all", [P, LAYERS * SMALL])
    cur = sb("small_cur", [P, SMALL])
    cosT = sb("cos_t", [P, TT, 32])
    sinT = sb("sin_t", [P, TT, 32])
    dist = sb("dist", [P, TT, S])
    distm = sb("dist_masked", [P, TT, S])
    cb = sb("c_bcast", [P, KB, 32])
    ccol = sb("c_col", [P, KB])
    ada_part = sb("ada_part", [P, U])
    ada_row = sb("ada_row", [1, U])
    ada_b = sb("ada_b_row", [1, U])
    ropeq = sb("rope_q", [P, TT, 4, 64])
    ropet = sb("rope_tmp", [P, TT, 4, 32])
    kr2 = sb("rope_k", [P, TT, 2, 64])
    posi = sb("pos_int", [P, TT], i32)
    posp = sb("pos_col", [P, TT])
    ss = sb("sum_sq", [P, 8])
    rin = sb("rms_in", [P, 8])
    rms = sb("rms_out", [P, 8])
    half = sb("minus_half", [P, 8])
    mx = sb("row_max", [P, 2, TT])
    mm = sb("row_max_scaled", [P, 2, TT])
    nm = sb("row_max_neg", [P, 2, TT])
    den = sb("row_sum", [P, 2, TT])
    es = sb("sink_exp", [P, 2, TT])
    rec = sb("row_rec", [P, 2, TT])
    lam = sb("lam", [P, 4])
    bank = [ctx.enter_context(nc.psum_tensor(f"bank{i}", [P, U], f32)) for i in range(8)]
    psS, psO, psTA, psTD = bank[4], bank[5], bank[6], bank[7]
    ident = cst[:, C_ID:C_ID + P]
    y_hi, y_lo = HT_r, QK_r
    w_at = (D_IN - 4 * U, 0)
    w_hi = [PROJ_r[:, :, at:at + 4 * U].rearrange("p t (k n) -> p t k n", k=4) for at in w_at]

    w_in = [sem(f"weights_in{i}") for i in range(RING)]
    loading = sem("first_columns_loading")
    w_hi_ready, w_lo_ready, y_hi_ready = (sem(n) for n in ("weights_rounded", "weights_remainder", "y_rounded"))
    hu_used = sem("half_unit_used")
    in_small1 = sem("small_in_layer1")
    in_x, in_small, in_pos, half_ready, cb_ready, angles_ready, setup_a, row_b, mod_out = (
        sem(n) for n in ("x_in", "small_in", "pos_in", "half_ready", "c_bcast_ready", "angles_ready", "setup_a", "ada_b_in", "mod_out"))
    h_ready, pj_ready, pj_copied, xo = (sem(n) for n in ("h_ready", "sums_ready", "proj_copied", "x_added"))
    ta_ready, ta_copied, td_ready, td_copied = (sem(n) for n in ("ta_ready", "ta_copied", "td_ready", "td_copied"))
    s_ready, s_used, m_ready, e_ready, c_ready = (
        sem(n) for n in ("scores_ready", "scores_used", "max_ready", "exp_ready", "diff_ready"))
    o_ready, o_used, sq_ready, rin_ready, rms_ready, row_ready = (
        sem(n) for n in ("o_ready", "y_ready", "squares_ready", "rms_in_ready", "rms_ready", "ada_row_ready"))
    cn_ready, rope_ready, lam_in, lam_ready, cur_ready = (
        sem(n) for n in ("c_normed", "rope_ready", "lam_in", "lam_exp", "small_cur_ready"))
    dve_step, act_step = sem("dve_step"), sem("act_step")

    m = Parts()
    m.a, m.ring, m.PROJ_r, m.ring_r, m.y_hi, m.y_lo, m.w_hi_ready, m.w_lo_ready, m.y_hi_ready, m.f32 = (
        a, ring, PROJ_r, ring_r, y_hi, y_lo, w_hi_ready, w_lo_ready, y_hi_ready, f32)
    m.X, m.HT, m.PROJ, m.Y, m.QK, m.PB, m.PT, m.dist, m.distm, m.cb = (
        X, HT, PROJ, Y, QK, PB, PT, dist, distm, cb)
    m.ada_part, m.ropeq, m.ropet, m.kr2, m.ss, m.rin, m.rms, m.half, m.mx, m.mm = (
        ada_part, ropeq, ropet, kr2, ss, rin, rms, half, mx, mm)
    m.nm, m.den, m.es, m.rec, m.bank, m.ident, m.w_in, m.hu_used, m.xo, m.mod_out = (
        nm, den, es, rec, bank, ident, w_in, hu_used, xo, mod_out)
    m.h_ready, m.pj_copied, m.ta_ready, m.ta_copied, m.td_ready, m.td_copied, m.s_ready, m.s_used, m.m_ready, m.e_ready = (
        h_ready, pj_copied, ta_ready, ta_copied, td_ready, td_copied, s_ready, s_used, m_ready, e_ready)
    m.c_ready, m.o_ready, m.o_used, m.sq_ready, m.rin_ready, m.rms_ready, m.dve_step, m.half_ready = (
        c_ready, o_ready, o_used, sq_ready, rin_ready, rms_ready, dve_step, half_ready)
    m.beta, m.g, m.z, m.nz, m.ez, m.gsum, m.egc, m.beg = (
        sb(n, [P, TT, 8]) for n in ("beta", "g_log", "z", "minus_abs_z", "exp_z", "g_sum", "g_sum_exp", "beta_g"))
    m.gl, m.egl = (sb(n, [P, TT, 8, 2]) for n in ("g_last", "g_last_exp"))
    m.ea, m.kd, m.sm2, m.cwt = sb("exp_a", [P, 8]), sb("key_decay", [P, 8]), sb("small2", [P, 152]), sb("conv_w_t", [P, 64])
    m.rin16, m.rms16, m.half16 = (sb(n, [P, 16]) for n in ("rms_in16", "rms_out16", "minus_half16"))
    m.shift_in = sem("shift_in")
    m.g2_in, m.zeroed = sem("g2_in"), sem("moe_zeroed")
    m.rounds = sb("rounds", [P, 1], i32)
    m.x_in = [sem(f"expert_weights_in{i}") for i in range(NS)]
    (m.rows2_in, m.rows3_in, m.h2_ready, m.rt_ready, m.sel_ready, m.moe_start, m.rounds_ready, m.gm_ready, m.oh_ready, m.tx_ready,
     m.tx_copied, m.sc_used, m.sc_ready, m.dn_copied, m.dn_ready, m.hid_ready, m.silu_ready, m.sca_ready, m.moe_done, m.gd_ready,
     m.rexp_ready, m.vd_ready, m.ps_ready, m.x_final, m.out_ready, m.stored) = (
        sem(n) for n in ("rows2_in", "rows3_in", "h2_ready", "router_ready", "selected", "moe_start", "rounds_ready", "one_hot_gated",
                         "one_hot", "gather_ready", "gather_copied", "scatter_added", "scatter_ready", "down_copied", "down_ready",
                         "hidden_ready", "silu_ready", "gates_moved", "moe_done", "group_diff", "router_exp", "expert_diff",
                         "places_ready", "x_final", "out_ready", "stored"))
    for_batches = lambda n: [sem(f"{n}{b}") for b in (0, 1)]
    m.b_ready, m.b_done, m.bd_ready, m.dx_ready, m.d_ready = (
        for_batches(n) for n in ("delta_ready", "delta_done", "g_columns", "decay_log", "decay_exp"))
    (m.rows_in, m.cst2_in, m.x_normed, m.r_ready, m.r_done, m.oc_done, m.gc_ready, m.gc_copied, m.egc_ready, m.state_zero,
     m.conv_ready, m.cv_ready, m.beta_ready, m.z_ready, m.ez_ready, m.g_done, m.ck_ready, m.ck_half, m.on_done) = (
        sem(n) for n in ("rows_in", "cst2_in", "x_normed", "chunk_ready", "chunk_done", "chunk_out", "g_sum_ready", "g_sum_copied",
                         "g_sum_exp_ready", "state_zero", "conv_silu", "conv_done", "beta_ready", "z_ready", "ez_ready", "g_done",
                         "ck_ready", "ck_half", "delta_normed"))

    block = ctx.enter_context(nc.Block())
    w_in_d, w_out_d = a["w_in"], a["w_out"]
    mod = m.mod = nc.dram_tensor("mod_scratch", [1, 6 * D], f32).ap()

    def half_rows(w, j):
        return w[j * 1024:(j + 1) * 1024, :].rearrange("(k p) n -> p k n", p=P)

    def small_loads(l):
        at = l * SMALL
        return ((small_all[:, at + G_:at + G_ + KB], a["norm_g"][l].rearrange("(k p) -> p k", p=P)),
                (small_all[:, at + QN_:at + QN_ + 3], a["mla_q_norm"][l].rearrange("(k p) -> p k", p=P)),
                (small_all[:, at + QN_ + 3:at + QN_ + 5], a["mla_kv_norm"][l].rearrange("(k p) -> p k", p=P)),
                (small_all[:, at + SK_:at + SK_ + 8], a["swa_sink"][l:l + 1, :].partition_broadcast(P)),
                (small_all[:, at + LP_:at + LP_ + 256], a["diff_lambda"][l:l + 1].rearrange("a b c -> a (b c)").partition_broadcast(P)),
                (small_all[:, at + SB_:at + SB_ + 128], a["diff_subln"][l:l + 1, :].partition_broadcast(P)),
                (small_all[:, at + LC_:at + LC_ + 2], a["lam_init"][l:l + 1, :].partition_broadcast(P)))

    m.half_rows = half_rows
    second_buffers(m)
    moe_buffers(m)

    def slot(i):
        return ring[:, i % RING, :]

    uq = ring[:, 1, 0:QR_K * UQ].rearrange("p (k n) -> p k n", k=QR_K)
    ukv = [ring[:, 0, 16 * REST:16 * REST + UKV], ring[:, 1, QR_K * UQ:QR_K * UQ + UKV]]
    rest = ring[:, 0, 0:16 * REST].rearrange("p (k n) -> p k n", k=KB)
    mlaq, mlakv = PROJ[:, :, 0:UQ], PROJ[:, :, AG:AG + UKV]

    def heads(group):
        kind, g = group[0], int(group[1])
        return [(kind, g, c) for c in (0, 1)] if kind == "D" else [(kind, 2 * g + c, None) for c in (0, 1)]

    @block.sync
    def _(sp):
        sp.dma_start(posi[:, :], a["positions"].rearrange("(t p) -> p t", p=P),
                     allow_slow_non_contiguous=True).then_inc(in_pos, 16)
        sp.dma_start(PT[:, :, :, :].rearrange("p a b c -> p (a b c)").bitcast(i32)[:, 0:S],
                     a["positions"].rearrange("(a n) -> a n", a=1).partition_broadcast(P)).then_inc(in_pos, 16)
        sp.dma_start(ccol[:, :], a["c_2"][0].rearrange("(k p) -> p k", p=P),
                     allow_slow_non_contiguous=True).then_inc(in_pos, 16)
        sp.dma_start(X[:, :, :], a["x"][0].rearrange("(t p) d -> p t d", p=P)).then_inc(in_x, 16)
        with sp.Fori(0, LAYERS) as l:
            n = 0

            def load(dst, src, apart=False):
                sp.wait_ge(hu_used, l * PER["hu"] + n + 1)
                if n == 0:
                    sp.wait_ge(in_x, 16)
                if apart:
                    sp.sem_inc(loading, 1)
                sp.dma_start(dst, src).then_inc(w_in[n % RING], 16)

            wl = w_in_d[bass.ds(l, 1)].rearrange("a k n -> (a k) n")
            wo = w_out_d[bass.ds(l, 1)].rearrange("a k n -> (a k) n")
            for p, u in enumerate(ORDER):
                if u == 11:
                    load(rest, wl[:, 11 * U:D_IN].rearrange("(k p) n -> p k n", p=P))
                    ukv_d = a["mla_w_ukv"][bass.ds(l, 1)].rearrange("a k n -> (a k) n")
                    load(ukv[0], ukv_d[0:P, :])
                    n += 1
                    load(uq, a["mla_w_uq"][bass.ds(l, 1)].rearrange("a (k p) n -> p (a k) n", p=P))
                    load(ukv[1], ukv_d[P:2 * P, :])
                    n += 1
                else:
                    for j in (0, 1):
                        load(slot(n).rearrange("p (k n) -> p k n", k=8), half_rows(wl[:, u * U:(u + 1) * U], j),
                             apart=u + j == 0)
                        n += 1
                for j in (0, 1):
                    src = a["ada_w_2"][0, j * 1024:(j + 1) * 1024, bass.ds(l * 12 * U + p * U, U)]
                    load(slot(n).rearrange("p (k n) -> p k n", k=8), src.rearrange("(k p) n -> p k n", p=P))
                    n += 1
            for u in range(4):
                for j in (0, 1):
                    load(slot(n).rearrange("p (k n) -> p k n", k=8), half_rows(wo[:, u * U:(u + 1) * U], j))
                    n += 1
            assert n == PER["hu"]
        second_sync(m, sp)
        moe_sync(m, sp)
        for t in range(TT):
            sp.wait_ge(m.out_ready, t + 1)
            sp.dma_start(out[0, t * P:(t + 1) * P, :], X[:, t, :]).then_inc(m.stored, 16)
        sp.wait_ge(m.stored, 16 * TT)

    @block.gpsimd
    def _(pool):
        nc.gpsimd.memset(half[:, :], -0.5).then_inc(half_ready, 1)
        for dst, src in small_loads(1):
            pool.dma_start(dst, src, allow_slow_non_contiguous=True).then_inc(in_small1, 16)
        pool.wait_ge(half_ready, 1)
        with pool.Fori(0, LAYERS) as l:
            r_in = Tally(l * PER["rin"])

            def root(i, j):
                pool.wait_ge(rin_ready, r_in.next())
                nc.gpsimd.tensor_tensor(rms[:, i:j], rin[:, i:j], half[:, i:j], ALU.pow).then_inc(rms_ready, 1)

            root(0, 2)
            for p in range(12):
                for kind, arg in TASKS.get(p, ()):
                    if kind == "mla_norm":
                        root(2, 6)
                    if kind == "out" and arg[0] == "D":
                        root(6, 8)

        second_gpsimd(nc, m, pool)
        moe_gpsimd(nc, m, pool)

    @block.tensor
    def _(pe):
        pe.sem_inc(hu_used, RING)
        pe.wait_ge(in_small, 16 * 8)
        with pe.Fori(0, LAYERS) as l:
            load = [Tally(l * (15 if i < 2 else 14) * 16) for i in range(RING)]
            ta, td = Tally(l * PER["ta"], 1), Tally(l * PER["td"], 1)
            pjc, xoc = Tally(l * PER["pja"]), Tally(l * PER["xo"], 1)
            s, o, e, c = Tally(l * PER["s"], 1), Tally(l * PER["o"], 1), Tally(l * PER["e"]), Tally(l * PER["c"])
            hu = 0

            def transposes(by_act, sources):
                t, ready, copied, ps = (ta, ta_ready, ta_copied, psTA) if by_act else (td, td_ready, td_copied, psTD)
                pe.wait_ge(copied, t.now())
                for i, src in enumerate(sources):
                    last = nc.tensor.transpose(ps[:, i * P:(i + 1) * P], src, ident)
                last.then_inc(ready, 1)
                t.next()

            def copied():
                pe.wait_ge(ta_copied, ta.now())
                pe.wait_ge(td_copied, td.now())

            def proj(v, lhs, width, chunk, blocks, signal, by=1):
                for k in range(blocks):
                    for t in range(TT):
                        last = nc.tensor.matmul(bank[2 * (v % 2) + t][:, 0:width], lhs[:, k, t * P:(t + 1) * P],
                                                chunk(k), start=k == 0, stop=k == blocks - 1)
                last.then_inc(signal, by)

            def halves(v, steps):
                nonlocal hu
                total, at, queue = sum(x for x, _ in steps) + 1, 0, []
                for x, do in steps:
                    at += x
                    queue.append((16 * at // total, do))
                for j in (0, 1):
                    pe.wait_ge(w_in[hu % RING], load[hu % RING].next(16))
                    w = slot(hu).rearrange("p (k n) -> p k n", k=8)
                    for k in range(8):
                        while queue and queue[0][0] <= 8 * j + k:
                            queue.pop(0)[1]()
                        for t in range(TT):
                            last = nc.tensor.matmul(bank[2 * (v % 2) + t][:, :], HT[:, 8 * j + k, t * P:(t + 1) * P],
                                                    w[:, k, :], start=j == 0 and k == 0, stop=j == 1 and k == 7)
                    last.then_inc(hu_used, 1)
                    hu += 1

            def scores(kind, h, comp):
                pe.wait_ge(s_used, s.now())
                s.next()
                copied()
                for t in range(TT):
                    out = psS[:, t * S:(t + 1) * S]
                    tok = slice(t * P, (t + 1) * P)
                    if kind == "M":
                        q = slice(64 * (h % 2), 64 * (h % 2) + 64)
                        nc.tensor.matmul(out, QK[:, 5 + h, tok], QK[:, 9 + h, :], start=True, stop=False)
                        last = nc.tensor.matmul(out, QK[q, 13 + h // 2, tok], QK[q, 15, :], start=False, stop=True)
                    elif kind == "D":
                        q = slice(64 * comp, 64 * comp + 64)
                        last = nc.tensor.matmul(out, QK[q, h, tok], QK[q, 4 + h, :], start=True, stop=True)
                    else:
                        last = nc.tensor.matmul(out, QK[:, 8 + h if h < 4 else h - 4, tok], QK[:, 12 + h // 4, :],
                                                start=True, stop=True)
                last.then_inc(s_ready, 1)

            def flip(pb):
                transposes(True, [PB[:, pb, qt, kt * P:(kt + 1) * P] for kt in range(TT) for qt in range(TT)])

            def weighted(value):
                pe.wait_ge(o_used, o.now())
                o.next()
                pe.wait_ge(ta_copied, ta.now())
                for t in range(TT):
                    for kt in range(TT):
                        last = nc.tensor.matmul(psO[:, t * P:(t + 1) * P], PT[:, kt, t, :], value(kt),
                                                start=kt == 0, stop=kt == TT - 1)
                last.then_inc(o_ready, 1)

            def mla_up():
                copied()
                for n, (lo, hi) in enumerate(((0, 512), (512, 768))):
                    if n == 0:
                        pe.wait_ge(pj_copied, pjc.base + 2)
                    else:
                        pe.wait_ge(pj_copied, pjc.base + 3)
                    proj(3 + n, QK[:, 0:3, :], hi - lo, lambda k: uq[:, k, lo:hi], QR_K, pj_ready)
                for n in range(2):
                    pe.wait_ge(pj_copied, pjc.base + 4 + n)
                    proj(5 + n, QK[:, 3:5, :], U, lambda k: ukv[k][:, n * U:(n + 1) * U], KVR_K,
                         hu_used if n else pj_ready, 2 if n else 1)

            def flip_ready(arg, i):
                if arg[0] == "D":
                    pe.wait_ge(c_ready, c.next())
                elif i == 0:
                    pe.wait_ge(e_ready, e_of[arg] - 1)
                else:
                    pe.wait_ge(e_ready, e_of[arg])
                flip(i)

            def begin(arg, *h):
                if arg not in e_of:
                    e_of[arg] = e.next(2)
                scores(*h)

            def rope_queries():
                pe.wait_ge(rope_ready, l + 1)
                transposes(True, [ropeq[:, t, 2 * i:2 * i + 2, :] for i in (0, 1) for t in range(TT)])

            def evacuated(v, do):
                pe.wait_ge(pj_copied, pjc.base + v)
                do()

            def pieces(kind, arg, v):
                if kind == "mla_norm":
                    pe.wait_ge(cn_ready, l + 1)
                    cq = lambda b, t: PROJ[:, t, CQ + b * P:CQ + (b + 1) * P]
                    return [(1, lambda b=b: transposes(False, [cq(i, t) for i in b for t in range(TT)])) for b in ((0, 1), (2, 3), (4,))]
                if kind == "mla_up":
                    return [(1, mla_up)]
                if kind == "mla_rope":
                    out = []
                    for x, width in ((mlaq, 192), (mlakv, S)):
                        for h in (0, 2):
                            out.append((1, lambda h=h, x=x, width=width: evacuated(8, lambda: transposes(
                                h == 0, [x[:, t, (h + i) * width:(h + i) * width + P] for i in (0, 1) for t in range(TT)]))))
                    return out + [(1, rope_queries), (1, lambda: transposes(False, [kr2[:, t, :, :] for t in range(TT)]))]
                if kind in ("prep_d", "prep_w"):
                    cols = (DQ, DQ + 2 * P, DK, DK + 2 * P) if kind == "prep_d" else ((AQ, AQ + 2 * P, AK), (AQ + 4 * P, AQ + 6 * P))[arg]
                    return [(1, lambda i=i, at=at: evacuated(v, lambda: transposes(
                        i % 2 == 0, [PROJ[:, t, at + b * P:at + (b + 1) * P] for b in (0, 1) for t in range(TT)])))
                            for i, at in enumerate(cols)]
                if kind == "soft":
                    return [(1, lambda h=h: begin(arg, *h)) for h in heads(arg)]
                out = []
                for i, (k, h, _) in enumerate(heads(arg)):
                    if k == "D" and i == 1:
                        break
                    at = {"M": AG + h * S + P, "D": DV + h * P, "W": AV + (h // 4) * P}[k]
                    out.append((1 if i else 4, lambda i=i: flip_ready(arg, i)))
                    out.append((1, lambda at=at: weighted(lambda kt: PROJ[:, kt, at:at + P])))
                return out

            def ada_sum():
                pe.wait_ge(td_copied, td.now())
                nc.tensor.matmul(psTD[0:1, :], cst[:, C_SEL:C_SEL + 1], ada_part[:, :], start=True, stop=True)\
                    .then_inc(td_ready, 1)
                td.next()

            def split_halves(v, n):
                nonlocal hu
                for j in (0, 1):
                    i = 2 * n + j
                    pe.wait_ge(w_hi_ready, l * 8 + i + 1)
                    lo = ring_r[:, hu % RING, :].rearrange("p (k n) -> p k n", k=8)
                    for k in range(8):
                        hi = w_hi[i % 2][:, k // 4, k % 4, :]
                        for part in (y_hi, y_lo):
                            for t in range(TT):
                                nc.tensor.matmul(bank[2 * (v % 2) + t][:, :], part[:, 8 * j + k, t * P:(t + 1) * P], hi,
                                                 start=j == 0 and k == 0 and part is y_hi, stop=False)
                    pe.wait_ge(w_lo_ready, l * 8 + i + 1)
                    for k in range(8):
                        for t in range(TT):
                            last = nc.tensor.matmul(bank[2 * (v % 2) + t][:, :], y_hi[:, 8 * j + k, t * P:(t + 1) * P],
                                                    lo[:, k, :], start=False, stop=j == 1 and k == 7)
                    last.then_inc(hu_used, 1)
                    hu += 1

            pe.wait_ge(h_ready, l + 1)
            for j in range(8):
                transposes(j % 2 == 0, [Y[:, t, (2 * j + b) * P:(2 * j + b + 1) * P] for b in (0, 1) for t in range(TT)])
            copied()
            e_of = {}
            v = 0
            later = []
            for p, u in enumerate(ORDER):
                if v >= 2:
                    pe.wait_ge(pj_copied, pjc.base + v - 1)
                if u == 11:
                    for _, do in later:
                        do()
                    pe.wait_ge(w_in[0], load[0].next(32))
                    pe.wait_ge(w_in[1], load[1].next(32))
                    proj(v, HT, REST, lambda k: rest[:, k, :], KB, pj_ready)
                else:
                    halves(v, later)
                v += 1
                later = []
                if u == 11:
                    mla_up()
                    v += 4
                    hu += 2
                if p == 0:
                    pe.wait_ge(cb_ready, 1)
                pe.wait_ge(td_copied, td.now())
                for j in (0, 1):
                    pe.wait_ge(w_in[hu % RING], load[hu % RING].next(16))
                    w = slot(hu).rearrange("p (k n) -> p k n", k=8)
                    for k in range(8):
                        g = k % 4
                        last = nc.tensor.matmul(psTD[32 * g:32 * g + 32, :], cb[:, 8 * j + k, :], w[:, k, :],
                                                start=j == 0 and k < 4, stop=j == 1 and k >= 4)
                    last.then_inc(hu_used, 1)
                    hu += 1
                td.next()
                later = [(1, ada_sum)]
                if p in DIRECT:
                    ada_sum()
                    later = []
                for kind, arg in TASKS.get(p, ()):
                    if kind != "mla_up":
                        later += pieces(kind, arg, v)
                if p in DIRECT:
                    for _, do in later:
                        do()
                    later = []
            for kind, arg in TASKS[12]:
                for _, do in pieces(kind, arg, v):
                    do()
            pe.wait_ge(o_used, o.now())
            for j in range(8):
                transposes(j % 2 == 0, [Y[:, t, (2 * j + b) * P:(2 * j + b + 1) * P] for b in (0, 1) for t in range(TT)])
            copied()
            for n in range(4):
                if n >= 2:
                    pe.wait_ge(xo, xoc.base + n)
                split_halves(v, n)
                v += 1
            assert hu == PER["hu"] and ta.n - 1 == PER["ta"] and td.n - 1 == PER["td"], (hu, ta.n, td.n)
            assert s.n - 1 == PER["s"] and e.n == PER["e"] and o.n - 1 == PER["o"] and c.n == PER["c"], (s.n, e.n, o.n, c.n)

        second_tensor(nc, m, pe)
        moe_tensor(nc, m, pe)

    @block.scalar
    def _(act):
        A_ = nc.scalar.activation
        steps = 0
        act.sem_inc(ta_copied, 1)
        act.dma_start(cst[:, :], a["cst1"]).then_inc(in_small, 16)
        for dst, src in small_loads(0):
            act.dma_start(dst, src, allow_slow_non_contiguous=True).then_inc(in_small, 16)
        act.wait_ge(in_pos, 48)
        A_(ccol[:, :], ccol[:, :], ACT.Silu).then_inc(setup_a, 1)
        act.wait_ge(angles_ready, 1)
        A_(sinT[:, :, :], dist[:, 0, 0:64].rearrange("p (t n) -> p t n", t=TT), ACT.Sin).then_inc(setup_a, 1)
        A_(cosT[:, :, :], dist[:, 1, 0:64].rearrange("p (t n) -> p t n", t=TT), ACT.Sin).then_inc(setup_a, 1)
        act.wait_ge(in_x, 16)
        with act.Fori(0, LAYERS) as l:
            pj, ta = Tally(l * PER["pj"]), Tally(l * PER["ta"])
            mr, o, hu_at = Tally(l * PER["m"]), Tally(l * PER["o"]), 0
            pjc = Tally(l * PER["pja"])
            rr = Tally(l * PER["rout"])
            o_count = 0

            def copy(dst, src):
                act.wait_ge(ta_ready, ta.next())
                A_(dst, src, ACT.Copy).then_inc(ta_copied, 1)

            def evac(v, out, width, silu):
                for t in range(TT):
                    src = bank[2 * (v % 2) + t]
                    cuts = [(0, silu[0], ACT.Copy), (silu[0], silu[1], ACT.Silu), (silu[1], width, ACT.Copy)]
                    for lo, hi, f in cuts:
                        if hi > lo:
                            last = A_(out(t, lo, hi), src[:, lo:hi], f)
                last.then_inc(pj_copied, 1)
                pjc.next()

            def step(kind, arg):
                nonlocal o_count
                if kind == "mla_norm":
                    act.wait_ge(pj_copied, pjc.now())
                    for i, (at, w) in enumerate(((CQ, 384), (CKV, 256))):
                        for t in range(TT):
                            junk = PB[:, :, :, :].rearrange("p a t n -> p (a t n)")[:, t * 384:t * 384 + w] if i == 0 else \
                                (ropeq[:, 0, :, :].rearrange("p h n -> p (h n)") if t else PB[:, 1, 1, :])
                            last = A_(junk, PROJ[:, t, at:at + w], ACT.Square, accum_out=ss[:, 2 + 2 * i + t:3 + 2 * i + t])
                    last.then_inc(sq_ready, 1)
                elif kind == "mla_up":
                    for n, (lo, hi) in enumerate(((0, 512), (512, 768))):
                        act.wait_ge(pj_ready, pj.next())
                        evac(3 + n, lambda t, x, y: mlaq[:, t, lo + x:lo + y], hi - lo, (0, 0))
                    act.wait_ge(pj_ready, pj.next())
                    evac(5, lambda t, x, y: mlakv[:, t, x:y], U, (0, 0))
                    act.wait_ge(hu_used, l * PER["hu"] + RING + 10)
                    evac(6, lambda t, x, y: mlakv[:, t, U + x:U + y], U, (0, 0))
                elif kind == "mla_rope":
                    copy(QK[:, 5:7, :], psTA[:, :])
                    copy(QK[:, 9:11, :], psTA[:, :])
                    copy(QK[:, 13:15, :], psTA[:, :])
                elif kind == "prep_d":
                    copy(QK[:, 0:2, :], psTA[:, :])
                    copy(QK[:, 4:6, :], psTA[:, :])
                elif kind == "prep_w" and arg == 0:
                    copy(QK[:, 8:10, :], psTA[:, :])
                    copy(QK[:, 12:14, :], psTA[:, :])
                elif kind == "prep_w":
                    copy(QK[:, 0:2, :], psTA[:, :])
                elif kind == "soft":
                    for i, (k, h, _) in enumerate(heads(arg)):
                        act.wait_ge(m_ready, mr.next())
                        if k == "W":
                            A_(es[:, i, :], mm[:, i, :], ACT.Exp, bias=cur[:, SK_ + h:SK_ + h + 1], scale=-1.0)
                        sc = {"M": SC192, "D": SC64, "W": SC128}[k]
                        for t in range(TT):
                            last = A_(PB[:, i, t, :], PB[:, i, t, :], ACT.Exp, bias=nm[:, i, t:t + 1], scale=sc,
                                      accum_out=den[:, i, t:t + 1])
                        last.then_inc(e_ready, 1)
                elif kind == "out":
                    for _ in range(1 if arg[0] == "D" else 2):
                        copy(PT[:, :, :, :], psTA[:, :])
                        n = o.next()
                        o_count += 1
                        if arg[0] == "D":
                            act.wait_ge(o_ready, n)
                            for t in range(TT):
                                at = t * P
                                last = A_(ropeq[:, t, 0:2, :].rearrange("p h n -> p (h n)"), psO[:, at:at + P], ACT.Square,
                                          accum_out=ss[:, 6 + t:7 + t])
                            last.then_inc(sq_ready, 1)

            def load_b(p):
                act.dma_start(ada_b[:, :], a["ada_b_2"][0:1, bass.ds(l * 12 * U + p * U, U)]).then_inc(row_b, 16)

            act.wait_ge(xo, l * PER["xo"] + 1)
            load_b(0)
            for t in range(TT):
                last = A_(Y[:, t, :], X[:, t, :], ACT.Square, accum_out=ss[:, t:t + 1])
            last.then_inc(sq_ready, 1)
            act.wait_ge(lam_in, l + 1)
            A_(lam[:, 2:4], lam[:, 0:2], ACT.Exp).then_inc(lam_ready, 1)
            act.wait_ge(rms_ready, l * PER["rout"] + 1)
            for t in range(TT):
                last = A_(Y[:, t, :], X[:, t, :], ACT.Copy, scale=rms[:, t:t + 1])
            last.then_inc(h_ready, 1)
            for j in range(0, 8, 2):
                act.wait_ge(ta_ready, ta.next())
                for b in (0, 1):
                    last = A_(HT[:, 2 * j + b, :], psTA[:, b * S:(b + 1) * S], ACT.Copy, scale=cur[:, G_ + 2 * j + b:G_ + 2 * j + b + 1])
                last.then_inc(ta_copied, 1)
            v = 0
            for p, u in enumerate(ORDER):
                if u == 11:
                    act.wait_ge(pj_ready, pj.next())
                else:
                    hu_at += 2
                    act.wait_ge(hu_used, l * PER["hu"] + RING + hu_at)
                silu = {3: (0, 512), 4: (0, 512), 6: (192, 512), 7: (0, 192), 10: (192, 512), 11: (0, 192)}.get(u, (0, 0))
                evac(v, lambda t, x, y: PROJ[:, t, u * U + x:u * U + y], REST if u == 11 else U, silu)
                v += 1
                for kind, arg in TASKS.get(p, ()):
                    step(kind, arg)
                    if kind == "mla_up":
                        v += 4
                        hu_at += 2
                hu_at += 2
                act.wait_ge(row_ready, l * 12 + p + 1)
                act.dma_start(mod[0:1, bass.ds(l * 12 * U + p * U, U)], ada_row[:, :]).then_inc(mod_out, 16)
                if p < 11:
                    load_b(p + 1)
            act.wait_ge(mod_out, l * 12 * 16 + 12 * 16)
            def round_weights(n):
                i = n % RING
                loads = 15 if i < 2 else 14
                act.wait_ge(w_in[i], (l * loads + loads - 1 + n // RING) * 16)
                A_(w_hi[n % 2], slot(n).rearrange("p (t k n) -> p t k n", t=2, k=4), ACT.Copy).then_inc(w_hi_ready, 1)

            act.wait_ge(o_used, l * PER["o"] + 1 + 8)
            round_weights(0)
            for kind, arg in TASKS[12]:
                step(kind, arg)
            for j in range(0, 8, 2):
                act.wait_ge(ta_ready, ta.next())
                A_(y_hi[:, 2 * j:2 * j + 2, :], psTA[:, :], ACT.Copy).then_inc(y_hi_ready, 1)
            act.wait_ge(o_used, l * PER["o"] + 1 + PER["o"])
            for n in range(1, 8):
                if n >= 2:
                    act.wait_ge(hu_used, l * PER["hu"] + RING + 48 + n - 1)
                round_weights(n)
            assert ta.n == PER["ta"] and pj.n == PER["pj"] and pjc.n == PER["pja"] and mr.n == PER["m"], (ta.n, pj.n, pjc.n, mr.n)

        second_scalar(nc, m, act, ACT)
        moe_scalar(nc, m, act, ACT)

    @block.vector
    def _(dve):
        V = nc.vector
        steps = 0
        base = 0

        def link(ins):
            nonlocal steps
            steps += 1
            ins.then_inc(dve_step, 1)
            dve.wait_ge(dve_step, base + steps)

        dve.sem_inc(td_copied, 1)
        dve.sem_inc(s_used, 1)
        dve.sem_inc(o_used, 1)
        dve.sem_inc(xo, 1)
        dve.wait_ge(in_small, 16 * 8)
        dve.wait_ge(in_pos, 48)
        prow = PB[:, 0, 0, :]
        pint = PT[:, :, :, :].rearrange("p a b c -> p (a b c)").bitcast(i32)[:, 0:S]
        V.tensor_copy(prow, pint)
        link(V.tensor_copy(posp[:, :], posi[:, :]))
        ang, k_, r_, w_ = (PB[:, 1, 0, i * 64:(i + 1) * 64] for i in range(4))
        for t in range(TT):
            last = V.tensor_scalar(ang[:, t * 32:(t + 1) * 32], cst[:, C_FREQ:C_FREQ + 32], posp[:, t:t + 1], None, ALU.mult)
        link(last)
        link(V.tensor_scalar(k_, ang, 1 / (2 * math.pi), MAGIC, ALU.mult, ALU.add))
        link(V.tensor_scalar(k_, k_, -MAGIC, None, ALU.add))
        for part in (TWO_PI_A, TWO_PI_B, TWO_PI_C):
            link(V.scalar_tensor_tensor(ang, k_, -part, ang, ALU.mult, ALU.add))
        link(V.tensor_scalar(dist[:, 0, 0:64], ang, -3.1415925, 3.1415925, ALU.max, ALU.min))
        link(V.tensor_scalar(r_, ang, math.pi / 2, None, ALU.add))
        link(V.tensor_scalar(w_, r_, math.pi, -2 * math.pi, ALU.is_gt, ALU.mult))
        link(V.tensor_tensor(r_, r_, w_, ALU.add))
        dve.wait_ge(setup_a, 1)
        V.tensor_copy(cb[:, :, :], ccol[:, :].unsqueeze(2).to_broadcast([P, KB, 32])).then_inc(cb_ready, 1)
        V.tensor_scalar(dist[:, 1, 0:64], r_, -3.1415925, 3.1415925, ALU.max, ALU.min).then_inc(angles_ready, 1)
        dve.wait_ge(setup_a, 3)
        for t in range(TT):
            last = V.tensor_scalar(dist[:, t, :], prow, posp[:, t:t + 1], None, ALU.subtract)
        link(last)
        link(V.scalar_tensor_tensor(dist[:, :, :], dist[:, :, :], -1.0, dist[:, :, :], ALU.mult, ALU.max))
        link(V.tensor_scalar(distm[:, :, :], dist[:, :, :], float(P), BIG, ALU.is_gt, ALU.mult))
        link(V.tensor_tensor(distm[:, :, :], distm[:, :, :], dist[:, :, :], ALU.add))
        setup_steps = steps
        with dve.Fori(0, LAYERS) as l:
            base, steps = l * PER["dve"] + setup_steps, 0
            td, s, o, q, e = Tally(l * PER["td"]), Tally(l * PER["s"]), Tally(l * PER["o"]), Tally(l * PER["q"]), Tally(l * PER["e"])
            rr, row = Tally(l * PER["rout"]), Tally(l * 12)
            td_c, s_c, o_c = Tally(l * PER["td"], 1), Tally(l * PER["s"], 1), Tally(l * PER["o"], 1)
            pjc = Tally(l * PER["pja"])
            td_w = 0
            hu_at = 0

            def copy(dst, src):
                dve.wait_ge(td_ready, l * PER["tdr"] + tdr.next())
                V.tensor_copy(dst, src).then_inc(td_copied, 1)

            tdr = Tally(0)

            def copy_gain(pairs):
                dve.wait_ge(td_ready, l * PER["tdr"] + tdr.next())
                for dst, src, g in pairs:
                    last = V.tensor_scalar(dst, src, g, None, ALU.mult)
                last.then_inc(td_copied, 1)

            def mean(i, j, n):
                return V.tensor_scalar(rin[:, i:j], ss[:, i:j], 1.0 / n, EPS, ALU.mult, ALU.add)

            link(V.tensor_copy(cur[:, :], small_all[:, bass.ds(l * SMALL, SMALL)]))
            dve.wait_ge(sq_ready, q.next())
            mean(0, 2, D).then_inc(rin_ready, 1)
            rr.next()
            lp = cur[:, LP_:LP_ + 256].rearrange("p (a b n) -> p a b n", a=2, b=2)
            prod = ropet[:, :, :, :].rearrange("p t h n -> p (t h n)")[:, 0:P].rearrange("p (a n) -> p a n", a=2)
            link(V.tensor_tensor(prod, lp[:, :, 0, :], lp[:, :, 1, :], ALU.mult))
            V.tensor_reduce(lam[:, 0:2], prod, AX.X, ALU.add).then_inc(lam_in, 1)
            link(V.tensor_scalar(cur[:, SB_:SB_ + P], cur[:, SB_:SB_ + P], cur[:, LC_ + 1:LC_ + 2], None, ALU.mult))
            for j in range(1, 8, 2):
                copy_gain([(HT[:, 2 * j + b, :], psTD[:, b * S:(b + 1) * S], cur[:, G_ + 2 * j + b:G_ + 2 * j + b + 1]) for b in (0, 1)])
            dve.wait_ge(lam_ready, l + 1)
            link(V.tensor_tensor(lam[:, 0:1], lam[:, 3:4], lam[:, 2:3], ALU.subtract))
            link(V.tensor_tensor(lam[:, 1:2], lam[:, 0:1], cur[:, LC_:LC_ + 1], ALU.subtract))

            def rotate(dst, x1, x2, heads_):
                shape = [P, TT, heads_, 32]
                cos, sin = (x[:, :, :].unsqueeze(2).to_broadcast(shape) for x in (cosT, sinT))
                tmp = ropet[:, :, 0:heads_, :]
                for lo, f, g, op in ((0, cos, sin, ALU.subtract), (32, sin, cos, ALU.add)):
                    V.tensor_tensor(dst[:, :, :, lo:lo + 32], x1, f, ALU.mult)
                    link(V.tensor_tensor(tmp, x2, g, ALU.mult))
                    last = V.tensor_tensor(dst[:, :, :, lo:lo + 32], dst[:, :, :, lo:lo + 32], tmp, op)
                    if lo == 0:
                        link(last)
                return last

            def step(kind, arg):
                if kind == "mla_norm":
                    dve.wait_ge(sq_ready, q.next())
                    mean(2, 4, 384)
                    mean(4, 6, 256).then_inc(rin_ready, 1)
                    dve.wait_ge(rms_ready, rr.next())
                    for i, (at, w) in enumerate(((CQ, 384), (CKV, 256))):
                        for t in range(TT):
                            x = PROJ[:, t, at:at + w]
                            last = V.tensor_scalar(x, x, rms[:, 2 + 2 * i + t:3 + 2 * i + t], None, ALU.mult)
                    last.then_inc(cn_ready, 1)
                    for bs in ((0, 1), (2, 3), (4,)):
                        copy_gain([(QK[:, b, :], psTD[:, i * S:(i + 1) * S], cur[:, QN_ + b:QN_ + b + 1]) for i, b in enumerate(bs)])
                elif kind == "mla_rope":
                    dve.wait_ge(pj_copied, pjc.base + 7)
                    copy(QK[:, 7:9, :], psTD[:, :])
                    copy(QK[:, 11:13, :], psTD[:, :])
                    xq = mlaq.rearrange("p t (h n) -> p t h n", h=4)
                    link(rotate(ropeq, xq[:, :, :, 128:160], xq[:, :, :, 160:192], 4))
                    x1, x2 = (PROJ[:, :, at:at + 32].unsqueeze(2).to_broadcast([P, TT, 2, 32]) for at in (KR, KR + 32))
                    rotate(kr2, x1, x2, 2).then_inc(rope_ready, 1)
                    dve.wait_ge(td_ready, l * PER["tdr"] + tdr.next())
                    V.tensor_copy(QK[:, 15, :], psTD[:, 0:S]).then_inc(td_copied, 1)
                elif kind == "prep_d":
                    dve.wait_ge(pj_copied, pjc.base + v)
                    g = PROJ[:, :, DG:D_IN].rearrange("p t (h n) -> p t h n", h=4)
                    link(V.tensor_tensor(g, g, cur[:, SB_:SB_ + P].unsqueeze(1).unsqueeze(1).to_broadcast([P, TT, 4, P]), ALU.mult))
                    copy(QK[:, 2:4, :], psTD[:, :])
                    copy(QK[:, 6:8, :], psTD[:, :])
                elif kind == "prep_w":
                    copy(QK[:, 2:4, :] if arg else QK[:, 10:12, :], psTD[:, :])
                elif kind == "soft":
                    for i, (k, h, _) in enumerate(heads(arg)):
                        dve.wait_ge(s_ready, s.next())
                        pb, ps = PB[:, i, :, :], psS[:, :].rearrange("p (t n) -> p t n", t=TT)
                        if k == "M":
                            ins = V.tensor_copy(pb, ps)
                        elif k == "D":
                            ins = V.scalar_tensor_tensor(pb, dist[:, :, :], -SLOPES4[h] / SC64, ps, ALU.mult, ALU.add)
                        else:
                            ins = V.scalar_tensor_tensor(pb, distm[:, :, :], -SLOPES8[h] / SC128, ps, ALU.mult, ALU.add)
                        ins.then_inc(s_used, 1)
                        dve.wait_ge(s_used, s_c.next())
                        link(V.tensor_reduce(mx[:, i, :], pb, AX.X, ALU.max))
                        if k == "W":
                            link(V.tensor_scalar(mm[:, i, :], mx[:, i, :], SC128, cur[:, SK_ + h:SK_ + h + 1], ALU.mult, ALU.max))
                            last = V.tensor_scalar(nm[:, i, :], mm[:, i, :], -1.0, None, ALU.mult)
                        else:
                            last = V.tensor_scalar(nm[:, i, :], mx[:, i, :], -(SC192 if k == "M" else SC64), None, ALU.mult)
                        last.then_inc(m_ready, 1)
                elif kind == "out" and arg[0] == "D":
                    h = int(arg[1])
                    dve.wait_ge(e_ready, e.next(2))
                    link(V.reciprocal(rec[:, :, :], den[:, :, :]))
                    link(V.tensor_scalar(rec[:, 1, :], rec[:, 1, :], lam[:, 1:2], None, ALU.mult))
                    for t in range(TT):
                        last = V.tensor_scalar(PB[:, 0, t, :], PB[:, 0, t, :], rec[:, 0, t:t + 1], None, ALU.mult)
                    link(last)
                    for t in range(TT):
                        last = V.scalar_tensor_tensor(PB[:, 0, t, :], PB[:, 1, t, :], rec[:, 1, t:t + 1], PB[:, 0, t, :], ALU.mult, ALU.add)
                    last.then_inc(c_ready, 1)
                    dve.wait_ge(sq_ready, q.next())
                    mean(6, 8, P).then_inc(rin_ready, 1)
                    dve.wait_ge(rms_ready, rr.next())
                    dve.wait_ge(o_ready, o.next())
                    for t in range(TT):
                        at = t * P
                        last = V.scalar_tensor_tensor(Y[:, t, 1536 + h * P:1536 + (h + 1) * P], psO[:, at:at + P], rms[:, 6 + t:7 + t],
                                                      PROJ[:, t, DG + h * P:DG + (h + 1) * P], ALU.mult, ALU.mult)
                    last.then_inc(o_used, 1)
                elif kind == "out":
                    dve.wait_ge(pj_copied, pjc.base + v)
                    for i, (k, h, _) in enumerate(heads(arg)):
                        dve.wait_ge(e_ready, e.next())
                        if k == "W":
                            link(V.tensor_tensor(den[:, i, :], den[:, i, :], es[:, i, :], ALU.add))
                        link(V.reciprocal(rec[:, i, :], den[:, i, :]))
                        dve.wait_ge(o_ready, o.next())
                        gate, to = (BG, 1024) if k == "M" else (AG, 0)
                        for t in range(TT):
                            at = t * P
                            last = V.scalar_tensor_tensor(Y[:, t, to + h * P:to + (h + 1) * P], psO[:, at:at + P], rec[:, i, t:t + 1],
                                                          PROJ[:, t, gate + h * P:gate + (h + 1) * P], ALU.mult, ALU.mult)
                        last.then_inc(o_used, 1)

            td_c.next(4)
            v = 0
            for p, u in enumerate(ORDER):
                v += 1
                if u == 11:
                    v += 4
                hu_at += 4
                dve.wait_ge(hu_used, l * PER["hu"] + RING + hu_at)
                V.tensor_copy(ada_part[:, :], psTD[:, :]).then_inc(td_copied, 1)
                td_c.next()
                dve.wait_ge(td_ready, l * PER["tdr"] + tdr.next())
                dve.wait_ge(row_b, l * 12 * 16 + (p + 1) * 16)
                if p > 0:
                    dve.wait_ge(mod_out, l * 12 * 16 + p * 16)
                V.tensor_tensor(ada_row[:, :], psTD[0:1, :], ada_b[:, :], ALU.add).then_inc(td_copied, 1)
                dve.wait_ge(td_copied, td_c.next())
                dve.sem_inc(row_ready, 1)
                for kind, arg in TASKS.get(p, ()):
                    step(kind, arg)
                    td_c.next({"mla_norm": 3, "mla_rope": 3, "prep_d": 2, "prep_w": 1}.get(kind, 0))
            def remainders(n):
                dve.wait_ge(w_hi_ready, l * 8 + n + 1)
                w = slot(n).rearrange("p (t k n) -> p t k n", t=2, k=4)
                lo = ring_r[:, n % RING, :].rearrange("p (t k n) -> p t k n", t=2, k=4)
                V.tensor_tensor(lo, w, w_hi[n % 2].bitcast(f32), ALU.subtract).then_inc(w_lo_ready, 1)

            remainders(0)
            for kind, arg in TASKS[12]:
                step(kind, arg)
            for j in range(8):
                dst = slice(2 * j, 2 * j + 2)
                if j % 2 == 0:
                    dve.wait_ge(y_hi_ready, l * 4 + j // 2 + 1)
                else:
                    dve.wait_ge(td_ready, l * PER["tdr"] + tdr.next())
                    link(V.tensor_copy(y_hi[:, dst, :], psTD[:, :]))
                ps, cop = (psTD, td_copied) if j % 2 else (psTA, ta_copied)
                V.tensor_tensor(y_lo[:, dst, :], ps[:, :].rearrange("p (a n) -> p a n", a=2), y_hi[:, dst, :].bitcast(f32), ALU.subtract)\
                    .then_inc(cop, 1)
            for n in range(1, 4):
                remainders(n)
            for n in range(4):
                dve.wait_ge(hu_used, l * PER["hu"] + RING + 50 + 2 * n)
                for t in range(TT):
                    x = X[:, t, n * U:(n + 1) * U]
                    last = V.tensor_tensor(x, x, bank[2 * (v % 2) + t][:, :], ALU.add)
                last.then_inc(xo, 1)
                v += 1
                if n in (0, 1):
                    remainders(4 + 2 * n)
                    remainders(5 + 2 * n)
            dve.wait_ge(in_small1, 16 * 7)
            assert tdr.n == PER["tdr"] and steps == PER["dve"] and q.n == PER["q"] and rr.n == PER["rout"], (tdr.n, steps, q.n, rr.n)
        steps2 = second_vector(nc, m, dve, AX, LAYERS * PER["dve"] + setup_steps)
        moe_vector(nc, m, dve, AX, steps2)


def host_constants():
    c = np.zeros((P, C1), np.float32)
    c[:, C_ID:C_ID + P] = np.eye(P, dtype=np.float32)
    c[:, C_FREQ:C_FREQ + 32] = np.float32(10000.0) ** (-np.arange(0, 64, 2, dtype=np.float32) / np.float32(64))
    c[0:P:32, C_SEL] = 1.0
    lam = [0.8 - 0.6 * math.exp(-0.3 * l) for l in range(LAYERS)]
    return {"cst1": c, "lam_init": np.array([[x, 1.0 - x] for x in lam], np.float32), **second_constants(), **moe_constants()}


def kernel(**inputs):
    import numpy as _np
    import concourse.bacc as _bacc
    from concourse import mybir as _mybir
    from concourse.bass_utils import run_bass_kernel_spmd as _run

    nc = _bacc.Bacc("TRN2", target_bir_lowering=False, num_devices=1)
    arrays, a = {}, {}
    for name, x in {**inputs, **host_constants()}.items():
        x = _np.ascontiguousarray(x)
        arrays[f"in_{name}_dram"] = x
        a[name] = nc.dram_tensor(f"in_{name}_dram", x.shape, _mybir.dt.from_np(x.dtype), kind="ExternalInput").ap()
    out = nc.dram_tensor("out_0_dram", (1, S, D), _mybir.dt.float32, kind="ExternalOutput").ap()
    with ExitStack() as ctx:
        program(nc, ctx, a, out)
    return _run(nc, [arrays], core_ids=[0]).results[0]["out_0_dram"]
```
